# Optimizing a Trainium2 kernel written in Bass

```python
import math
import jax, jax.numpy as jnp
from jax import lax
import numpy as np

D_MODEL = 1024
BATCH = 1
SEQ = 1024
DEPTH = 1

PLE_DIM = 256
D_FF = 2816
EPS = 1e-6
NSA_HEADS = 4
NSA_HEAD_DIM = 128
NSA_KV_DIM = 128
CMP_BLOCK = 32
CMP_STRIDE = 16
SLC_BLOCK = 64
SLC_TOPK = 16
WINDOW = 512
NSA_QBLOCK = 64
FORCE_BONUS = 1e4
NEG = -1e30
GLA_HEADS = 4
GLA_KEY_DIM = 64
GLA_VAL_DIM = 128
GLA_GATE_RANK = 16
GLA_GATE_NORM = 16.0
GLA_CHUNK = 64

NSA_WIDTH = NSA_HEADS * NSA_HEAD_DIM
GLA_WIDTH = GLA_HEADS * GLA_VAL_DIM
MIX_WIDTH = NSA_WIDTH + GLA_WIDTH
IN_SPLITS = (NSA_WIDTH,
             NSA_KV_DIM, NSA_KV_DIM,
             NSA_KV_DIM, NSA_KV_DIM,
             NSA_KV_DIM, NSA_KV_DIM,
             3 * NSA_HEADS,
             GLA_HEADS * GLA_KEY_DIM,
             GLA_HEADS * GLA_KEY_DIM,
             GLA_WIDTH,
             GLA_GATE_RANK,
             GLA_WIDTH)
IN_WIDTH = sum(IN_SPLITS)

kernel_name = "hymba_nsa_gla_macaron_block"

def _rmsnorm(x, g):
    x32 = x.astype(jnp.float32)
    y = x32 * lax.rsqrt(jnp.mean(x32 * x32, axis=-1, keepdims=True) + EPS)
    return (y * g.astype(jnp.float32)).astype(x.dtype)

def _swiglu(u, wg, wu, wd):
    return (jax.nn.silu(u @ wg) * (u @ wu)) @ wd

def _nsa(q, k_cmp, v_cmp, k_slc, v_slc, k_win, v_win, gate_logits,
         cpe_k, cw1_k, cw2_k, cpe_v, cw1_v, cw2_v):
    B, S, H, Dh = q.shape
    Dk = k_cmp.shape[-1]
    dt = q.dtype
    n_cmp = (S - CMP_BLOCK) // CMP_STRIDE + 1
    n_slc = S // SLC_BLOCK
    topk = min(SLC_TOPK, n_slc)

    blk_idx = jnp.arange(n_cmp)[:, None] * CMP_STRIDE + jnp.arange(CMP_BLOCK)[None, :]

    def compress(t, pe, w1, w2):
        blocks = t[:, blk_idx] + pe
        hid = jax.nn.silu(jnp.einsum('bnld,lde->bne', blocks, w1))
        return hid @ w2

    kc = compress(k_cmp, cpe_k, cw1_k, cw2_k)
    vc = compress(v_cmp, cpe_v, cw1_v, cw2_v)
    cmp_start = jnp.arange(n_cmp) * CMP_STRIDE
    cmp_end = cmp_start + CMP_BLOCK - 1
    slc_start = jnp.arange(n_slc) * SLC_BLOCK
    overlap = ((cmp_start[:, None] < slc_start[None, :] + SLC_BLOCK)
               & (cmp_start[:, None] + CMP_BLOCK > slc_start[None, :])).astype(jnp.float32)

    kb = k_slc.reshape(B, n_slc, SLC_BLOCK, Dk)
    vb = v_slc.reshape(B, n_slc, SLC_BLOCK, Dk)
    pad = jnp.zeros((B, WINDOW, Dk), k_win.dtype)
    kw_pad = jnp.concatenate([pad, k_win], axis=1)
    vw_pad = jnp.concatenate([pad, v_win], axis=1)
    qs = q * (NSA_HEAD_DIM ** -0.5)
    blk_ids = jnp.arange(n_slc)

    def block(qb_idx):
        q0 = qb_idx * NSA_QBLOCK
        qb = lax.dynamic_slice_in_dim(qs, q0, NSA_QBLOCK, axis=1)
        gb = lax.dynamic_slice_in_dim(gate_logits, q0, NSA_QBLOCK, axis=1)
        t = q0 + jnp.arange(NSA_QBLOCK)

        s_c = jnp.einsum('bqhd,bnd->bhqn', qb, kc).astype(jnp.float32)
        m_c = cmp_end[None, :] <= t[:, None]
        p_c = jax.nn.softmax(jnp.where(m_c, s_c, NEG), axis=-1) * m_c
        o_c = jnp.einsum('bhqn,bnd->bqhd', p_c.astype(vc.dtype), vc)

        imp = jnp.einsum('bhqn,ns->bqs', p_c, overlap)
        cur = t // SLC_BLOCK
        valid = blk_ids[None, :] <= cur[:, None]
        forced = ((blk_ids[None, :] == 0) | (blk_ids[None, :] == cur[:, None])
                  | (blk_ids[None, :] == cur[:, None] - 1))
        imp = jnp.where(valid, imp + jnp.where(forced, FORCE_BONUS, 0.0), -1.0)
        _, sel = lax.top_k(imp, topk)
        kg = jax.vmap(lambda kb_b, i_b: kb_b[i_b])(kb, sel)
        vg = jax.vmap(lambda vb_b, i_b: vb_b[i_b])(vb, sel)
        pos = sel[..., None] * SLC_BLOCK + jnp.arange(SLC_BLOCK)
        m_s = pos <= t[None, :, None, None]
        s_s = jnp.einsum('bqhd,bqnld->bhqnl', qb, kg).astype(jnp.float32)
        s_s = jnp.where(m_s[:, None], s_s, NEG)
        p_s = jax.nn.softmax(s_s.reshape(B, H, NSA_QBLOCK, -1), axis=-1).reshape(s_s.shape)
        o_s = jnp.einsum('bhqnl,bqnld->bqhd', p_s.astype(vg.dtype), vg)

        kw = lax.dynamic_slice_in_dim(kw_pad, q0, WINDOW + NSA_QBLOCK, axis=1)
        vw = lax.dynamic_slice_in_dim(vw_pad, q0, WINDOW + NSA_QBLOCK, axis=1)
        s_pos = q0 - WINDOW + jnp.arange(WINDOW + NSA_QBLOCK)
        diff = t[:, None] - s_pos[None, :]
        m_w = (diff >= 0) & (diff < WINDOW) & (s_pos[None, :] >= 0)
        s_w = jnp.einsum('bqhd,bkd->bhqk', qb, kw).astype(jnp.float32)
        p_w = jax.nn.softmax(jnp.where(m_w, s_w, NEG), axis=-1)
        o_w = jnp.einsum('bhqk,bkd->bqhd', p_w.astype(vw.dtype), vw)

        g = jax.nn.sigmoid(gb.astype(jnp.float32))
        out = (g[..., 0:1] * o_c.astype(jnp.float32) + g[..., 1:2] * o_s.astype(jnp.float32)
               + g[..., 2:3] * o_w.astype(jnp.float32))
        return out.astype(dt)

    outs = lax.map(block, jnp.arange(S // NSA_QBLOCK))
    return outs.transpose(1, 0, 2, 3, 4).reshape(B, S, H, Dh)

def _gla(q, k, v, g_log):
    B, S, H, dk = q.shape
    dv = v.shape[-1]
    dt = v.dtype
    C = GLA_CHUNK
    N = S // C

    def chunks(a):
        return a.astype(jnp.float32).reshape(B, N, C, H, -1).transpose(1, 0, 3, 2, 4)

    qc, kc, vc, gc = chunks(q), chunks(k), chunks(v), chunks(g_log)
    b = jnp.cumsum(gc, axis=3)
    b_last = b[:, :, :, -1:, :]
    q_dec = qc * jnp.exp(b) * (GLA_KEY_DIM ** -0.5)
    k_dec = kc * jnp.exp(-b)
    k_to_end = kc * jnp.exp(b_last - b)
    causal = jnp.tril(jnp.ones((C, C), jnp.float32))
    A = jnp.einsum('nbhid,nbhjd->nbhij', q_dec, k_dec) * causal
    o_intra = jnp.einsum('nbhij,nbhjv->nbhiv', A, vc)

    def step(state, inp):
        q_d, k_e, v_c, decay = inp
        o_inter = jnp.einsum('bhid,bhdv->bhiv', q_d, state)
        state = state * decay[:, :, 0, :, None] + jnp.einsum('bhjd,bhjv->bhdv', k_e, v_c)
        return state, o_inter

    state0 = jnp.zeros((B, H, dk, dv), jnp.float32)
    _, o_inter = lax.scan(step, state0, (q_dec, k_to_end, vc, jnp.exp(b_last)))
    o = o_intra + o_inter
    return o.transpose(1, 0, 3, 2, 4).reshape(B, S, H, dv).astype(dt)

def setup_inputs(seed: int = 0) -> dict:
    key = jax.random.key(seed)
    ks = iter(jax.random.split(key, 40))
    L, D, F = DEPTH, D_MODEL, D_FF

    def nrm(shape, scale):
        return jax.random.normal(next(ks), shape, jnp.float32) * scale

    def gain(shape):
        return 1.0 + 0.05 * jax.random.normal(next(ks), shape, jnp.float32)

    d = {}
    d["x"] = nrm((BATCH, SEQ, D), 1.0)
    d["p"] = nrm((DEPTH, BATCH, SEQ, PLE_DIM), 1.0)
    d["ffn1_pre_g"] = gain((L, D))
    d["ffn1_post_g"] = gain((L, D))
    d["ffn1_w_gate"] = nrm((L, D, F), D ** -0.5)
    d["ffn1_w_up"] = nrm((L, D, F), D ** -0.5)
    d["ffn1_w_down"] = nrm((L, F, D), F ** -0.5)
    d["mix_pre_g"] = gain((L, D))
    d["mix_post_g"] = gain((L, D))
    d["w_in"] = nrm((L, D, IN_WIDTH), D ** -0.5)
    d["cmp_k_pe"] = nrm((L, CMP_BLOCK, NSA_KV_DIM), 0.1)
    d["cmp_k_w1"] = nrm((L, CMP_BLOCK, NSA_KV_DIM, NSA_KV_DIM), (CMP_BLOCK * NSA_KV_DIM) ** -0.5)
    d["cmp_k_w2"] = nrm((L, NSA_KV_DIM, NSA_KV_DIM), NSA_KV_DIM ** -0.5)
    d["cmp_v_pe"] = nrm((L, CMP_BLOCK, NSA_KV_DIM), 0.1)
    d["cmp_v_w1"] = nrm((L, CMP_BLOCK, NSA_KV_DIM, NSA_KV_DIM), (CMP_BLOCK * NSA_KV_DIM) ** -0.5)
    d["cmp_v_w2"] = nrm((L, NSA_KV_DIM, NSA_KV_DIM), NSA_KV_DIM ** -0.5)
    d["nsa_out_g"] = gain((L, NSA_HEADS, NSA_HEAD_DIM))
    d["gla_gate_up"] = nrm((L, GLA_GATE_RANK, GLA_HEADS * GLA_KEY_DIM), GLA_GATE_RANK ** -0.5)
    d["gla_gate_bias"] = nrm((L, GLA_HEADS * GLA_KEY_DIM), 0.1)
    d["gla_out_g"] = gain((L, GLA_HEADS, GLA_VAL_DIM))
    d["w_out"] = nrm((L, MIX_WIDTH, D), MIX_WIDTH ** -0.5)
    d["ffn2_pre_g"] = gain((L, D))
    d["ffn2_post_g"] = gain((L, D))
    d["ffn2_w_gate"] = nrm((L, D, F), D ** -0.5)
    d["ffn2_w_up"] = nrm((L, D, F), D ** -0.5)
    d["ffn2_w_down"] = nrm((L, F, D), F ** -0.5)
    d["ple_proj"] = nrm((L, PLE_DIM, D), PLE_DIM ** -0.5)
    d["ple_gate"] = nrm((L, D, D), D ** -0.5)
    d["ple_post_g"] = gain((L, D))
    return d

def reference(x, p, ffn1_pre_g, ffn1_post_g, ffn1_w_gate, ffn1_w_up, ffn1_w_down,
              mix_pre_g, mix_post_g, w_in, cmp_k_pe, cmp_k_w1, cmp_k_w2,
              cmp_v_pe, cmp_v_w1, cmp_v_w2, nsa_out_g, gla_gate_up, gla_gate_bias,
              gla_out_g, w_out, ffn2_pre_g, ffn2_post_g, ffn2_w_gate, ffn2_w_up,
              ffn2_w_down, ple_proj, ple_gate, ple_post_g):
    B, S, D = x.shape
    split_points = np.cumsum(IN_SPLITS)[:-1].tolist()
    h = x
    for i in range(DEPTH):
        f = _swiglu(_rmsnorm(h, ffn1_pre_g[i]), ffn1_w_gate[i], ffn1_w_up[i], ffn1_w_down[i])
        h = h + 0.5 * _rmsnorm(f, ffn1_post_g[i])

        u = _rmsnorm(h, mix_pre_g[i])
        proj = u @ w_in[i]
        (nq, nkc, nvc, nks, nvs, nkw, nvw, ngate,
         gq, gk, gv, gdown, gog) = jnp.split(proj, split_points, axis=-1)

        o_nsa = _nsa(nq.reshape(B, S, NSA_HEADS, NSA_HEAD_DIM), nkc, nvc, nks, nvs, nkw, nvw,
                     ngate.reshape(B, S, NSA_HEADS, 3),
                     cmp_k_pe[i], cmp_k_w1[i], cmp_k_w2[i], cmp_v_pe[i], cmp_v_w1[i], cmp_v_w2[i])
        o_nsa = _rmsnorm(o_nsa, nsa_out_g[i]).reshape(B, S, NSA_WIDTH)

        g_pre = (gdown @ gla_gate_up[i] + gla_gate_bias[i]).astype(jnp.float32)
        g_log = (jax.nn.log_sigmoid(g_pre) / GLA_GATE_NORM).reshape(B, S, GLA_HEADS, GLA_KEY_DIM)
        o_gla = _gla(gq.reshape(B, S, GLA_HEADS, GLA_KEY_DIM),
                     gk.reshape(B, S, GLA_HEADS, GLA_KEY_DIM),
                     gv.reshape(B, S, GLA_HEADS, GLA_VAL_DIM), g_log)
        o_gla = _rmsnorm(o_gla, gla_out_g[i]) * jax.nn.silu(gog.reshape(B, S, GLA_HEADS, GLA_VAL_DIM))
        o_gla = o_gla.reshape(B, S, GLA_WIDTH)

        mix = jnp.concatenate([o_nsa, o_gla], axis=-1) @ w_out[i]
        h = h + _rmsnorm(mix, mix_post_g[i])

        f = _swiglu(_rmsnorm(h, ffn2_pre_g[i]), ffn2_w_gate[i], ffn2_w_up[i], ffn2_w_down[i])
        h = h + 0.5 * _rmsnorm(f, ffn2_post_g[i])

        e = p[i] @ ple_proj[i]
        gate = jax.nn.sigmoid(h @ ple_gate[i])
        h = h + _rmsnorm(e * gate, ple_post_g[i])
    return h


_drawn_inputs = setup_inputs


def setup_inputs(seed=0):
    import zlib

    import numpy as np

    out = dict(_drawn_inputs(seed))
    spreads = {}
    factors = {'cmp_k_pe': 7.055,
     'gla_gate_bias': 4.157,
     'gla_out_g': 3.837,
     'ffn2_pre_g': 2.731,
     'ffn2_post_g': 4.03,
     'nsa_out_g': 3.393,
     'ple_post_g': 2.962}
    for name, (base, spread) in spreads.items():
        noise = np.random.default_rng([zlib.crc32(name.encode()), seed]).standard_normal(out[name].shape)
        drawn = base * np.exp(spread * noise) if base else spread * noise
        out[name] = __import__('jax').numpy.asarray(drawn.astype(out[name].dtype))
    for name, factor in factors.items():
        out[name] = (out[name] * factor).astype(out[name].dtype)
    return out
```

```python
import concourse.bass as bass
from concourse import mybir
from concourse.alu_op_type import AluOpType as ALU

ACT = mybir.ActivationFunctionType
AX = mybir.AxisListType
F32 = mybir.dt.float32
F32R = mybir.dt.float32r
BF16 = mybir.dt.bfloat16

P = 128
SEQ = 1024
D = 1024
KC = D // P
HALF = 512
NT = SEQ // P
F = 2816
ITERS = F // (2 * P)
EPS = 1e-6
NEG = -1e30

HEADS = 4
DH = 128
CMP_BLOCK, CMP_STRIDE = 32, 16
N_CMP = (SEQ - CMP_BLOCK) // CMP_STRIDE + 1
CMPW = 64
WINDOW = 512
WT = WINDOW // P
SLC_BLOCK, SLC_TOPK = 64, 16
assert SLC_TOPK >= SEQ // SLC_BLOCK

GK, GV, RANK, CHUNK = 64, 128, 16, 64
PAIRS = 2
N_CHUNK = SEQ // CHUNK
GATE_NORM = 16.0
PLE = 256

IN_NAMES = ["q", "kc", "vc", "ks", "vs", "kw", "vw", "gate", "gq", "gk", "gv", "gdown", "gog"]
IN_SPLITS = [512, 128, 128, 128, 128, 128, 128, 12, 256, 256, 512, 16, 512]
COL = {n: sum(IN_SPLITS[:i]) for i, n in enumerate(IN_NAMES)}
GATES = 3 * HEADS
SMALL = GATES + RANK
VT = 2 * P + SMALL

SLOTS, RAWS, AHEAD = 6, 3, 4
U_FFN = [0, 6 * ITERS + 22 + 8]
U_IN = 6 * ITERS
U_OUT = U_IN + 22
U_PLE = U_FFN[1] + 6 * ITERS
U_END = U_PLE + 2 + KC
assert all(u % SLOTS == 0 for u in U_FFN)

Q0 = [0, 4 * ITERS]
R0 = [0, 16 * ITERS + 16]
R_OUT = 16 * ITERS
R_E = R0[1] + 16 * ITERS
R_G = R_E + 16

IN_PAIRS = [(("q", 0), ("ks", 0)), (("q", 1), ("kw", 0)), (("q", 2), ("gk", 0)), (("q", 3), ("gk", 1)),
            (("gq", 0), ("kc", 0)), (("gq", 1), ("vc", 0)), (("gog", 0), ("gog", 1)), (("gog", 2), ("gog", 3))]
TOK_PAIRS = [(COL["vs"], COL["vw"]), (COL["gv"], COL["gv"] + P), (COL["gv"] + 2 * P, COL["gv"] + 3 * P)]
V_TOK = 4 * len(IN_PAIRS)
V_END = V_TOK + NT * len(TOK_PAIRS)


def tile_owner(v):
    if v < V_TOK:
        p, i = v // 4, v % 2
        return "act" if i == 0 or IN_PAIRS[p][0][0] == "gog" else "dve"
    return "act" if v % 2 == 0 else "dve"


def owner_rank(v):
    return sum(tile_owner(w) == tile_owner(v) for w in range(v + 1))


def passes(hi_lo_w, hi_lo_x):
    return ((hi_lo_w[0], hi_lo_x[0]), (hi_lo_w[0], hi_lo_x[1]), (hi_lo_w[1], hi_lo_x[0]))


VEC_ROWS = [("ffn1_pre_g", 8), ("ffn1_post_g", 8), ("mix_pre_g", 8), ("mix_post_g", 8), ("ffn2_pre_g", 8),
            ("ffn2_post_g", 8), ("ple_post_g", 8), ("nsa_out_g", 4), ("gla_out_g", 4), ("gla_gate_bias", 2)]
VEC_AT = {n: sum(c for _, c in VEC_ROWS[:i]) for i, (n, _) in enumerate(VEC_ROWS)}
NVEC = sum(c for _, c in VEC_ROWS)
HALVED = ("ffn1_post_g", "ffn2_post_g")


def build(nc, A, out):
    base = -(-nc.sbuf_base // 64) * 64

    def place(name, shape, dt, offset):
        return nc.alloc_sbuf_tensor_at(name, shape, dt, offset=offset)

    def size(shape, dt):
        n = 2 if dt == BF16 else 4
        for s in shape[1:]:
            n *= s
        return -(-n // 32) * 32

    class Region:

        def __init__(self, start, end):
            self.at, self.end = start, end

        def take(self, name, shape, dt=F32):
            t = place(name, shape, dt, self.at)
            self.at += size(shape, dt)
            assert self.at <= self.end, (name, self.at, self.end)
            return t

    const = Region(base, nc.sbuf_usable_end)
    ident = const.take("ident", [P, P])
    ones = const.take("ones", [P, P])
    identb = const.take("identb", [P, P], BF16)
    neg_future = const.take("neg_future", [P, P], BF16)
    neg_past = const.take("neg_past", [P, P], BF16)
    neg_cmp = const.take("neg_cmp", [P, NT, CMPW], BF16)
    cmp_valid = const.take("cmp_valid", [P, NT, CMPW])
    gla_causal = const.take("gla_causal", [P, P])
    vec_rows = const.take("vec_rows", [P, P])
    pe_rows = const.take("pe_rows", [2 * CMP_BLOCK, P])
    vec = const.take("vec", [P, NVEC])
    pe = const.take("pe", [P, 2 * CMP_BLOCK])
    rms = const.take("rms", [P, 2, 16])
    rstd = const.take("rstd", [P, 2, 16])
    zero = const.take("zero", [P, 1])
    eps = const.take("eps", [P, 1])
    w_raw = const.take("w_raw", [P, RAWS, KC * P])
    w_hi = const.take("w_hi", [P, SLOTS, KC * P], F32R)
    w_lo = const.take("w_lo", [P, SLOTS, KC * P], F32R)
    u_at = const.at
    u_hi = const.take("u_hi", [P, KC, SEQ], F32R)
    u_lo = const.take("u_lo", [P, KC, SEQ], F32R)
    u_end = const.at
    stage_at, stage_end = const.at, nc.sbuf_usable_end

    ffn = Region(stage_at, stage_end)
    xT = ffn.take("xT", [P, KC, SEQ])
    fT = ffn.take("fT", [P, KC, SEQ])
    h_hi = ffn.take("h_hi", [P, 2, SEQ], F32R)
    h_lo = ffn.take("h_lo", [P, 2, SEQ], F32R)
    sg = ffn.take("sg", [P, 2, HALF])
    h32 = ffn.take("h32", [P, 2, HALF])
    p_in = ffn.take("p_in", [P, 2, PLE])

    mix = Region(stage_at, stage_end)
    oT = mix.take("oT", [P, 2 * HEADS, SEQ])
    qT = mix.take("qT", [P, HEADS, SEQ])
    gq = mix.take("gq", [P, PAIRS, SEQ])
    gv_at = mix.at
    gv = mix.take("gv", [P, NT, HEADS * GV])
    ksT = mix.take("ksT", [P, SEQ])
    kwT = mix.take("kwT", [P, SEQ])
    vtok = mix.take("vtok", [P, NT, VT])
    kcT = mix.take("kcT", [P, CMPW])
    vc = mix.take("vc", [CMPW, P])
    gate = mix.take("gate", [P, NT, GATES])
    pre = Region(stage_at, stage_at + 4 * 2 * HEADS * SEQ)
    kcmp = pre.take("kcmp", [P, 2, SEQ])
    gk = pre.take("gk", [P, PAIRS, SEQ])
    small_raw = pre.take("small_raw", [P, KC, SMALL])
    small_hi = pre.take("small_hi", [P, KC, SMALL], F32R)
    small_lo = pre.take("small_lo", [P, KC, SMALL], F32R)
    gog_out = pre.take("gog_out", [P, 4, HALF])
    gla = Region(u_at, u_end)
    gx = gla.take("gx", [P, PAIRS, SEQ])
    gb = gla.take("gb", [P, PAIRS, SEQ])
    ge = gla.take("ge", [P, PAIRS, SEQ])
    kend = gla.take("kend", [P, NT, PAIRS * P])
    state = gla.take("state", [P, N_CHUNK, PAIRS, GV])
    at_sb = gla.take("at_sb", [P, 2, HEADS * P])
    scan_keep = gla.take("scan_keep", [P, SEQ])
    w1 = gla.take("w1", [P, 2, 8, P])
    kv_a = place("kv_a", [P, 2, SEQ], F32, u_at + 8192 * 4)
    kv_b = place("kv_b", [P, 2, SEQ], F32, u_at + 8192 * 5)
    gla_small = Region(stage_at + 4 * HEADS * SEQ, stage_at + 8 * HEADS * SEQ)
    gdT = gla_small.take("gdT", [RANK, SEQ])
    gup = gla_small.take("gup", [RANK, PAIRS * P])
    decay = gla_small.take("decay", [P, PAIRS, N_CHUNK])
    hid = gla_small.take("hid", [P, 2, CMPW])
    w2 = gla_small.take("w2", [P, 2, P])
    PW = SEQ + WINDOW + P + CMPW
    att = Region(u_at, u_end)
    prob = att.take("prob", [P, 2, HEADS, PW])
    probT = att.take("probT", [P, 4, HALF])
    gog = place("gog", [P, HEADS, SEQ], F32, gv_at)
    mx_at = stage_at + 4 * (2 * HEADS * SEQ + HEADS * SEQ)
    small = Region(mx_at, mx_at + 8192)
    neg_max = small.take("neg_max", [P, 2, 3 * HEADS])
    row_sum = small.take("row_sum", [P, 2, 3 * HEADS])
    inv_sum = small.take("inv_sum", [P, 2, 3 * HEADS])
    p_scale = small.take("p_scale", [P, 2, 3 * HEADS])
    h_diag = place("h_diag", [P, 2, HALF], F32, mx_at)
    h_sq = place("h_sq", [P, 2, HALF], F32, mx_at + 4096)

    PS = nc.alloc_psum_tensor("PS", [P, 8, HALF], F32)

    x_spill = nc.dram_tensor("x_spill", [KC, P, SEQ], F32).ap()
    gog_spill = nc.dram_tensor("gog_spill", [HEADS, P, SEQ], F32).ap()

    def sem(name):
        return nc.alloc_semaphore(name)

    raw_loaded = [sem(f"raw_loaded{i}") for i in range(RAWS)]
    hi_ready, lo_ready = sem("hi_ready"), sem("lo_ready")
    x_loaded = [sem(f"x_loaded{i}") for i in range(4)]
    vec_loaded, masks_made, vec_turned, vec_kept = sem("vec_loaded"), sem("masks_made"), sem("vec_turned"), sem("vec_kept")
    xt_turned, xt_act, xt_dve = sem("xt_turned"), sem("xt_act"), sem("xt_dve")
    sq_ready, sq_used, rms_ready, rstd_ready = sem("sq_ready"), sem("sq_used"), sem("rms_ready"), sem("rstd_ready")
    diag_ready, rb_ready = sem("diag_ready"), sem("rb_ready")
    f_scaled, x_ready = sem("f_scaled"), sem("x_ready")
    u32_ready, uhi_ready, ulo_ready = sem("u32_ready"), sem("uhi_ready"), sem("ulo_ready")
    gu_ready, silu_done, h_done, hhi_ready, hlo_ready = sem("gu_ready"), sem("silu_done"), sem("h_done"), sem("hhi_ready"), sem("hlo_ready")
    f_ready, f_kept = sem("f_ready"), sem("f_kept")
    x_spilled, x_back = sem("x_spilled"), sem("x_back")
    v_ready, v_act, v_dve = sem("v_ready"), sem("v_act"), sem("v_dve")
    small_loaded, small_hi_ready, small_lo_ready = sem("small_loaded"), sem("small_hi_ready"), sem("small_lo_ready")
    gog_spilled = [sem(f"gog_spilled{i}") for i in range(4)]
    gog_back = sem("gog_back")
    gup_loaded, gd_turned, gd_kept, gpre_ready, gx_ready = sem("gup_loaded"), sem("gd_turned"), sem("gd_kept"), sem("gpre_ready"), sem("gx_ready")
    g_act, g_dve = sem("g_act"), sem("g_dve")
    w2_loaded = sem("w2_loaded")
    w1_loaded = [sem("w1_loaded0"), sem("w1_loaded1")]
    w1_used, kv_biased, hid_ready, hid_kept, cmp_ready, cmp_kept = sem("w1_used"), sem("kv_biased"), sem("hid_ready"), sem("hid_kept"), sem("cmp_ready"), sem("cmp_kept")
    kend_turned, kend_kept = sem("kend_turned"), sem("kend_kept")
    outer_ready, state_ready = sem("outer_ready"), sem("state_ready")
    a_ready, a_masked, go_done, go_kept = sem("a_ready"), sem("a_masked"), sem("go_done"), sem("go_kept")
    s_ready, max_done, exp_done, p_scaled, r_ready = sem("s_ready"), sem("max_done"), sem("exp_done"), sem("p_scaled"), sem("r_ready")
    pt_ready, pt_act, pt_dve = sem("pt_ready"), sem("pt_act"), sem("pt_dve")
    o_kept, pv_done = sem("o_kept"), sem("pv_done")
    hsq_ready, hsq_used, hrms_ready, hrstd_ready, hdiag_ready, hrb_ready = (
        sem("hsq_ready"), sem("hsq_used"), sem("hrms_ready"), sem("hrstd_ready"), sem("hdiag_ready"), sem("hrb_ready"))
    hn_scaled, mhi_ready, mlo_ready = sem("hn_scaled"), sem("mhi_ready"), sem("mlo_ready")
    p_loaded = [sem("p_loaded0"), sem("p_loaded1")]
    p_turned, p_hi, p_lo = sem("p_turned"), sem("p_hi"), sem("p_lo")
    sig_done, t_ready = sem("sig_done"), sem("t_ready")
    y_turned, y_act, y_dve = sem("y_turned"), sem("y_act"), sem("y_dve")
    y_stored = [sem(f"y_stored{i}") for i in range(RAWS)]

    def half(t, c, h):
        return t[:, c, h * HALF:(h + 1) * HALF]

    w_gate = [A["ffn1_w_gate"], A["ffn2_w_gate"]]
    w_up = [A["ffn1_w_up"], A["ffn2_w_up"]]
    w_down = [A["ffn1_w_down"], A["ffn2_w_down"]]

    def load_columns(sp, raw, w, col):
        return sp.dma_start(w_raw[:, raw, :].rearrange("p (k f) -> p k f", k=KC),
                            w[0].rearrange("(k p) f -> p k f", p=P)[:, :, bass.ds(col, P)])

    def load_rows(sp, raw, w, row):
        return sp.dma_start(w_raw[:, raw, :], w[0][bass.ds(row, P), :])

    def sp_load(sp, u):
        if u >= RAWS:
            sp.wait_ge(lo_ready, u - RAWS + 1)
        raw = u % RAWS
        for n in range(2):
            if U_FFN[n] <= u < U_FFN[n] + 6 * ITERS:
                t, j = divmod(u - U_FFN[n], 6)
                if j < 4:
                    ins = load_columns(sp, raw, (w_gate, w_up)[j % 2][n], (2 * t + j // 2) * P)
                else:
                    ins = load_rows(sp, raw, w_down[n], (2 * t + j - 4) * P)
        if U_IN <= u < U_OUT:
            p, i = divmod(u - U_IN, 2)
            if p < len(IN_PAIRS):
                name, m = IN_PAIRS[p][i]
                col = COL[name] + m * P
            else:
                col = TOK_PAIRS[p - len(IN_PAIRS)][i]
            ins = load_columns(sp, raw, A["w_in"], col)
        if U_OUT <= u < U_FFN[1]:
            ins = load_columns(sp, raw, A["w_out"], (u - U_OUT) * P)
        if U_PLE <= u < U_PLE + 2:
            ins = load_rows(sp, raw, A["ple_proj"], (u - U_PLE) * P)
        if u >= U_PLE + 2:
            ins = load_columns(sp, raw, A["ple_gate"], (u - U_PLE - 2) * P)
        ins.then_inc(raw_loaded[raw], 16)

    def sp_ffn(sp, n, t, first):
        for j in range(first, 6):
            sp.wait_ge(lo_ready, t * 6 + (U_FFN[n] + j - RAWS + 1))
            if j < 4:
                ins = load_columns(sp, j % RAWS, (w_gate, w_up)[j % 2][n], t * (2 * P) + (j // 2) * P)
            else:
                ins = load_rows(sp, j % RAWS, w_down[n], t * (2 * P) + (j - 4) * P)
            ins.then_inc(raw_loaded[j % RAWS], 16)

    def act_round(act, u, j, free=None):
        if free is not None:
            act.wait_ge(*free)
        act.wait_ge(raw_loaded[j % RAWS], (u // RAWS + 1) * 16 if isinstance(u, int) else u)
        act.activation(w_hi[:, j % SLOTS, :], w_raw[:, j % RAWS, :], ACT.Copy).then_inc(hi_ready, 1)

    def dve_rest(dve, u, j):
        dve.wait_ge(hi_ready, u + 1)
        dve.tensor_tensor(w_lo[:, j % SLOTS, :], w_raw[:, j % RAWS, :], w_hi[:, j % SLOTS, :].bitcast(F32),
                          ALU.subtract).then_inc(lo_ready, 1)

    def act_norm(act, k, src, ready):
        h = k % 2
        for c in range(KC):
            i = KC * k + c
            act.wait_ge(*ready(h, c))
            if i >= 2:
                act.wait_ge(sq_used, i - 1)
            act.activation(sg[:, i % 2, :], half(src, c, h), ACT.Square).then_inc(sq_ready, 1)
        act.wait_ge(sq_used, KC * (k + 1))
        if k >= 2:
            act.wait_ge(rstd_ready, k - 1)
        act.activation(rms[:, h, 0:4], PS[:, h, 0:4], ACT.Sqrt, scale=1.0 / D, bias=eps[:, 0:1]).then_inc(rms_ready, 1)

    def pe_norm(pe_, k):
        h = k % 2
        for c in range(KC):
            i = KC * k + c
            pe_.wait_ge(sq_ready, i + 1)
            for t in range(4):
                mm = pe_.matmul(PS[:, h, t:t + 1], sg[:, i % 2, t * P:(t + 1) * P], ones[:, 0:1],
                                start=(c == 0 and t == 0), stop=(c == KC - 1), skip_group_check=True)
            mm.then_inc(sq_used, 1)
        pe_.wait_ge(diag_ready, k + 1)
        pe_.matmul(PS[:, 2 + h, :], ones[:, :], h32[:, h, :], start=True, stop=True).then_inc(rb_ready, 1)

    def dve_norm(dve, k):
        h = k % 2
        dve.wait_ge(rms_ready, k + 1)
        dve.reciprocal(rstd[:, h, 0:4], rms[:, h, 0:4]).then_inc(rstd_ready, 1)
        dve.wait_ge(rstd_ready, k + 1)
        dve.tensor_tensor(h32[:, h, :].rearrange("p (t q) -> p t q", t=4),
                          ident[:, :].unsqueeze(1).to_broadcast([P, 4, P]),
                          rstd[:, h, 0:4].unsqueeze(2).to_broadcast([P, 4, P]), ALU.mult).then_inc(diag_ready, 1)

    def dve_residual(dve, pi, k, gain):
        h = k % 2
        dve.wait_ge(rb_ready, k + 1)
        for c in range(KC):
            g = vec[:, VEC_AT[gain] + c:VEC_AT[gain] + c + 1]
            dve.scalar_tensor_tensor(half(fT, c, h), half(fT, c, h), g, PS[:, 2 + h, :], ALU.mult, ALU.mult)\
               .then_inc(f_scaled, 1)
        for c in range(KC):
            dve.wait_ge(f_scaled, 16 * pi + 8 * h + c + 1)
            dve.tensor_tensor(half(xT, c, h), half(xT, c, h), half(fT, c, h), ALU.add).then_inc(x_ready, 1)

    def dve_apply(dve, a, k, gain):
        h = k % 2
        dve.wait_ge(rb_ready, k + 1)
        for c in range(KC + 1):
            if c < KC:
                g = vec[:, VEC_AT[gain] + c:VEC_AT[gain] + c + 1]
                if a > 0:
                    dve.wait_ge(x_ready, 16 * (a - 1) + 8 * h + c + 1)
                dve.scalar_tensor_tensor(half(fT, c, h), half(xT, c, h), g, PS[:, 2 + h, :], ALU.mult, ALU.mult)\
                   .then_inc(u32_ready, 1)
            if c > 0:
                dve_lo(dve, a, h, c - 1, fT)

    def dve_lo(dve, a, h, c, src):
        dve.wait_ge(uhi_ready, 16 * a + 8 * h + c + 1)
        dve.tensor_tensor(half(u_lo, c, h), half(src, c, h), half(u_hi, c, h).bitcast(F32), ALU.subtract)\
           .then_inc(ulo_ready, 1)

    def act_hi(act, a, h, src, ready):
        for c in range(KC):
            act.wait_ge(*ready(h, c))
            act.activation(half(u_hi, c, h), half(src, c, h), ACT.Copy).then_inc(uhi_ready, 1)

    def pe_gate_up(pe_, n, t, c, h, first):
        q = 2 * c + h
        if not (first and n == 0 and q < 2):
            pe_.wait_ge(h_done, t * 4 + (Q0[n] + q - 1))
        for i in range(2):
            if h == 0:
                pe_.wait_ge(lo_ready, t * 6 + (U_FFN[n] + 2 * c + i + 1))
            for k in range(KC):
                if first and c == 0 and i == 0:
                    pe_.wait_ge(ulo_ready, 16 * 2 * n + 8 * h + k + 1)
                w = [x[:, 2 * c + i, k * P:(k + 1) * P] for x in (w_hi, w_lo)]
                for s, (a, b) in enumerate(passes(w, [half(x, k, h) for x in (u_hi, u_lo)])):
                    mm = pe_.matmul(PS[:, 2 * i + h, :], a, b, start=(k == 0 and s == 0), stop=(k == KC - 1 and s == 2))
            mm.then_inc(gu_ready, 1)

    def pe_down(pe_, n, t, first):
        pe_.wait_ge(lo_ready, t * 6 + (U_FFN[n] + 6))
        for h in range(2):
            pe_.wait_ge(hlo_ready, t * 4 + (Q0[n] + 2 + h + 1))
            for m in range(KC):
                r = 8 * h + m
                if not (first and n == 0 and r < 4):
                    pe_.wait_ge(f_kept, t * 16 + (R0[n] + r - 3))
                for c in range(2):
                    w = [x[:, 4 + c, m * P:(m + 1) * P] for x in (w_hi, w_lo)]
                    for s, (a, b) in enumerate(passes(w, [half(x, c, h) for x in (h_hi, h_lo)])):
                        mm = pe_.matmul(PS[:, 4 + r % 4, :], a, b, start=(c == 0 and s == 0), stop=(c == 1 and s == 2))
                mm.then_inc(f_ready, 1)

    def pe_ffn(pe_, n, t, first):
        for c in range(2):
            for h in range(2):
                pe_gate_up(pe_, n, t, c, h, first)
        pe_down(pe_, n, t, first)

    def act_ffn(act, n, t, first):
        for c in range(3):
            free = [(f_ready, t * 16 + R0[n]), (gu_ready, t * 8 + (2 * Q0[n] + 4)), (gu_ready, t * 8 + (2 * Q0[n] + 8))][c]
            if first and n == 0 and c == 0:
                free = None
            for i in range(2):
                j = 2 * c + i + AHEAD
                landed = t * 32 + ((U_FFN[n] + j) // RAWS + 1) * 16
                if free is not None:
                    act.wait_ge(*free)
                act.wait_ge(raw_loaded[j % RAWS], landed)
                act.activation(w_hi[:, j % SLOTS, :], w_raw[:, j % RAWS, :], ACT.Copy).then_inc(hi_ready, 1)
            if c == 2:
                break
            for h in range(2):
                q = 2 * c + h
                act.wait_ge(gu_ready, t * 8 + (2 * (Q0[n] + q) + 1))
                if not (first and n == 0 and q < 2):
                    act.wait_ge(h_done, t * 4 + (Q0[n] + q - 1))
                act.activation(sg[:, h, :], PS[:, h, :], ACT.Silu).then_inc(silu_done, 1)

    def dve_ffn(dve, n, t, first):
        for c in range(3):
            for i in range(2):
                j = 2 * c + i + AHEAD
                dve_rest(dve, t * 6 + (U_FFN[n] + j), j)
            if c == 2:
                break
            for h in range(2):
                q = 2 * c + h
                dve.wait_ge(silu_done, t * 4 + (Q0[n] + q + 1))
                dve.wait_ge(gu_ready, t * 8 + (2 * (Q0[n] + q) + 2))
                if not (first and n == 0 and q < 2):
                    dve.wait_ge(hlo_ready, t * 4 + (Q0[n] + q - 1))
                dve.tensor_tensor(h32[:, h, :], sg[:, h, :], PS[:, 2 + h, :], ALU.mult).then_inc(h_done, 1)
                dve.wait_ge(h_done, t * 4 + (Q0[n] + q + 1))
                if not (first and n == 0):
                    dve.wait_ge(f_ready, t * 16 + (R0[n] - 16 + 8 * (h + 1)))
                dve.tensor_copy(half(h_hi, c, h), h32[:, h, :]).then_inc(hhi_ready, 1)
                dve.wait_ge(hhi_ready, t * 4 + (Q0[n] + q + 1))
                dve.tensor_tensor(half(h_lo, c, h), h32[:, h, :], half(h_hi, c, h).bitcast(F32), ALU.subtract)\
                   .then_inc(hlo_ready, 1)
        for h in range(2):
            for m in range(KC):
                r = 8 * h + m
                dve.wait_ge(f_ready, t * 16 + (R0[n] + r + 1))
                if first:
                    dve.tensor_copy(half(fT, m, h), PS[:, 4 + r % 4, :]).then_inc(f_kept, 1)
                else:
                    dve.wait_ge(f_kept, t * 16 + (R0[n] + r - 15))
                    dve.tensor_tensor(half(fT, m, h), half(fT, m, h), PS[:, 4 + r % 4, :], ALU.add).then_inc(f_kept, 1)

    def f_done(n):
        return lambda h, c: (f_kept, R0[n] + 16 * (ITERS - 1) + 8 * h + c + 1)

    def x_done(pi):
        return lambda h, c: (x_ready, 16 * pi + 8 * h + c + 1)

    def u32_done(a):
        return lambda h, c: (u32_ready, 16 * a + 8 * h + c + 1)

    with nc.Block() as block:
        @block.sync
        def _(sp):
            for i in range(4):
                sp.dma_start(fT[:, 2 * i:2 * i + 2, :], A["x"][0].rearrange("(t p) d -> p t d", p=P)[:, 2 * i:2 * i + 2, :])\
                  .then_inc(x_loaded[i], 16)
                if i == 0:
                    for name, rows in VEC_ROWS:
                        src = A[name].rearrange("l (c p) -> (l c) p", p=P) if len(A[name].shape) == 2 \
                            else A[name].rearrange("l c p -> (l c) p")
                        sp.dma_start(vec_rows[VEC_AT[name]:VEC_AT[name] + rows, :], src).then_inc(vec_loaded, 16)
                    for i2, name in enumerate(("cmp_k_pe", "cmp_v_pe")):
                        sp.dma_start(pe_rows[i2 * CMP_BLOCK:(i2 + 1) * CMP_BLOCK, :], A[name][0]).then_inc(vec_loaded, 16)
            for u in range(RAWS):
                sp_load(sp, u)

        @block.gpsimd
        def _(pool):
            pool.memset(ident[:, :], 0.0).then_inc(masks_made, 1)
            pool.memset(identb[:, :], 0.0).then_inc(masks_made, 1)
            pool.memset(neg_future[:, :], 0.0).then_inc(masks_made, 1)
            pool.memset(neg_past[:, :], 0.0).then_inc(masks_made, 1)
            pool.memset(neg_cmp[:, :, :], 0.0).then_inc(masks_made, 1)
            pool.memset(cmp_valid[:, :, :], 1.0).then_inc(masks_made, 1)
            pool.memset(gla_causal[:, :], 1.0).then_inc(masks_made, 1)
            pool.wait_ge(masks_made, 7)
            for m in (ident, identb):
                pool.affine_select(out=m[:, :], in_=m[:, :], compare_op=ALU.not_equal, fill=1.0, base=0,
                                   pattern=[[-1, P]], channel_multiplier=1).then_inc(masks_made, 1)
            pool.affine_select(out=neg_future[:, :], in_=neg_future[:, :], compare_op=ALU.is_ge, fill=NEG, base=0,
                               pattern=[[-1, P]], channel_multiplier=1).then_inc(masks_made, 1)
            pool.affine_select(out=neg_past[:, :], in_=neg_past[:, :], compare_op=ALU.is_gt, fill=NEG, base=0,
                               pattern=[[1, P]], channel_multiplier=-1).then_inc(masks_made, 1)
            for m, fill in ((neg_cmp, NEG), (cmp_valid, 0.0)):
                pool.affine_select(out=m[:, :, :], in_=m[:, :, :], compare_op=ALU.is_ge, fill=fill,
                                   base=-(CMP_BLOCK - 1), pattern=[[P, NT], [-CMP_STRIDE, CMPW]],
                                   channel_multiplier=1).then_inc(masks_made, 1)
            pool.affine_select(out=gla_causal[:, :], in_=gla_causal[:, :], compare_op=ALU.is_ge, fill=0.0, base=0,
                               pattern=[[1, P]], channel_multiplier=-1).then_inc(masks_made, 1)
            pool.wait_ge(masks_made, 14)
            pool.memset(gla_causal[0:CHUNK, CHUNK:P], 0.0).then_inc(masks_made, 1)

        @block.tensor
        def _(pe_):
            pe_.wait_ge(masks_made, 8)
            pe_.wait_ge(vec_loaded, 16 * (len(VEC_ROWS) + 2))
            pe_.transpose(PS[:, 0, 0:NVEC], vec_rows[0:NVEC, :], ident[0:NVEC, 0:NVEC]).then_inc(vec_turned, 1)
            pe_.transpose(PS[:, 1, 0:2 * CMP_BLOCK], pe_rows[:, :], ident[0:2 * CMP_BLOCK, 0:2 * CMP_BLOCK]).then_inc(vec_turned, 1)
            for h in range(2):
                for c in range(KC):
                    r = KC * h + c
                    if c == 0:
                        pe_.wait_ge(x_loaded[2 * h], 16)
                        pe_.wait_ge(x_loaded[2 * h + 1], 16)
                    if r >= 6:
                        pe_.wait_ge((xt_act, xt_dve)[r % 2], (r - 6) // 2 + 1)
                    for t in range(4):
                        mm = pe_.transpose(PS[:, 2 + r % 6, t * P:(t + 1) * P], fT[:, 4 * h + t, c * P:(c + 1) * P], ident[:, :])
                    mm.then_inc(xt_turned, 1)

        @block.scalar
        def _(act):
            for r in range(0, 2 * KC, 2):
                act.wait_ge(xt_turned, r + 1)
                act.activation(half(xT, r % KC, r // KC), PS[:, 2 + r % 6, :], ACT.Copy).then_inc(xt_act, 1)

        @block.vector
        def _(dve):
            dve.memset(ones[:, :], 1.0)
            dve.memset(eps[:, :], EPS)
            dve.memset(zero[:, :], 0.0)
            dve.wait_ge(vec_turned, 1)
            dve.tensor_copy(vec[:, :], PS[:, 0, 0:NVEC]).then_inc(vec_kept, 1)
            dve.wait_ge(vec_turned, 2)
            dve.tensor_copy(pe[:, :], PS[:, 1, 0:2 * CMP_BLOCK])
            dve.wait_ge(vec_kept, 1)
            for name in HALVED:
                g = vec[:, VEC_AT[name]:VEC_AT[name] + KC]
                dve.tensor_scalar(g, g, 0.5, None, ALU.mult)
            for r in range(1, 2 * KC, 2):
                dve.wait_ge(xt_turned, r + 1)
                dve.tensor_copy(half(xT, r % KC, r // KC), PS[:, 2 + r % 6, :]).then_inc(xt_dve, 1)

    with nc.Block() as block:
        @block.sync
        def _(sp):
            for u in range(RAWS, 6):
                sp_load(sp, u)
            with sp.Fori(1, ITERS) as t:
                sp_ffn(sp, 0, t, 0)
            for u in range(U_IN, U_IN + AHEAD + RAWS):
                sp_load(sp, u)
            for c in range(KC):
                sp.wait_ge(x_ready, 8 + c + 1)
                sp.dma_start(x_spill[c], xT[:, c, :]).then_inc(x_spilled, 16)

        @block.scalar
        def _(act):
            act_norm(act, 0, xT, lambda h, c: (xt_turned, 1))
            for u in range(AHEAD):
                act_round(act, u, u)
                if u == 1:
                    act_hi(act, 0, 0, fT, u32_done(0))
            act_norm(act, 1, xT, lambda h, c: (xt_turned, 1))
            act_hi(act, 0, 1, fT, u32_done(0))
            act_ffn(act, 0, 0, True)
            with act.Fori(1, ITERS) as t:
                act_ffn(act, 0, t, False)
            for k in (2, 3):
                act_norm(act, k, fT, f_done(0))
            for k in (4, 5):
                act_norm(act, k, xT, x_done(0))
            for h in range(2):
                act_hi(act, 1, h, fT, u32_done(1))

        @block.vector
        def _(dve):
            dve_norm(dve, 0)
            for u in range(2):
                dve_rest(dve, u, u)
            dve_apply(dve, 0, 0, "ffn1_pre_g")
            for u in range(2, AHEAD):
                dve_rest(dve, u, u)
            dve_norm(dve, 1)
            dve_apply(dve, 0, 1, "ffn1_pre_g")
            dve_ffn(dve, 0, 0, True)
            with dve.Fori(1, ITERS) as t:
                dve_ffn(dve, 0, t, False)
            for k in (2, 3):
                dve_norm(dve, k)
                dve_residual(dve, 0, k, "ffn1_post_g")
            for k in (4, 5):
                dve_norm(dve, k)
                dve_apply(dve, 1, k, "mix_pre_g")

        @block.tensor
        def _(pe_):
            pe_norm(pe_, 0)
            pe_norm(pe_, 1)
            pe_ffn(pe_, 0, 0, True)
            with pe_.Fori(1, ITERS) as t:
                pe_ffn(pe_, 0, t, False)
            for k in (2, 3, 4, 5):
                pe_norm(pe_, k)

    def fm_target(name, m, h):
        if name == "q":
            return half(qT, m, h), float(DH) ** -0.5
        if name == "gq":
            return half(gq, m, h), float(GK) ** -0.5
        if name == "ks":
            return ksT[:, h * HALF:(h + 1) * HALF], 1.0
        if name == "kw":
            return kwT[:, h * HALF:(h + 1) * HALF], 1.0
        if name == "gk":
            return half(gk, m, h), 1.0
        return half(kcmp, "kc vc".split().index(name), h), 1.0

    def in_free(p):
        if p == 0:
            return f_ready, R_OUT
        return v_ready, 4 * p if p <= len(IN_PAIRS) else V_TOK + NT * (p - len(IN_PAIRS))

    with nc.Block() as block:
        @block.sync
        def _(sp):
            for u in range(U_IN + AHEAD + RAWS, U_OUT + AHEAD + RAWS):
                sp_load(sp, u)

        @block.scalar
        def _(act):
            w_in_k = A["w_in"][0].rearrange("(k p) f -> p k f", p=P)
            for p in range(len(IN_PAIRS) + len(TOK_PAIRS)):
                for i in range(2):
                    u = U_IN + 2 * p + i + AHEAD
                    act_round(act, u, u, in_free(p))
                if p == 2:
                    act.wait_ge(x_spilled, 16 * KC)
                    act.dma_start(small_raw[:, :, 0:GATES], w_in_k[:, :, COL["gate"]:COL["gate"] + GATES]).then_inc(small_loaded, 16)
                    act.dma_start(small_raw[:, :, GATES:SMALL], w_in_k[:, :, COL["gdown"]:COL["gdown"] + RANK]).then_inc(small_loaded, 16)
                if p == 6:
                    act.wait_ge(small_loaded, 32)
                    act.activation(small_hi[:, :, :], small_raw[:, :, :], ACT.Copy).then_inc(small_hi_ready, 1)
                if p < len(IN_PAIRS):
                    for h in range(2):
                        for i in range(2):
                            v = 4 * p + 2 * h + i
                            if tile_owner(v) != "act":
                                continue
                            act.wait_ge(v_ready, v + 1)
                            name, m = IN_PAIRS[p][i]
                            if name == "gog":
                                g = v % 4
                                if m >= 2:
                                    act.wait_ge(gog_spilled[g], 16)
                                act.activation(gog_out[:, g, :], PS[:, v % 8, :], ACT.Silu).then_inc(v_act, 1)
                                act.wait_ge(v_act, owner_rank(v))
                                act.dma_start(gog_spill[m, :, h * HALF:(h + 1) * HALF], gog_out[:, g, :])\
                                   .then_inc(gog_spilled[g], 16)
                            else:
                                dst, scale = fm_target(name, m, h)
                                act.activation(dst, PS[:, v % 8, :], ACT.Copy, scale=scale).then_inc(v_act, 1)
                else:
                    n = p - len(IN_PAIRS)
                    for t in range(0, NT, 2):
                        v = V_TOK + NT * n + t
                        act.wait_ge(v_ready, v + 1)
                        dst, w = (vtok[:, t, :], VT) if n == 0 else (gv[:, t, (n - 1) * 2 * P:n * 2 * P], 2 * P)
                        act.activation(dst, PS[:, v % 8, 0:w], ACT.Copy).then_inc(v_act, 1)
            for g in range(4):
                act.wait_ge(gog_spilled[g], 32)

        @block.vector
        def _(dve):
            for p in range(len(IN_PAIRS) + len(TOK_PAIRS)):
                for i in range(2):
                    u = U_IN + 2 * p + i + AHEAD
                    dve_rest(dve, u, u)
                if p == 2:
                    dve.wait_ge(x_spilled, 16 * KC)
                if p == 6:
                    dve.wait_ge(small_hi_ready, 1)
                    dve.tensor_tensor(small_lo[:, :, :], small_raw[:, :, :], small_hi[:, :, :].bitcast(F32), ALU.subtract)\
                       .then_inc(small_lo_ready, 1)
                if p < len(IN_PAIRS):
                    for h in range(2):
                        for i in range(2):
                            v = 4 * p + 2 * h + i
                            if tile_owner(v) != "dve":
                                continue
                            dve.wait_ge(v_ready, v + 1)
                            dst, _scale = fm_target(*IN_PAIRS[p][i], h)
                            dve.tensor_copy(dst, PS[:, v % 8, :]).then_inc(v_dve, 1)
                else:
                    n = p - len(IN_PAIRS)
                    for t in range(1, NT, 2):
                        v = V_TOK + NT * n + t
                        dve.wait_ge(v_ready, v + 1)
                        dst, w = (vtok[:, t, :], VT) if n == 0 else (gv[:, t, (n - 1) * 2 * P:n * 2 * P], 2 * P)
                        dve.tensor_copy(dst, PS[:, v % 8, 0:w]).then_inc(v_dve, 1)

        @block.tensor
        def _(pe_):
            def bank_free(v):
                if v >= 8:
                    pe_.wait_ge(v_act if tile_owner(v - 8) == "act" else v_dve, owner_rank(v - 8))

            for p in range(len(IN_PAIRS)):
                for h in range(2):
                    for i in range(2):
                        v = 4 * p + 2 * h + i
                        bank_free(v)
                        u = U_IN + 2 * p + i
                        if h == 0:
                            pe_.wait_ge(lo_ready, u + 1)
                        for k in range(KC):
                            w = [x[:, u % SLOTS, k * P:(k + 1) * P] for x in (w_hi, w_lo)]
                            for s, (a, b) in enumerate(passes(w, [half(x, k, h) for x in (u_hi, u_lo)])):
                                mm = pe_.matmul(PS[:, v % 8, :], a, b, start=(k == 0 and s == 0), stop=(k == KC - 1 and s == 2))
                        mm.then_inc(v_ready, 1)
            for n in range(len(TOK_PAIRS)):
                u = U_IN + 2 * (len(IN_PAIRS) + n)
                pe_.wait_ge(lo_ready, u + 2)
                if n == 0:
                    pe_.wait_ge(small_lo_ready, 1)
                for t in range(NT):
                    v = V_TOK + NT * n + t
                    bank_free(v)
                    for k in range(KC):
                        x = [y[:, k, t * P:(t + 1) * P] for y in (u_hi, u_lo)]
                        w = [y[:, u % SLOTS:u % SLOTS + 2, k * P:(k + 1) * P] for y in (w_hi, w_lo)]
                        for s, (a, b) in enumerate(passes(x, w)):
                            mm = pe_.matmul(PS[:, v % 8, 0:2 * P].rearrange("p (a b) -> p a b", a=2), a, b,
                                            start=(k == 0 and s == 0), stop=(k == KC - 1 and s == 2))
                    if n == 0:
                        for k in range(KC):
                            x = [y[:, k, t * P:(t + 1) * P] for y in (u_hi, u_lo)]
                            w = [y[:, k, :] for y in (small_hi, small_lo)]
                            for s, (a, b) in enumerate(passes(x, w)):
                                mm = pe_.matmul(PS[:, v % 8, 2 * P:VT], a, b, start=(k == 0 and s == 0),
                                                stop=(k == KC - 1 and s == 2))
                    mm.then_inc(v_ready, 1)

    with nc.Block() as block:
        W1 = [A["cmp_k_w1"][0], A["cmp_v_w1"][0]]
        NW1 = CMP_BLOCK // 8

        def outer(n, pair):
            col = ((n // 2) % 2 * PAIRS + pair) * P
            return PS[:, 4 * (n % 2) + n // 4, col:col + P]

        @block.sync
        def _(sp):
            sp.dma_start(gup[:, :], A["gla_gate_up"][0]).then_inc(gup_loaded, 16)
            for n in range(2):
                sp.dma_start(w2[:, n, :], A[("cmp_k_w2", "cmp_v_w2")[n]][0]).then_inc(w2_loaded, 16)
            for i in range(2 * NW1):
                n, l0 = i // NW1, (i % NW1) * 8
                if i >= 2:
                    sp.wait_ge(w1_used, i - 1)
                sp.dma_start(w1[:, i % 2, :, :], W1[n][l0:l0 + 8].rearrange("l d e -> d l e")).then_inc(w1_loaded[i % 2], 16)

        @block.scalar
        def _(act):
            flat = [x[:, :, :].rearrange("p a b -> p (a b)") for x in (gx, gb, ge)]
            act.activation(gate[:, :, :], vtok[:, :, 2 * P:2 * P + GATES], ACT.Sigmoid)
            act.wait_ge(gx_ready, 4)
            act.activation(flat[1], flat[0], ACT.Abs).then_inc(g_act, 1)
            act.wait_ge(g_act, 1)
            act.activation(flat[1], flat[1], ACT.Exp, scale=-1.0).then_inc(g_act, 1)
            act.wait_ge(g_act, 2)
            act.activation(flat[1], flat[1], ACT.Ln, bias=1.0).then_inc(g_act, 1)
            act.wait_ge(g_dve, 3)
            act.activation(flat[2], flat[1], ACT.Exp, scale=1.0 / GATE_NORM).then_inc(g_act, 1)
            act.wait_ge(g_dve, 4)
            act.activation(flat[0], flat[0], ACT.Exp, scale=1.0 / GATE_NORM).then_inc(g_act, 1)
            act.wait_ge(g_dve, 5)
            act.activation(flat[2], flat[1], ACT.Exp, scale=-1.0 / GATE_NORM).then_inc(g_act, 1)
            b_last = gb[:, :, :].rearrange("p a (n c) -> p a n c", c=CHUNK)[:, :, :, CHUNK - 1]
            act.activation(decay[:, :, :], b_last, ACT.Exp, scale=1.0 / GATE_NORM).then_inc(g_act, 1)
            for n in range(2):
                act.wait_ge(hid_ready, n + 1)
                act.activation(hid[:, n, 0:N_CMP], PS[:, 6 + n, 0:N_CMP], ACT.Silu).then_inc(hid_kept, 1)
            for j in range(4):
                act.wait_ge(kend_turned, j + 1)
                act.activation(kend[:, 2 * j:2 * j + 2, :], PS[:, j, :].rearrange("p (a b) -> p a b", a=2), ACT.Copy)\
                   .then_inc(kend_kept, 1)
            for h in range(2):
                act.wait_ge(go_done, 4 * (h + 1))
                for hd in range(HEADS):
                    act.activation(half(oT, HEADS + hd, h), PS[:, hd, :], ACT.Copy).then_inc(go_kept, 1)

        @block.vector
        def _(dve):
            keep = scan_keep[:, :].rearrange("p (n c) -> p n c", c=CHUNK)
            chain = lambda n: dve.wait_ge(g_dve, n)
            for j in range(2):
                dve.wait_ge(gd_turned, j + 1)
                dve.tensor_copy(gdT[:, j * HALF:(j + 1) * HALF], PS[0:RANK, j, :]).then_inc(gd_kept, 1)
            for j in range(4):
                pair, h = divmod(j, 2)
                dve.wait_ge(gpre_ready, j + 1)
                bias = vec[:, VEC_AT["gla_gate_bias"] + pair:VEC_AT["gla_gate_bias"] + pair + 1]
                dve.tensor_scalar(half(gx, pair, h), PS[:, 2 + j, :], bias, None, ALU.add).then_inc(gx_ready, 1)
            for n in range(2):
                src = kcmp[:, n, :].rearrange("p (n c) -> p n c", c=CMP_STRIDE)
                for hb, dst in ((0, kv_a), (1, kv_b)):
                    at0 = n * CMP_BLOCK + hb * CMP_STRIDE
                    dve.tensor_tensor(dst[:, n, :].rearrange("p (n c) -> p n c", c=CMP_STRIDE), src,
                                      pe[:, at0:at0 + CMP_STRIDE].unsqueeze(1).to_broadcast([P, SEQ // CMP_STRIDE, CMP_STRIDE]),
                                      ALU.add).then_inc(kv_biased, 1)
            dve.memset(kcT[:, :], 0.0).then_inc(cmp_kept, 1)
            dve.memset(vc[:, :], 0.0).then_inc(cmp_kept, 1)
            dve.memset(scan_keep[:, :], 1.0).then_inc(cmp_kept, 1)
            dve.wait_ge(cmp_kept, 3)
            dve.memset(keep[:, :, 0:1], 0.0).then_inc(cmp_kept, 1)
            dve.wait_ge(g_act, 3)
            flat = [x[:, :, :].rearrange("p a b -> p (a b)") for x in (gx, gb, ge)]
            dve.scalar_tensor_tensor(flat[0], flat[0], 0.0, flat[1], ALU.min, ALU.subtract).then_inc(g_dve, 1)
            chain(1)
            dve.wait_ge(cmp_kept, 4)
            for pair in range(PAIRS):
                dve.tensor_tensor_scan(gb[:, pair, :], scan_keep[:, :], gx[:, pair, :], 0.0, ALU.mult, ALU.add)\
                   .then_inc(g_dve, 1)
            chain(3)
            by_chunk = [x[:, :, :].rearrange("p a (n c) -> p (a n) c", c=CHUNK) for x in (gx, gb)]
            dve.tensor_tensor(by_chunk[0], by_chunk[1][:, :, CHUNK - 1:CHUNK].to_broadcast([P, PAIRS * N_CHUNK, CHUNK]),
                              by_chunk[1], ALU.subtract).then_inc(g_dve, 1)
            dve.wait_ge(g_act, 4)
            dve.tensor_tensor(gq[:, :, :], gq[:, :, :], ge[:, :, :], ALU.mult).then_inc(g_dve, 1)
            dve.wait_ge(g_act, 5)
            dve.tensor_tensor(gx[:, :, :], gx[:, :, :], gk[:, :, :], ALU.mult).then_inc(g_dve, 1)
            chain(6)
            dve.wait_ge(g_act, 6)
            dve.tensor_tensor(gk[:, :, :], gk[:, :, :], ge[:, :, :], ALU.mult).then_inc(g_dve, 1)
            dve.wait_ge(cmp_ready, 1)
            dve.tensor_copy(kcT[:, 0:N_CMP], PS[:, 6, P:P + N_CMP]).then_inc(cmp_kept, 1)
            dve.wait_ge(cmp_ready, 2)
            dve.tensor_copy(vc[0:N_CMP, :], PS[0:N_CMP, 7, P:2 * P]).then_inc(cmp_kept, 1)
            dve.wait_ge(g_act, 7)
            for n in range(N_CHUNK - 1):
                dve.wait_ge(outer_ready, min(n // 4 * 4 + 2 + n % 2, N_CHUNK - 2) + 1)
                if n > 0:
                    dve.wait_ge(state_ready, 2 * n)
                for pair in range(PAIRS):
                    add = outer(n, pair)
                    if n == 0:
                        dve.tensor_copy(state[:, 1, pair, :], add).then_inc(state_ready, 1)
                    else:
                        dve.scalar_tensor_tensor(state[:, n + 1, pair, :], state[:, n, pair, :], decay[:, pair, n:n + 1],
                                                 add, ALU.mult, ALU.add).then_inc(state_ready, 1)
            for t in range(NT):
                dve.wait_ge(a_ready, t + 1)
                if t >= 2:
                    dve.wait_ge(go_done, t - 1)
                dve.tensor_tensor(at_sb[:, t % 2, :].rearrange("p (a b i) -> p a b i", a=2, b=2),
                                  PS[:, 4 + 2 * (t % 2):6 + 2 * (t % 2), 0:2 * P].rearrange("p a (b i) -> p a b i", b=2),
                                  gla_causal[:, :].unsqueeze(1).unsqueeze(1).to_broadcast([P, 2, 2, P]), ALU.mult).then_inc(a_masked, 1)

        @block.tensor
        def _(pe_):
            for t in range(NT):
                mm = pe_.transpose(PS[0:RANK, t // 4, (t % 4) * P:(t % 4 + 1) * P], vtok[:, t, 2 * P + GATES:VT], ident[:, :])
                if t % 4 == 3:
                    mm.then_inc(gd_turned, 1)
            pe_.wait_ge(gup_loaded, 16)
            for j in range(4):
                pair, h = divmod(j, 2)
                pe_.wait_ge(gd_kept, h + 1)
                pe_.matmul(PS[:, 2 + j, :], gup[:, pair * P:(pair + 1) * P], gdT[:, h * HALF:(h + 1) * HALF],
                           start=True, stop=True).then_inc(gpre_ready, 1)
            for i in range(2 * NW1):
                n = i // NW1
                if i % NW1 == 0:
                    pe_.wait_ge(kv_biased, 2 * n + 2)
                pe_.wait_ge(w1_loaded[i % 2], 16 * (i // 2 + 1))
                for l8 in range(8):
                    l = (i % NW1) * 8 + l8
                    src = (kv_a, kv_b)[l // CMP_STRIDE]
                    mm = pe_.matmul(PS[:, 6 + n, 0:N_CMP], w1[:, i % 2, l8, :],
                                    src[:, n, l:l + CMP_STRIDE * (N_CMP - 1) + 1:CMP_STRIDE],
                                    start=(l == 0), stop=(l == CMP_BLOCK - 1))
                if i % NW1 == NW1 - 1:
                    mm.then_inc(hid_ready, 1)
                else:
                    mm.then_inc(w1_used, 1)
            pe_.wait_ge(w2_loaded, 32)
            pe_.wait_ge(hid_kept, 1)
            pe_.matmul(PS[:, 6, P:P + N_CMP], w2[:, 0, :], hid[:, 0, 0:N_CMP], start=True, stop=True).then_inc(cmp_ready, 1)
            pe_.wait_ge(hid_kept, 2)
            pe_.matmul(PS[0:N_CMP, 7, P:2 * P], hid[:, 1, 0:N_CMP], w2[:, 1, :], start=True, stop=True).then_inc(cmp_ready, 1)
            pe_.wait_ge(g_dve, 6)
            pe_.wait_ge(gx_ready, 4)
            for j in range(4):
                for i in range(4):
                    t, pair = 2 * j + i // 2, i % 2
                    mm = pe_.transpose(PS[:, j, i * P:(i + 1) * P], gx[:, pair, t * P:(t + 1) * P], ident[:, :])
                mm.then_inc(kend_turned, 1)
            pe_.wait_ge(cmp_kept, 6)
            for n in range(N_CHUNK - 1):
                t, lo = n // 2, (n % 2) * CHUNK
                if n % 4 == 0:
                    pe_.wait_ge(kend_kept, n // 4 + 1)
                if n == 0:
                    pe_.wait_ge(kend_kept, 4)
                for hd in range(HEADS):
                    pair, hh = divmod(hd, 2)
                    mm = pe_.matmul(outer(n, pair)[hh * GK:(hh + 1) * GK, :],
                                    kend[lo:lo + CHUNK, t, hd * GK:(hd + 1) * GK],
                                    gv[lo:lo + CHUNK, t, hd * GV:(hd + 1) * GV], start=True, stop=True)
                mm.then_inc(outer_ready, 1)
            pe_.wait_ge(g_dve, 7)
            pe_.wait_ge(state_ready, 2 * (N_CHUNK - 1))

            def scores(t):
                if t >= 2:
                    pe_.wait_ge(a_masked, t - 1)
                for hd in range(HEADS):
                    pair, hh = divmod(hd, 2)
                    rows = slice(hh * GK, (hh + 1) * GK)
                    mm = pe_.matmul(PS[:, 4 + 2 * (t % 2) + hh, pair * P:(pair + 1) * P], gk[rows, pair, t * P:(t + 1) * P],
                                    gq[rows, pair, t * P:(t + 1) * P], start=True, stop=True)
                mm.then_inc(a_ready, 1)

            scores(0)
            for t in range(NT):
                if t + 1 < NT:
                    scores(t + 1)
                if t == 4:
                    pe_.wait_ge(go_kept, HEADS)
                pe_.wait_ge(a_masked, t + 1)
                for hd in range(HEADS):
                    pair, hh = divmod(hd, 2)
                    rows = slice(hh * GK, (hh + 1) * GK)
                    col = (t % 4) * P
                    pe_.matmul(PS[:, hd, col:col + P], gv[:, t, hd * GV:(hd + 1) * GV], at_sb[:, t % 2, (2 * hh + pair) * P:(2 * hh + pair + 1) * P],
                               start=True, stop=True, skip_group_check=True)
                    for s in range(2):
                        n = 2 * t + s
                        if n > 0:
                            mm = pe_.matmul(PS[:, hd, col + s * CHUNK:col + (s + 1) * CHUNK], state[rows, n, pair, :],
                                            gq[rows, pair, n * CHUNK:(n + 1) * CHUNK], start=False, stop=True,
                                            skip_group_check=True)
                mm.then_inc(go_done, 1)

    OFF = [0, SEQ, SEQ + WINDOW + P]

    def factor(j):
        return HEADS + j

    def win_lo(i):
        return max(0, i - WT)

    def width(i, j):
        return (i + 1) * P if j < HEADS else (i + 1 - win_lo(i)) * P

    def key_tiles(i):
        return [(0, kt, kt * P) for kt in range(i + 1)] + \
               [(1, kt, (kt - win_lo(i)) * P) for kt in range(win_lo(i), i + 1)] + [(2, 0, 0)]

    first_tile = [sum(len(key_tiles(x)) for x in range(i)) for i in range(NT + 1)]

    def share(i, j):
        n = len(key_tiles(i))
        return range(n * j // 9, n * (j + 1) // 9)

    with nc.Block() as block:
        @block.sync
        def _(sp):
            for hd in range(HEADS):
                sp.dma_start(gog[:, hd, :], gog_spill[hd]).then_inc(gog_back, 16)
            sp.wait_ge(gog_back, 16 * HEADS)

        @block.scalar
        def _(act):
            for i in range(-1, NT):
                for j in range(9):
                    if i + 1 < NT:
                        it = 9 * (i + 1) + j
                        b, slot, par = j // HEADS, it % 2, (i + 1) % 2
                        act.wait_ge(max_done, it + 1)
                        if i + 1 >= 2 and j == 0:
                            act.wait_ge(pv_done, first_tile[i])
                        if b < 2:
                            w = width(i + 1, j)
                            act.activation(prob[:, par, j % HEADS, OFF[b]:OFF[b] + w],
                                           PS[:, 2 * slot:2 * slot + 2, :].rearrange("p a b -> p (a b)")[:, 0:w], ACT.Exp,
                                           bias=neg_max[:, par, factor(j):factor(j) + 1],
                                           accum_out=row_sum[:, par, factor(j):factor(j) + 1]).then_inc(exp_done, 1)
                        else:
                            for hd in range(HEADS):
                                ins = act.activation(prob[:, par, hd, OFF[2]:OFF[2] + CMPW],
                                                     PS[:, 2 * slot, hd * CMPW:(hd + 1) * CMPW], ACT.Exp,
                                                     bias=neg_max[:, par, hd:hd + 1],
                                                     accum_out=row_sum[:, par, hd:hd + 1])
                            ins.then_inc(exp_done, 1)
                    if i >= 0:
                        for m in share(i, j):
                            n = first_tile[i] + m
                            if n % 2 == 0:
                                rows = CMPW if key_tiles(i)[m][0] == 2 else P
                                act.wait_ge(pt_ready, n + 1)
                                if n >= 4:
                                    act.wait_ge(pv_done, n - 3)
                                act.activation(probT[0:rows, n % 4, :], PS[0:rows, 4 + n % 2, :], ACT.Copy).then_inc(pt_act, 1)
                if i >= 0:
                    act.wait_ge(pv_done, first_tile[i + 1])
                    act.activation(oT[:, 0:HEADS, i * P:(i + 1) * P],
                                   PS[:, 6 + i % 2, :].rearrange("p (h q) -> p h q", h=HEADS), ACT.Copy).then_inc(o_kept, 1)

        @block.vector
        def _(dve):
            for i in range(-1, NT):
                if i >= 0:
                    par = i % 2
                    dve.wait_ge(exp_done, 9 * (i + 1))
                    dve.reciprocal(inv_sum[:, par, :], row_sum[:, par, :]).then_inc(r_ready, 1)
                    dve.wait_ge(r_ready, i + 1)
                    dve.tensor_tensor(p_scale[:, par, :].rearrange("p (b h) -> p b h", b=3),
                                      inv_sum[:, par, :].rearrange("p (b h) -> p b h", b=3),
                                      gate[:, i, :].rearrange("p (h b) -> p b h", b=3),
                                      ALU.mult).then_inc(p_scaled, 1)
                    dve.wait_ge(p_scaled, 13 * i + 1)
                    for j in range(8):
                        b = j // HEADS
                        pr = prob[:, par, j % HEADS, OFF[b]:OFF[b] + width(i, j)]
                        dve.tensor_scalar(pr, pr, p_scale[:, par, factor(j):factor(j) + 1], None, ALU.mult).then_inc(p_scaled, 1)
                    for hd in range(HEADS):
                        pr = prob[:, par, hd, OFF[2]:OFF[2] + CMPW]
                        dve.scalar_tensor_tensor(pr, pr, p_scale[:, par, hd:hd + 1], cmp_valid[:, i, :],
                                                 ALU.mult, ALU.mult).then_inc(p_scaled, 1)
                for j in range(9):
                    if i + 1 < NT:
                        it = 9 * (i + 1) + j
                        slot, par = it % 2, (i + 1) % 2
                        dve.wait_ge(s_ready, it + 1)
                        if i + 1 >= 2 and j == 0:
                            dve.wait_ge(exp_done, 9 * i)
                        if j < 8:
                            w = width(i + 1, j)
                            dve.tensor_reduce(neg_max[:, par, factor(j):factor(j) + 1],
                                              PS[:, 2 * slot:2 * slot + 2, :].rearrange("p a b -> p (a b)")[:, 0:w],
                                              AX.X, ALU.max, negate=True).then_inc(max_done, 1)
                        else:
                            dve.tensor_reduce(neg_max[:, par, 0:HEADS],
                                              PS[:, 2 * slot, 0:HEADS * CMPW].rearrange("p (h n) -> p h n", h=HEADS),
                                              AX.X, ALU.max, negate=True).then_inc(max_done, 1)
                    if i >= 0:
                        for m in share(i, j):
                            n = first_tile[i] + m
                            if n % 2 == 1:
                                rows = CMPW if key_tiles(i)[m][0] == 2 else P
                                dve.wait_ge(pt_ready, n + 1)
                                if n >= 4:
                                    dve.wait_ge(pv_done, n - 3)
                                dve.tensor_copy(probT[0:rows, n % 4, :], PS[0:rows, 4 + n % 2, :]).then_inc(pt_dve, 1)

        @block.tensor
        def _(pe_):
            def scores(i, j):
                it = 9 * i + j
                slot = it % 2
                if it >= 2:
                    pe_.wait_ge(exp_done, it - 1)
                if j < 8:
                    hd, keys, lo = (j, ksT, 0) if j < HEADS else (j - HEADS, kwT, win_lo(i) * P)
                    w = width(i, j)
                    wide = PS[:, 2 * slot:2 * slot + 2, :].rearrange("p a b -> p (a b)")
                    for c0 in range(0, w, HALF):
                        c1 = min(w, c0 + HALF)
                        masks = [(m, at0) for m, at0, on in ((neg_past, 0, j >= HEADS and i >= WT), (neg_future, w - P, True))
                                 if on and c0 <= at0 < c1]
                        mm = pe_.matmul(wide[:, c0:c1], qT[:, hd, i * P:(i + 1) * P], keys[:, lo + c0:lo + c1],
                                        start=True, stop=True)
                        for m, at0 in masks:
                            mm = pe_.matmul(wide[:, at0:at0 + P], identb[:, :], m[:, :], start=False, stop=True,
                                            skip_group_check=True)
                else:
                    for hd in range(HEADS):
                        pe_.matmul(PS[:, 2 * slot, hd * CMPW:(hd + 1) * CMPW], qT[:, hd, i * P:(i + 1) * P], kcT[:, :],
                                   start=(hd == 0), stop=True, skip_group_check=True)
                    mm = pe_.matmul(PS[:, 2 * slot, 0:HEADS * CMPW].rearrange("p (h n) -> p h n", h=HEADS), identb[:, :],
                                    neg_cmp[:, i, :].unsqueeze(1).to_broadcast([P, HEADS, CMPW]), start=False, stop=True,
                                    skip_group_check=True)
                mm.then_inc(s_ready, 1)

            def turn(i, m):
                b, kt, at0 = key_tiles(i)[m]
                n = first_tile[i] + m
                rows = CMPW if b == 2 else P
                pe_.wait_ge(p_scaled, 13 * i + (5, 9, 13)[b])
                if n >= 2:
                    pe_.wait_ge((pt_act, pt_dve)[n % 2], (n - 2) // 2 + 1)
                for hd in range(HEADS):
                    mm = pe_.transpose(PS[0:rows, 4 + n % 2, hd * P:(hd + 1) * P],
                                       prob[:, i % 2, hd, OFF[b] + at0:OFF[b] + at0 + rows], ident[:, :])
                mm.then_inc(pt_ready, 1)

            def values(i, m):
                b, kt, at0 = key_tiles(i)[m]
                n, last = first_tile[i] + m, m == len(key_tiles(i)) - 1
                rows = CMPW if b == 2 else P
                v = (vtok[:, kt, 0:P], vtok[:, kt, P:2 * P], vc[:, :])[b]
                pe_.wait_ge((pt_act, pt_dve)[n % 2], n // 2 + 1)
                if m == 0 and i >= 2:
                    pe_.wait_ge(o_kept, i - 1)
                mm = pe_.matmul(PS[:, 6 + i % 2, :], v, probT[0:rows, n % 4, :], start=(m == 0), stop=last)
                mm.then_inc(pv_done, 1)

            waiting = []
            for i in range(-1, NT):
                for j in range(9):
                    if i + 1 < NT:
                        scores(i + 1, j)
                    if i >= 0:
                        for m in share(i, j):
                            turn(i, m)
                            waiting.append((i, m))
                            if len(waiting) > 1:
                                values(*waiting.pop(0))
                if i >= 0:
                    values(*waiting.pop(0))

    groups = [(h, kind) for h in range(2) for kind in range(2)]

    def scaled_first(x):
        return 6 * (x // 8 * 2) + (x % 8 + 1 if x % 8 < 4 else 4 + 2 * (x % 4) + 1)

    def scaled_at(x):
        return scaled_first(x) + (x // 4) % 2

    with nc.Block() as block:
        @block.scalar
        def _(act):
            def squares(g):
                h, kind = groups[g]
                for hd in range(HEADS):
                    x = 4 * g + hd
                    if x >= 2:
                        act.wait_ge(hsq_used, x - 1)
                    act.activation(h_sq[:, x % 2, :], half(oT, 4 * kind + hd, h), ACT.Square).then_inc(hsq_ready, 1)
                act.wait_ge(hsq_used, 4 * (g + 1))
                if g >= 2:
                    act.wait_ge(hrstd_ready, g - 1)
                act.activation(rms[:, g % 2, :], PS[:, 6 + g % 2, 0:16], ACT.Sqrt, scale=1.0 / DH, bias=eps[:, 0:1])\
                   .then_inc(hrms_ready, 1)

            squares(0)
            for g, (h, kind) in enumerate(groups):
                if g + 1 < len(groups):
                    squares(g + 1)
                for hd in range(HEADS):
                    x = 4 * g + hd
                    act.wait_ge(hn_scaled, scaled_at(x))
                    act.activation(half(u_hi, 4 * kind + hd, h), half(oT, 4 * kind + hd, h), ACT.Copy).then_inc(mhi_ready, 1)

        @block.tensor
        def _(pe_):
            for g in range(len(groups)):
                for hd in range(HEADS):
                    x = 4 * g + hd
                    pe_.wait_ge(hsq_ready, x + 1)
                    if hd == 0 and g >= 2:
                        pe_.wait_ge(hrms_ready, g - 1)
                    for t in range(4):
                        mm = pe_.matmul(PS[:, 6 + g % 2, 4 * hd + t:4 * hd + t + 1], h_sq[:, x % 2, t * P:(t + 1) * P],
                                        ones[:, 0:1], start=(hd == 0 and t == 0), stop=True, skip_group_check=True)
                    mm.then_inc(hsq_used, 1)
                for hd in range(HEADS):
                    x = 4 * g + hd
                    pe_.wait_ge(hdiag_ready, x + 1)
                    if x >= 6:
                        pe_.wait_ge(hn_scaled, scaled_first(x - 6))
                    pe_.matmul(PS[:, x % 6, :], ones[:, :], h_diag[:, x % 2, :], start=True, stop=True).then_inc(hrb_ready, 1)

        @block.vector
        def _(dve):
            for g, (h, kind) in enumerate(groups):
                dve.wait_ge(hrms_ready, g + 1)
                dve.reciprocal(rstd[:, g % 2, :], rms[:, g % 2, :]).then_inc(hrstd_ready, 1)
                dve.wait_ge(hrstd_ready, g + 1)

                def diag(hd):
                    x = 4 * g + hd
                    if x >= 2:
                        dve.wait_ge(hrb_ready, x - 1)
                    dve.tensor_tensor(h_diag[:, x % 2, :].rearrange("p (t q) -> p t q", t=4),
                                      ident[:, :].unsqueeze(1).to_broadcast([P, 4, P]),
                                      rstd[:, g % 2, 4 * hd:4 * hd + 4].unsqueeze(2).to_broadcast([P, 4, P]),
                                      ALU.mult).then_inc(hdiag_ready, 1)

                def scale(hd):
                    x = 4 * g + hd
                    o = half(oT, 4 * kind + hd, h)
                    gn = VEC_AT[("nsa_out_g", "gla_out_g")[kind]] + hd
                    dve.wait_ge(hrb_ready, x + 1)
                    dve.scalar_tensor_tensor(o, o, vec[:, gn:gn + 1], PS[:, x % 6, :], ALU.mult, ALU.mult).then_inc(hn_scaled, 1)
                    if kind == 1:
                        dve.wait_ge(hn_scaled, scaled_first(x))
                        dve.tensor_tensor(o, o, half(gog, hd, h), ALU.mult).then_inc(hn_scaled, 1)

                def rest(hd):
                    x = 4 * g + hd
                    ch = 4 * kind + hd
                    dve.wait_ge(mhi_ready, x + 1)
                    dve.tensor_tensor(half(u_lo, ch, h), half(oT, ch, h), half(u_hi, ch, h).bitcast(F32), ALU.subtract)\
                       .then_inc(mlo_ready, 1)

                diag(0)
                diag(1)
                for hd in range(HEADS):
                    scale(hd)
                    if hd + 2 < HEADS:
                        diag(hd + 2)
                    if hd > 0:
                        rest(hd - 1)
                rest(HEADS - 1)

    with nc.Block() as block:
        @block.sync
        def _(sp):
            for c in range(KC):
                sp.dma_start(xT[:, c, :], x_spill[c]).then_inc(x_back, 16)
            for u in range(U_OUT + AHEAD + RAWS, U_FFN[1] + 6):
                sp_load(sp, u)
            with sp.Fori(1, ITERS) as t:
                sp_ffn(sp, 1, t, 0)
            p_src = A["p"][0, 0].rearrange("(t p) d -> t p d", p=P)
            for u in range(U_PLE, U_PLE + AHEAD + 2):
                sp_load(sp, u)
            for t in range(NT):
                if t >= 2:
                    sp.wait_ge(p_turned, t - 1)
                sp.dma_start(p_in[:, t % 2, :], p_src[t]).then_inc(p_loaded[t % 2], 16)
            for u in range(U_PLE + AHEAD + 2, U_END):
                sp_load(sp, u)
            for t in range(NT):
                sp.wait_ge(y_act, t + 1)
                sp.wait_ge(y_dve, t + 1)
                sp.dma_start(out[0, t * P:(t + 1) * P, :], w_raw[:, t % RAWS, :]).then_inc(y_stored[t % RAWS], 16)
            for i in range(RAWS):
                sp.wait_ge(y_stored[i], 16 * len(range(i, NT, RAWS)))

        @block.scalar
        def _(act):
            for s in range(4):
                for i in range(2):
                    u = U_OUT + 2 * s + i + AHEAD
                    act_round(act, u, u, (v_ready, V_END) if s == 0 else (f_ready, R_OUT + 4 * s))
            for k in (6, 7):
                act_norm(act, k, fT, lambda h, c: (f_kept, R_OUT + 4 * (c // 2) + 2 * h + c % 2 + 1))
            for k in (8, 9):
                act_norm(act, k, xT, x_done(1))
            for h in range(2):
                act_hi(act, 2, h, fT, u32_done(2))
            act_ffn(act, 1, 0, True)
            with act.Fori(1, ITERS) as t:
                act_ffn(act, 1, t, False)
            for j in range(4):
                act.wait_ge(p_turned, 2 * j + 2)
                act.wait_ge(f_ready, R_E)
                act.activation(h_hi[:, :, 2 * j * P:(2 * j + 2) * P], PS[:, j, :].rearrange("p (t c q) -> p c t q", t=2, c=2),
                               ACT.Copy).then_inc(p_hi, 1)
            for k in (10, 11):
                act_norm(act, k, fT, f_done(1))
            for h in range(2):
                act_hi(act, 3, h, xT, x_done(2))
            for s in range(4):
                if s < 3:
                    for i in range(2):
                        u = U_PLE + 2 * s + i + AHEAD
                        act_round(act, u, u, (f_ready, R_E if s == 0 else R_E + 16 + 4 * (s - 1)))
                for x in range(4 * s, 4 * s + 4):
                    act.wait_ge(f_ready, R_G + x + 1)
                    if x >= 2:
                        act.wait_ge(t_ready, x - 1)
                    act.activation(sg[:, x % 2, :], PS[:, 4 + x % 4, :], ACT.Sigmoid).then_inc(sig_done, 1)
            for k in (12, 13):
                act_norm(act, k, fT, lambda h, c: (t_ready, 16))
            for t in range(NT):
                act.wait_ge(y_turned, 2 * t + 1)
                if t >= RAWS:
                    act.wait_ge(y_stored[t % RAWS], 16 * (t // RAWS))
                act.activation(w_raw[:, t % RAWS, 0:HALF], PS[:, (2 * t) % 8, :], ACT.Copy).then_inc(y_act, 1)

        @block.vector
        def _(dve):
            for s in range(4):
                for i in range(2):
                    u = U_OUT + 2 * s + i + AHEAD
                    dve_rest(dve, u, u)
                for h in range(2):
                    for i in range(2):
                        r = R_OUT + 4 * s + 2 * h + i
                        dve.wait_ge(f_ready, r + 1)
                        dve.tensor_copy(half(fT, 2 * s + i, h), PS[:, 4 + r % 4, :]).then_inc(f_kept, 1)
            dve.wait_ge(x_back, 16 * KC)
            for k in (6, 7):
                dve_norm(dve, k)
                dve_residual(dve, 1, k, "mix_post_g")
            for k in (8, 9):
                dve_norm(dve, k)
                dve_apply(dve, 2, k, "ffn2_pre_g")
            dve_ffn(dve, 1, 0, True)
            with dve.Fori(1, ITERS) as t:
                dve_ffn(dve, 1, t, False)
            for j in range(4):
                dve.wait_ge(p_hi, j + 1)
                dst = [x[:, :, 2 * j * P:(2 * j + 2) * P].rearrange("p c (t q) -> p c t q", t=2) for x in (h_lo, h_hi)]
                dve.tensor_tensor(dst[0], PS[:, j, :].rearrange("p (t c q) -> p c t q", t=2, c=2), dst[1].bitcast(F32),
                                  ALU.subtract).then_inc(p_lo, 1)
            for k in (10, 11):
                dve_norm(dve, k)
                dve_residual(dve, 2, k, "ffn2_post_g")
            for h in range(2):
                for c in range(KC):
                    dve_lo(dve, 3, h, c, xT)
            for x in range(16):
                m, h = x // 2, x % 2
                dve.wait_ge(f_ready, R_E + x + 1)
                if x == 0:
                    dve.wait_ge(x_ready, 48)
                dve.tensor_copy(half(fT, m, h), PS[:, 4 + x % 4, :]).then_inc(f_kept, 1)
            for s in range(4):
                if s < 3:
                    for i in range(2):
                        u = U_PLE + 2 * s + i + AHEAD
                        dve_rest(dve, u, u)
                for x in range(4 * s, 4 * s + 4):
                    m, h = 2 * s + x % 2, (x % 4) // 2
                    dve.wait_ge(sig_done, x + 1)
                    if x == 0:
                        dve.wait_ge(f_kept, R_G)
                    dve.tensor_tensor(half(fT, m, h), half(fT, m, h), sg[:, x % 2, :], ALU.mult).then_inc(t_ready, 1)
            for k in (12, 13):
                dve_norm(dve, k)
                dve_residual(dve, 3, k, "ple_post_g")
            for t in range(NT):
                dve.wait_ge(y_turned, 2 * t + 2)
                if t >= RAWS:
                    dve.wait_ge(y_stored[t % RAWS], 16 * (t // RAWS))
                dve.tensor_copy(w_raw[:, t % RAWS, HALF:SEQ], PS[:, (2 * t + 1) % 8, :]).then_inc(y_dve, 1)

        @block.tensor
        def _(pe_):
            def tile(u, r, h, after=None):
                pe_.wait_ge(lo_ready, u + 1)
                if after is not None:
                    pe_.wait_ge(*after)
                for k in range(KC):
                    w = [x[:, u % SLOTS, k * P:(k + 1) * P] for x in (w_hi, w_lo)]
                    for s, (a, b) in enumerate(passes(w, [half(x, k, h) for x in (u_hi, u_lo)])):
                        mm = pe_.matmul(PS[:, 4 + r % 4, :], a, b, start=(k == 0 and s == 0), stop=(k == KC - 1 and s == 2))
                mm.then_inc(f_ready, 1)

            for s in range(4):
                for h in range(2):
                    for i in range(2):
                        r = R_OUT + 4 * s + 2 * h + i
                        tile(U_OUT + 2 * s + i, r, h, (f_kept, r - 3))
            for k in (6, 7, 8, 9):
                pe_norm(pe_, k)
            pe_ffn(pe_, 1, 0, True)
            with pe_.Fori(1, ITERS) as t:
                pe_ffn(pe_, 1, t, False)
            pe_.wait_ge(h_done, Q0[1] + 4 * ITERS)
            for t in range(NT):
                pe_.wait_ge(p_loaded[t % 2], 16 * (t // 2 + 1))
                for c in range(2):
                    mm = pe_.transpose(PS[:, t // 2, ((t % 2) * 2 + c) * P:((t % 2) * 2 + c + 1) * P], p_in[:, t % 2, c * P:(c + 1) * P], ident[:, :])
                mm.then_inc(p_turned, 1)
            pe_.wait_ge(p_lo, 4)
            for k in (10, 11):
                pe_norm(pe_, k)
            for x in range(16):
                m, h = x // 2, x % 2
                r = R_E + x
                pe_.wait_ge(lo_ready, U_PLE + 2)
                pe_.wait_ge(f_kept, r - 3)
                for c in range(2):
                    w = [y[:, (U_PLE + c) % SLOTS, m * P:(m + 1) * P] for y in (w_hi, w_lo)]
                    for s, (a, b) in enumerate(passes(w, [half(y, c, h) for y in (h_hi, h_lo)])):
                        mm = pe_.matmul(PS[:, 4 + r % 4, :], a, b, start=(c == 0 and s == 0), stop=(c == 1 and s == 2))
                mm.then_inc(f_ready, 1)
            for x in range(16):
                s, h, i = x // 4, (x % 4) // 2, x % 2
                if x < 2:
                    pe_.wait_ge(ulo_ready, 16 * 3 + 16)
                tile(U_PLE + 2 + 2 * s + i, R_G + x, h, (f_kept, R_G + x - 3) if x < 4 else (sig_done, x - 3))
            for k in (12, 13):
                pe_norm(pe_, k)
            for t in range(NT):
                for b in range(2):
                    n = 2 * t + b
                    pe_.wait_ge(x_ready, 48 + (16 if t >= 4 else 8))
                    if n >= 8:
                        pe_.wait_ge((y_act, y_dve)[b], (n - 8) // 2 + 1)
                    elif b == 0 and t < 2:
                        pe_.wait_ge(x_ready, 64)
                    for c in range(4):
                        mm = pe_.transpose(PS[:, n % 8, c * P:(c + 1) * P], xT[:, 4 * b + c, t * P:(t + 1) * P], ident[:, :])
                    mm.then_inc(y_turned, 1)


_INS = ["x", "p", "ffn1_pre_g", "ffn1_post_g", "ffn1_w_gate", "ffn1_w_up", "ffn1_w_down", "mix_pre_g", "mix_post_g",
        "w_in", "cmp_k_pe", "cmp_k_w1", "cmp_k_w2", "cmp_v_pe", "cmp_v_w1", "cmp_v_w2", "nsa_out_g", "gla_gate_up",
        "gla_gate_bias", "gla_out_g", "w_out", "ffn2_pre_g", "ffn2_post_g", "ffn2_w_gate", "ffn2_w_up", "ffn2_w_down",
        "ple_proj", "ple_gate", "ple_post_g"]


def kernel(**inputs):
    import numpy as _np
    import concourse.bacc as _bacc
    from concourse import mybir as _mybir
    from concourse.bass_utils import run_bass_kernel_spmd as _run

    nc = _bacc.Bacc("TRN2", target_bir_lowering=False, num_devices=1, dynamic_dma_scratch_size=1024)
    arrays, aps = {}, {}
    for name in _INS:
        a = _np.ascontiguousarray(inputs[name])
        arrays[f"in_{name}_dram"] = a
        aps[name] = nc.dram_tensor(f"in_{name}_dram", a.shape, _mybir.dt.from_np(a.dtype), kind="ExternalInput").ap()
    out = nc.dram_tensor("out_0_dram", (1, SEQ, D), _mybir.dt.float32, kind="ExternalOutput").ap()
    build(nc, aps, out)
    r = _run(nc, [arrays], core_ids=[0])
    return r.results[0]["out_0_dram"]
```

```python
import concourse.bass as bass
from concourse import mybir
from concourse.alu_op_type import AluOpType as ALU

ACT = mybir.ActivationFunctionType
AX = mybir.AxisListType
F32 = mybir.dt.float32
F32R = mybir.dt.float32r
BF16 = mybir.dt.bfloat16

P = 128
SEQ = 1024
D = 1024
KC = D // P
HALF = 512
NT = SEQ // P
F = 2816
ITERS = F // (2 * P)
EPS = 1e-6
NEG = -1e30

HEADS = 4
DH = 128
CMP_BLOCK, CMP_STRIDE = 32, 16
N_CMP = (SEQ - CMP_BLOCK) // CMP_STRIDE + 1
CMPW = 64
WINDOW = 512
WT = WINDOW // P
SLC_BLOCK, SLC_TOPK = 64, 16
assert SLC_TOPK >= SEQ // SLC_BLOCK

GK, GV, RANK, CHUNK = 64, 128, 16, 64
PAIRS = 2
N_CHUNK = SEQ // CHUNK
GATE_NORM = 16.0
PLE = 256

IN_NAMES = ["q", "kc", "vc", "ks", "vs", "kw", "vw", "gate", "gq", "gk", "gv", "gdown", "gog"]
IN_SPLITS = [512, 128, 128, 128, 128, 128, 128, 12, 256, 256, 512, 16, 512]
COL = {n: sum(IN_SPLITS[:i]) for i, n in enumerate(IN_NAMES)}
GATES = 3 * HEADS
SMALL = GATES + RANK
VT = 2 * P + SMALL

SLOTS, RAWS, AHEAD = 6, 3, 4
U_FFN = [0, 6 * ITERS + 22 + 8]
U_IN = 6 * ITERS
U_OUT = U_IN + 22
U_PLE = U_FFN[1] + 6 * ITERS
U_END = U_PLE + 2 + KC
assert all(u % SLOTS == 0 for u in U_FFN + [U_PLE])


def slot_of(u):
    return u % SLOTS if u < U_PLE + 2 else 2 + (u - U_PLE - 2) % (SLOTS - 2)


Q0 = [0, 4 * ITERS]
R0 = [0, 16 * ITERS + 16]
R_OUT = 16 * ITERS
R_G = R0[1] + 16 * ITERS

PAIR_ORDER = [(0, 0), (1, 0), (0, 1), (1, 1), (2, 0), (2, 1), (3, 0), (3, 1)]

IN_PAIRS = [(("q", 0), ("ks", 0)), (("q", 1), ("kw", 0)), (("q", 2), ("gk", 0)), (("q", 3), ("gk", 1)),
            (("gq", 0), ("kc", 0)), (("gq", 1), ("vc", 0)), (("gog", 0), ("gog", 1)), (("gog", 2), ("gog", 3))]
TOK_PAIRS = [(COL["vs"], COL["vw"]), (COL["gv"], COL["gv"] + P), (COL["gv"] + 2 * P, COL["gv"] + 3 * P)]
IN_ORDER = [(0, 0), (1, 0), (0, 1), (1, 1)] + [(p, h) for p in range(2, len(IN_PAIRS)) for h in range(2)]
V_TOK = 4 * len(IN_PAIRS)
V_END = V_TOK + NT * len(TOK_PAIRS)


def tile_owner(v):
    if v < V_TOK:
        (p, _), i = IN_ORDER[v // 2], v % 2
        return "act" if i == 0 or IN_PAIRS[p][0][0] == "gog" else "dve"
    return "act" if v % 2 == 0 else "dve"


def owner_rank(v):
    return sum(tile_owner(w) == tile_owner(v) for w in range(v + 1))


def v_bank(v):
    return (0, 2, 1, 3)[v] if v < 4 else v % 8


def passes(hi_lo_w, hi_lo_x):
    return ((hi_lo_w[0], hi_lo_x[0]), (hi_lo_w[0], hi_lo_x[1]), (hi_lo_w[1], hi_lo_x[0]))


VEC_ROWS = [("ffn1_pre_g", 8), ("ffn1_post_g", 8), ("mix_pre_g", 8), ("mix_post_g", 8), ("ffn2_pre_g", 8),
            ("ffn2_post_g", 8), ("ple_post_g", 8), ("nsa_out_g", 4), ("gla_out_g", 4), ("gla_gate_bias", 2)]
VEC_AT = {n: sum(c for _, c in VEC_ROWS[:i]) for i, (n, _) in enumerate(VEC_ROWS)}
NVEC = sum(c for _, c in VEC_ROWS)
HALVED = ("ffn1_post_g", "ffn2_post_g")


def build(nc, A, out):
    base = -(-nc.sbuf_base // 64) * 64

    def place(name, shape, dt, offset):
        return nc.alloc_sbuf_tensor_at(name, shape, dt, offset=offset)

    def size(shape, dt):
        n = 2 if dt == BF16 else 4
        for s in shape[1:]:
            n *= s
        return -(-n // 32) * 32

    class Region:

        def __init__(self, start, end):
            self.at, self.end = start, end

        def take(self, name, shape, dt=F32):
            t = place(name, shape, dt, self.at)
            self.at += size(shape, dt)
            assert self.at <= self.end, (name, self.at, self.end)
            return t

    const = Region(base, nc.sbuf_usable_end)
    ident = const.take("ident", [P, P])
    ones = const.take("ones", [P, P])
    identb = const.take("identb", [P, P], BF16)
    neg_future = const.take("neg_future", [P, P], BF16)
    neg_past = const.take("neg_past", [P, P], BF16)
    neg_cmp = const.take("neg_cmp", [P, NT, CMPW], BF16)
    cmp_valid = const.take("cmp_valid", [P, NT, CMPW])
    gla_causal = const.take("gla_causal", [P, P])
    vec_rows = const.take("vec_rows", [P, P])
    pe_rows = const.take("pe_rows", [2 * CMP_BLOCK, P])
    vec = const.take("vec", [P, NVEC])
    pe = const.take("pe", [P, 2 * CMP_BLOCK])
    rms = const.take("rms", [P, 2, 16])
    rstd = const.take("rstd", [P, 2, 16])
    zero = const.take("zero", [P, 1])
    eps = const.take("eps", [P, 1])
    w_raw = const.take("w_raw", [P, RAWS, KC * P])
    whi_at = const.at
    w_hi = const.take("w_hi", [P, SLOTS, KC * P], F32R)
    w_lo = const.take("w_lo", [P, SLOTS, KC * P], F32R)
    u_at = const.at
    u_hi = const.take("u_hi", [P, KC, SEQ], F32R)
    ulo_at = const.at
    u_lo = const.take("u_lo", [P, KC, SEQ], F32R)
    u_end = const.at
    stage_at, stage_end = const.at, nc.sbuf_usable_end

    ffn = Region(stage_at, stage_end)
    xT = ffn.take("xT", [P, KC, SEQ])
    fT = ffn.take("fT", [P, KC, SEQ])
    h_at = ffn.at
    h_hi = ffn.take("h_hi", [P, 2, SEQ], F32R)
    h_lo = ffn.take("h_lo", [P, 2, SEQ], F32R)
    sg = ffn.take("sg", [P, 2, HALF])
    h32 = ffn.take("h32", [P, 2, HALF])
    sq_sum = ffn.take("sq_sum", [P, HALF])
    u_first = place("u_first", [P, KC, HALF], F32, h_at)
    p_place = place("p_place", [P, KC, SEQ], F32, ulo_at)

    mix = Region(stage_at, stage_end)
    oT = mix.take("oT", [P, 2 * HEADS, SEQ])
    qT = mix.take("qT", [P, HEADS, SEQ])
    gq = mix.take("gq", [P, PAIRS, SEQ])
    gv_at = mix.at
    gv = mix.take("gv", [P, NT, HEADS * GV])
    ksT = mix.take("ksT", [P, SEQ])
    kwT = mix.take("kwT", [P, SEQ])
    vtok = mix.take("vtok", [P, NT, VT])
    kcT = mix.take("kcT", [P, CMPW])
    vc = mix.take("vc", [CMPW, P])
    gate = mix.take("gate", [P, NT, GATES])
    pre = Region(stage_at, stage_at + 4 * 2 * HEADS * SEQ)
    kcmp = pre.take("kcmp", [P, 2, SEQ])
    gk = pre.take("gk", [P, PAIRS, SEQ])
    gog_out = pre.take("gog_out", [P, 4, HALF])
    small_raw = pre.take("small_raw", [P, KC, SMALL])
    small_hi = pre.take("small_hi", [P, KC, SMALL], F32R)
    small_lo = pre.take("small_lo", [P, KC, SMALL], F32R)
    assert pre.at <= stage_at + 28 * 1024
    gla = Region(u_at, u_end)
    gx = gla.take("gx", [P, PAIRS, SEQ])
    gb = gla.take("gb", [P, PAIRS, SEQ])
    ge = gla.take("ge", [P, PAIRS, SEQ])
    kend = gla.take("kend", [P, NT, PAIRS * P])
    state = gla.take("state", [P, N_CHUNK, PAIRS, GV])
    at_sb = gla.take("at_sb", [P, 2, HEADS * P])
    scan_keep = gla.take("scan_keep", [P, SEQ])
    w1_late = gla.take("w1_late", [P, 2, 8, P])
    kv_a = place("kv_a", [P, 2, SEQ], F32, u_at + 8192 * 4)
    kv_b = place("kv_b", [P, 2, SEQ], F32, u_at + 8192 * 5)
    gla_small = Region(stage_at + 4 * HEADS * SEQ, stage_at + 8 * HEADS * SEQ)
    gdT = gla_small.take("gdT", [RANK, SEQ])
    gup = gla_small.take("gup", [RANK, PAIRS * P])
    decay = gla_small.take("decay", [P, PAIRS, N_CHUNK])
    hid = gla_small.take("hid", [P, 2, CMPW])
    w2 = gla_small.take("w2", [P, 2, P])
    assert gla_small.at <= stage_at + 24 * 1024
    w1_early = place("w1_early", [P, 2, 8, P], F32, stage_at + 24 * 1024)
    w1 = [w1_early[:, 0], w1_early[:, 1], w1_late[:, 0], w1_late[:, 1]]
    PW = SEQ + WINDOW + P + CMPW
    att = Region(u_at, u_end)
    prob = att.take("prob", [P, 2, HEADS, PW])
    probT = att.take("probT", [P, 4, HALF])
    gog = place("gog", [P, HEADS, SEQ], F32, gv_at)
    mx_at = stage_at + 4 * (2 * HEADS * SEQ + HEADS * SEQ)
    small = Region(mx_at, mx_at + 8192)
    neg_max = small.take("neg_max", [P, 2, 3 * HEADS])
    row_sum = small.take("row_sum", [P, 2, 3 * HEADS])
    inv_sum = small.take("inv_sum", [P, 2, 3 * HEADS])
    p_scale = small.take("p_scale", [P, 2, 3 * HEADS])
    h_diag = place("h_diag", [P, 2, HALF], F32, mx_at)
    h_sq = place("h_sq", [P, 2, HALF], F32, mx_at + 4096)

    PS = nc.alloc_psum_tensor("PS", [P, 8, HALF], F32)

    y_rows = place("y_rows", [P, NT, D], F32, whi_at)

    x_spill = nc.dram_tensor("x_spill", [KC, P, SEQ], F32).ap()
    gog_spill = nc.dram_tensor("gog_spill", [HEADS, P, SEQ], F32).ap()

    def sem(name):
        return nc.alloc_semaphore(name)

    raw_loaded = [sem(f"raw_loaded{i}") for i in range(RAWS)]
    hi_ready, lo_ready = sem("hi_ready"), sem("lo_ready")
    x_loaded = [sem(f"x_loaded{i}") for i in range(4)]
    vec_loaded, masks_made, vec_turned, vec_kept = sem("vec_loaded"), sem("masks_made"), sem("vec_turned"), sem("vec_kept")
    xt_turned, xt_act, xt_dve = sem("xt_turned"), sem("xt_act"), sem("xt_dve")
    sq_ready, sq_used, rms_ready, rstd_ready = sem("sq_ready"), sem("sq_used"), sem("rms_ready"), sem("rstd_ready")
    sq_pooled, sums_ready = sem("sq_pooled"), sem("sums_ready")
    rows_squared, const_ready = sem("rows_squared"), sem("const_ready")
    diag_ready, rb_ready = sem("diag_ready"), sem("rb_ready")
    f_scaled, x_ready = sem("f_scaled"), sem("x_ready")
    u32_ready, uhi_ready, ulo_ready = sem("u32_ready"), sem("uhi_ready"), sem("ulo_ready")
    gu_ready, silu_done, h_done, hhi_ready, hlo_ready = sem("gu_ready"), sem("silu_done"), sem("h_done"), sem("hhi_ready"), sem("hlo_ready")
    f_ready, f_kept = sem("f_ready"), sem("f_kept")
    x_spilled, x_back = sem("x_spilled"), sem("x_back")
    v_ready, v_act, v_dve = sem("v_ready"), sem("v_act"), sem("v_dve")
    small_loaded, small_hi_ready, small_lo_ready = sem("small_loaded"), sem("small_hi_ready"), sem("small_lo_ready")
    gog_spilled = [sem(f"gog_spilled{i}") for i in range(4)]
    gog_back = sem("gog_back")
    gup_loaded, gd_turned, gd_kept, gpre_ready, gx_ready = sem("gup_loaded"), sem("gd_turned"), sem("gd_kept"), sem("gpre_ready"), sem("gx_ready")
    g_act, g_dve = sem("g_act"), sem("g_dve")
    w2_loaded = sem("w2_loaded")
    w1_loaded = [sem(f"w1_loaded{i}") for i in range(4)]
    w1_used, kv_biased, hid_kept, cmp_ready, cmp_kept = sem("w1_used"), sem("kv_biased"), sem("hid_kept"), sem("cmp_ready"), sem("cmp_kept")
    kend_turned, kend_kept = sem("kend_turned"), sem("kend_kept")
    outer_ready, state_ready = sem("outer_ready"), sem("state_ready")
    a_ready, a_masked, go_done, go_kept = sem("a_ready"), sem("a_masked"), sem("go_done"), sem("go_kept")
    s_ready, max_done, exp_done, p_scaled, r_ready = sem("s_ready"), sem("max_done"), sem("exp_done"), sem("p_scaled"), sem("r_ready")
    pt_ready, pt_act, pt_dve = sem("pt_ready"), sem("pt_act"), sem("pt_dve")
    o_kept, pv_done = sem("o_kept"), sem("pv_done")
    hsq_ready, hsq_used, hrms_ready, hrstd_ready, hdiag_ready, hrb_ready = (
        sem("hsq_ready"), sem("hsq_used"), sem("hrms_ready"), sem("hrstd_ready"), sem("hdiag_ready"), sem("hrb_ready"))
    hn_scaled, mhi_ready, mlo_ready = sem("hn_scaled"), sem("mhi_ready"), sem("mlo_ready")
    p_loaded, p_turned, p_kept, p_hi, p_lo = sem("p_loaded"), sem("p_turned"), sem("p_kept"), sem("p_hi"), sem("p_lo")
    e_ready = sem("e_ready")
    sig_done, t_ready = sem("sig_done"), sem("t_ready")
    y_turned, y_act, y_dve = sem("y_turned"), sem("y_act"), sem("y_dve")
    y_stored = sem("y_stored")

    def half(t, c, h):
        return t[:, c, h * HALF:(h + 1) * HALF]

    w_gate = [A["ffn1_w_gate"], A["ffn2_w_gate"]]
    w_up = [A["ffn1_w_up"], A["ffn2_w_up"]]
    w_down = [A["ffn1_w_down"], A["ffn2_w_down"]]

    def load_columns(sp, raw, w, col):
        return sp.dma_start(w_raw[:, raw, :].rearrange("p (k f) -> p k f", k=KC),
                            w[0].rearrange("(k p) f -> p k f", p=P)[:, :, bass.ds(col, P)])

    def load_rows(sp, raw, w, row):
        return sp.dma_start(w_raw[:, raw, :], w[0][bass.ds(row, P), :])

    def sp_load(sp, u):
        if u >= RAWS:
            sp.wait_ge(lo_ready, u - RAWS + 1)
        raw = u % RAWS
        for n in range(2):
            if U_FFN[n] <= u < U_FFN[n] + 6 * ITERS:
                t, j = divmod(u - U_FFN[n], 6)
                if j < 4:
                    ins = load_columns(sp, raw, (w_gate, w_up)[j % 2][n], (2 * t + j // 2) * P)
                else:
                    ins = load_rows(sp, raw, w_down[n], (2 * t + j - 4) * P)
        if U_IN <= u < U_OUT:
            p, i = divmod(u - U_IN, 2)
            if p < len(IN_PAIRS):
                name, m = IN_PAIRS[p][i]
                col = COL[name] + m * P
            else:
                col = TOK_PAIRS[p - len(IN_PAIRS)][i]
            ins = load_columns(sp, raw, A["w_in"], col)
        if U_OUT <= u < U_FFN[1]:
            ins = load_columns(sp, raw, A["w_out"], (u - U_OUT) * P)
        if U_PLE <= u < U_PLE + 2:
            ins = load_rows(sp, raw, A["ple_proj"], (u - U_PLE) * P)
        if u >= U_PLE + 2:
            ins = load_columns(sp, raw, A["ple_gate"], (u - U_PLE - 2) * P)
        ins.then_inc(raw_loaded[raw], 16)

    def sp_ffn(sp, n, t, first):
        for j in range(first, 6):
            sp.wait_ge(lo_ready, t * 6 + (U_FFN[n] + j - RAWS + 1))
            if j < 4:
                ins = load_columns(sp, j % RAWS, (w_gate, w_up)[j % 2][n], t * (2 * P) + (j // 2) * P)
            else:
                ins = load_rows(sp, j % RAWS, w_down[n], t * (2 * P) + (j - 4) * P)
            ins.then_inc(raw_loaded[j % RAWS], 16)

    def act_round(act, u, free=None):
        if free is not None:
            act.wait_ge(*free)
        act.wait_ge(raw_loaded[u % RAWS], (u // RAWS + 1) * 16)
        act.activation(w_hi[:, slot_of(u), :], w_raw[:, u % RAWS, :], ACT.Copy).then_inc(hi_ready, 1)

    def dve_rest(dve, u, j=None):
        slot, raw = (slot_of(u), u % RAWS) if j is None else (j % SLOTS, j % RAWS)
        dve.wait_ge(hi_ready, u + 1)
        dve.tensor_tensor(w_lo[:, slot, :], w_raw[:, raw, :], w_hi[:, slot, :].bitcast(F32),
                          ALU.subtract).then_inc(lo_ready, 1)

    SUM_BANK = [None, None, 0, 1, 0, 5, 0, 1, 0, 5, 0, 1, 0, 1]
    ROW_BANK = [3, 6, 2, 4, 3, 6, 2, 4, 3, 6, 2, 3, 0, 1]

    def squares(k, i):
        return sg[:, i % 2, :] if k < 12 else w_raw[:, 0, (i % 2) * HALF:(i % 2 + 1) * HALF]

    SQUARES = [(k, c) for k in range(2, 14) for c in range(KC)]

    def adds(k):
        return (k - 2) * (KC - 1)

    def square_used(i):
        k, c = SQUARES[i]
        return adds(k) + max(1, c)

    def act_square(act, k, c, src, ready):
        i = SQUARES.index((k, c))
        act.wait_ge(*ready(k % 2, c))
        if i >= 2:
            act.wait_ge(sq_pooled, square_used(i - 2))
        act.activation(squares(k, i), half(src, c, k % 2), ACT.Square).then_inc(sq_ready, 1)

    def act_sqrt(act, k):
        act.wait_ge(sums_ready, k - 1)
        act.wait_ge(rstd_ready, k - 1)
        act.activation(rms[:, k % 2, 0:4], PS[:, SUM_BANK[k], 0:4], ACT.Sqrt, scale=1.0 / D, bias=eps[:, 0:1])\
           .then_inc(rms_ready, 1)

    def act_norm(act, k, src, ready):
        for c in range(KC):
            act_square(act, k, c, src, ready)
        act_sqrt(act, k)

    def pool_norm(pool, k):
        for c in range(1, KC):
            i = SQUARES.index((k, c))
            pool.wait_ge(sq_ready, i + 1)
            if c == 1:
                if k > 2:
                    pool.wait_ge(sums_ready, k - 2)
                pool.tensor_tensor(sq_sum[:, :], squares(k, i - 1), squares(k, i), ALU.add).then_inc(sq_pooled, 1)
            else:
                pool.wait_ge(sq_pooled, adds(k) + c - 1)
                pool.tensor_tensor(sq_sum[:, :], sq_sum[:, :], squares(k, i), ALU.add).then_inc(sq_pooled, 1)

    def pe_sum_up(pe_, k):
        pe_.wait_ge(sq_pooled, adds(k + 1))
        for t in range(4):
            mm = pe_.matmul(PS[:, SUM_BANK[k], t:t + 1], sq_sum[:, t * P:(t + 1) * P], ones[:, 0:1],
                            start=(t == 0), stop=True, skip_group_check=True)
        mm.then_inc(sums_ready, 1)

    def pe_row(pe_, k):
        pe_.wait_ge(diag_ready, k + 1)
        pe_.matmul(PS[:, ROW_BANK[k], :], ones[:, :], h32[:, k % 2, :], start=True, stop=True).then_inc(rb_ready, 1)

    def pe_between(pe_, k):
        pe_sum_up(pe_, k + 1)
        pe_row(pe_, k + 1)
        pe_sum_up(pe_, k + 2)
        pe_row(pe_, k + 2)

    def dve_norm(dve, k):
        dve.wait_ge(rms_ready, k + 1)
        dve.reciprocal(rstd[:, k % 2, 0:4], rms[:, k % 2, 0:4]).then_inc(rstd_ready, 1)
        dve.wait_ge(rstd_ready, k + 1)
        dve.tensor_tensor(h32[:, k % 2, :].rearrange("p (t q) -> p t q", t=4),
                          ident[:, :].unsqueeze(1).to_broadcast([P, 4, P]),
                          rstd[:, k % 2, 0:4].unsqueeze(2).to_broadcast([P, 4, P]), ALU.mult).then_inc(diag_ready, 1)

    def dve_residual(dve, pi, k, gain, before=None, rest=None, steps=range(KC + 2)):
        h = k % 2
        for c in steps:
            if before is not None:
                before(c)
            if c == 0:
                dve.wait_ge(rb_ready, k + 1)
            if c < KC:
                g = vec[:, VEC_AT[gain] + c:VEC_AT[gain] + c + 1]
                dve.scalar_tensor_tensor(half(fT, c, h), half(fT, c, h), g, PS[:, ROW_BANK[k], :], ALU.mult, ALU.mult)\
                   .then_inc(f_scaled, 1)
            if 1 <= c <= KC:
                dve.wait_ge(f_scaled, 16 * pi + 8 * h + c)
                dve.tensor_tensor(half(xT, c - 1, h), half(xT, c - 1, h), half(fT, c - 1, h), ALU.add).then_inc(x_ready, 1)
            if rest is not None and c >= 2:
                rest(c - 2)

    def dve_apply(dve, a, k, gain, dst=None):
        h = k % 2
        if dst is None:
            dst = lambda c: half(fT, c, h)
        dve.wait_ge(rb_ready, k + 1)
        for c in range(KC + 1):
            if c < KC:
                g = vec[:, VEC_AT[gain] + c:VEC_AT[gain] + c + 1]
                if a > 0:
                    dve.wait_ge(x_ready, 16 * (a - 1) + 8 * h + c + 1)
                dve.scalar_tensor_tensor(dst(c), half(xT, c, h), g, PS[:, ROW_BANK[k], :], ALU.mult, ALU.mult)\
                   .then_inc(u32_ready, 1)
            if c > 0:
                dve_lo(dve, a, h, c - 1, dst(c - 1))

    def dve_lo(dve, a, h, c, src):
        dve.wait_ge(uhi_ready, 16 * a + 8 * h + c + 1)
        dve.tensor_tensor(half(u_lo, c, h), src, half(u_hi, c, h).bitcast(F32), ALU.subtract).then_inc(ulo_ready, 1)

    def act_hi(act, h, c, src, ready):
        act.wait_ge(*ready)
        act.activation(half(u_hi, c, h), src, ACT.Copy).then_inc(uhi_ready, 1)

    def act_hi_half(act, h, src, ready):
        for c in range(KC):
            act_hi(act, h, c, half(src, c, h), ready(h, c))

    def pe_gate_up(pe_, n, t, h, c, first, after_step=None):
        q = 2 * h + c
        if not (first and n == 0 and q < 2):
            pe_.wait_ge(h_done, t * 4 + (Q0[n] + q - 1))
        if h == 0:
            pe_.wait_ge(lo_ready, t * 6 + (U_FFN[n] + 2 * c + 2))
        order = [(k, i) for k in range(KC) for i in range(2)] if first else [(k, i) for i in range(2) for k in range(KC)]
        for k, i in order:
            if first and c == 0 and i == 0:
                pe_.wait_ge(ulo_ready, 16 * 2 * n + 8 * h + k + 1)
            w = [x[:, 2 * c + i, k * P:(k + 1) * P] for x in (w_hi, w_lo)]
            for s, (a, b) in enumerate(passes(w, [half(x, k, h) for x in (u_hi, u_lo)])):
                mm = pe_.matmul(PS[:, 2 * i + c, :], a, b, start=(k == 0 and s == 0), stop=(k == KC - 1 and s == 2))
            if k == KC - 1:
                mm.then_inc(gu_ready, 1)
            if after_step is not None and i == 1:
                after_step(k)

    def pe_down(pe_, n, t, first, after_tile=None):
        pe_.wait_ge(lo_ready, t * 6 + (U_FFN[n] + 6))
        for h in range(2):
            pe_.wait_ge(hlo_ready, t * 4 + (Q0[n] + 2 * h + 2))
            for m in range(KC):
                r = 8 * h + m
                if not (first and n == 0 and r < 4):
                    pe_.wait_ge(f_kept, t * 16 + (R0[n] + r - 3))
                for c in range(2):
                    w = [x[:, 4 + c, m * P:(m + 1) * P] for x in (w_hi, w_lo)]
                    for s, (a, b) in enumerate(passes(w, [half(x, c, h) for x in (h_hi, h_lo)])):
                        mm = pe_.matmul(PS[:, 4 + r % 4, :], a, b, start=(c == 0 and s == 0), stop=(c == 1 and s == 2))
                mm.then_inc(f_ready, 1)
                if after_tile is not None:
                    after_tile(r)

    def pe_ffn(pe_, n, t, first, after_second=None, after_tile=None):
        for h in range(2):
            for c in range(2):
                pe_gate_up(pe_, n, t, h, c, first, after_second if (h, c) == (0, 1) else None)
        pe_down(pe_, n, t, first, after_tile)

    def act_silu(act, n, t, q, first):
        act.wait_ge(gu_ready, t * 8 + (2 * (Q0[n] + q) + 1))
        if not (first and n == 0 and q < 2):
            act.wait_ge(h_done, t * 4 + (Q0[n] + q - 1))
        act.activation(sg[:, q % 2, :], PS[:, q % 2, :], ACT.Silu).then_inc(silu_done, 1)

    def act_ffn(act, n, t, first):
        for c in range(3):
            free = [(f_ready, t * 16 + R0[n]), (gu_ready, t * 8 + (2 * Q0[n] + 6)), (gu_ready, t * 8 + (2 * Q0[n] + 8))][c]
            if first and n == 0 and c == 0:
                free = None
            for i in range(2):
                j = 2 * c + i + AHEAD
                landed = t * 32 + ((U_FFN[n] + j) // RAWS + 1) * 16
                if free is not None:
                    act.wait_ge(*free)
                act.wait_ge(raw_loaded[j % RAWS], landed)
                act.activation(w_hi[:, j % SLOTS, :], w_raw[:, j % RAWS, :], ACT.Copy).then_inc(hi_ready, 1)
            for q in ((0, 1, 2), (3,), ())[c]:
                if not (first and q == 0):
                    act_silu(act, n, t, q, first)

    def dve_h(dve, n, t, q, first):
        h, c = divmod(q, 2)
        dve.wait_ge(silu_done, t * 4 + (Q0[n] + q + 1))
        dve.wait_ge(gu_ready, t * 8 + (2 * (Q0[n] + q) + 2))
        if not (first and n == 0 and q < 2):
            dve.wait_ge(hlo_ready, t * 4 + (Q0[n] + q - 1))
        dve.tensor_tensor(h32[:, c, :], sg[:, c, :], PS[:, 2 + c, :], ALU.mult).then_inc(h_done, 1)
        dve.wait_ge(h_done, t * 4 + (Q0[n] + q + 1))
        if not (first and n == 0):
            dve.wait_ge(f_ready, t * 16 + (R0[n] - 16 + 8 * (h + 1)))
        dve.tensor_copy(half(h_hi, c, h), h32[:, c, :]).then_inc(hhi_ready, 1)
        dve.wait_ge(hhi_ready, t * 4 + (Q0[n] + q + 1))
        dve.tensor_tensor(half(h_lo, c, h), h32[:, c, :], half(h_hi, c, h).bitcast(F32), ALU.subtract)\
           .then_inc(hlo_ready, 1)

    def dve_keep(dve, n, t, r, first):
        m, h = r % 8, r // 8
        dve.wait_ge(f_ready, t * 16 + (R0[n] + r + 1))
        if first:
            dve.tensor_copy(half(fT, m, h), PS[:, 4 + r % 4, :]).then_inc(f_kept, 1)
        else:
            dve.wait_ge(f_kept, t * 16 + (R0[n] + r - 15))
            dve.tensor_tensor(half(fT, m, h), half(fT, m, h), PS[:, 4 + r % 4, :], ALU.add).then_inc(f_kept, 1)

    def dve_ffn(dve, n, t, first, tiles=16):
        for c in range(3):
            for i in range(2):
                j = 2 * c + i + AHEAD
                dve_rest(dve, t * 6 + (U_FFN[n] + j), j)
            for q in ((0, 1, 2), (3,), ())[c]:
                if not (first and q == 0):
                    dve_h(dve, n, t, q, first)
        for r in range(tiles):
            dve_keep(dve, n, t, r, first)

    LAST = ITERS - 1

    def pe_early(pe_, k, r):
        if r == 11:
            pe_sum_up(pe_, k)
        if r == 13:
            pe_row(pe_, k)

    def act_cross(act, k, pi, f_at, between=None):
        act_norm(act, k, fT, f_at)
        act_norm(act, k + 1, fT, f_at)
        act_norm(act, k + 2, xT, x_done(pi))
        act_hi_half(act, 0, fT, u32_done(pi + 1))
        act_norm(act, k + 3, xT, x_done(pi))
        if between is not None:
            between()
        act_hi_half(act, 1, fT, u32_done(pi + 1))

    def dve_cross(dve, k, pi, post, nxt, before, between=None):
        def first_half(c):
            before(c)
            if c == 7:
                dve_norm(dve, k + 1)

        dve_residual(dve, pi, k, post, first_half)
        dve_residual(dve, pi, k + 1, post, steps=range(3))
        dve_norm(dve, k + 2)
        dve_apply(dve, pi + 1, k + 2, nxt)
        dve_residual(dve, pi, k + 1, post, steps=range(3, KC + 1))
        dve_norm(dve, k + 3)
        if between is not None:
            between()
        dve_apply(dve, pi + 1, k + 3, nxt)

    def dve_ffn_last(dve, n, k):
        dve_ffn(dve, n, LAST, False, tiles=12)
        dve_norm(dve, k)
        dve_keep(dve, n, LAST, 12, False)
        dve_keep(dve, n, LAST, 13, False)

    def f_done(n):
        return lambda h, c: (f_kept, R0[n] + 16 * (ITERS - 1) + 8 * h + c + 1)

    def x_done(pi):
        return lambda h, c: (x_ready, 16 * pi + 8 * h + c + 1)

    def u32_done(a):
        return lambda h, c: (u32_ready, 16 * a + 8 * h + c + 1)

    def fm_target(name, m, h):
        if name == "q":
            return half(qT, m, h), float(DH) ** -0.5
        if name == "gq":
            return half(gq, m, h), float(GK) ** -0.5
        if name == "ks":
            return ksT[:, h * HALF:(h + 1) * HALF], 1.0
        if name == "kw":
            return kwT[:, h * HALF:(h + 1) * HALF], 1.0
        if name == "gk":
            return half(gk, m, h), 1.0
        return half(kcmp, "kc vc".split().index(name), h), 1.0

    def in_free(p):
        if p == 0:
            return f_ready, R_OUT
        if p == 1:
            return v_ready, 2 * (IN_ORDER.index((0, 1)) + 1)
        return v_ready, 4 * p if p <= len(IN_PAIRS) else V_TOK + NT * (p - len(IN_PAIRS))

    def in_tiles(p):
        lo, hi = [(0, 6), (6, 8)][p] if p < 2 else (4 * p, 4 * p + 4)
        return [(v,) + IN_PAIRS[IN_ORDER[v // 2][0]][v % 2] + (IN_ORDER[v // 2][1],) for v in range(lo, hi)]

    W1 = [A["cmp_k_w1"][0], A["cmp_v_w1"][0]]
    NW1 = CMP_BLOCK // 8

    def load_w1(sp, i):
        n, l0 = i // NW1, (i % NW1) * 8
        if i >= 4:
            sp.wait_ge(w1_used, i - 3)
        sp.dma_start(w1[i % 4], W1[n][l0:l0 + 8].rearrange("l d e -> d l e")).then_inc(w1_loaded[i % 4], 16)

    with nc.Block() as block:
        @block.sync
        def _(sp):
            x_rows = A["x"][0].rearrange("(t p) d -> p t d", p=P)

            def load_x(i):
                sp.dma_start(fT[:, 2 * i:2 * i + 2, :], x_rows[:, 2 * i:2 * i + 2, :]).then_inc(x_loaded[i], 16)

            load_x(0)
            load_x(1)
            for name, rows in VEC_ROWS:
                src = A[name].rearrange("l (c p) -> (l c) p", p=P) if len(A[name].shape) == 2 \
                    else A[name].rearrange("l c p -> (l c) p")
                sp.dma_start(vec_rows[VEC_AT[name]:VEC_AT[name] + rows, :], src).then_inc(vec_loaded, 16)
            for i, name in enumerate(("cmp_k_pe", "cmp_v_pe")):
                sp.dma_start(pe_rows[i * CMP_BLOCK:(i + 1) * CMP_BLOCK, :], A[name][0]).then_inc(vec_loaded, 16)
            sp_load(sp, 0)
            sp_load(sp, 1)
            load_x(2)
            load_x(3)
            for u in range(2, 6):
                sp_load(sp, u)
            with sp.Fori(1, ITERS) as t:
                sp_ffn(sp, 0, t, 0)
            for u in range(U_IN, U_IN + AHEAD + RAWS):
                sp_load(sp, u)
            for c in range(KC):
                sp.wait_ge(x_ready, 8 + c + 1)
                sp.dma_start(x_spill[c], xT[:, c, :]).then_inc(x_spilled, 16)
            for u in range(U_IN + AHEAD + RAWS, U_OUT + AHEAD + RAWS):
                sp_load(sp, u)
                if u == U_OUT:
                    sp.wait_ge(v_ready, V_TOK + NT)
                    load_w1(sp, 1)
                    load_w1(sp, 0)

        @block.gpsimd
        def _(pool):
            pool.memset(ident[:, :], 0.0).then_inc(masks_made, 1)
            pool.memset(identb[:, :], 0.0).then_inc(masks_made, 1)
            pool.memset(neg_future[:, :], 0.0).then_inc(masks_made, 1)
            pool.memset(neg_past[:, :], 0.0).then_inc(masks_made, 1)
            pool.memset(neg_cmp[:, :, :], 0.0).then_inc(masks_made, 1)
            pool.memset(cmp_valid[:, :, :], 1.0).then_inc(masks_made, 1)
            pool.memset(gla_causal[:, :], 1.0).then_inc(masks_made, 1)
            pool.wait_ge(masks_made, 7)
            for m in (ident, identb):
                pool.affine_select(out=m[:, :], in_=m[:, :], compare_op=ALU.not_equal, fill=1.0, base=0,
                                   pattern=[[-1, P]], channel_multiplier=1).then_inc(masks_made, 1)
            pool.affine_select(out=neg_future[:, :], in_=neg_future[:, :], compare_op=ALU.is_ge, fill=NEG, base=0,
                               pattern=[[-1, P]], channel_multiplier=1).then_inc(masks_made, 1)
            pool.affine_select(out=neg_past[:, :], in_=neg_past[:, :], compare_op=ALU.is_gt, fill=NEG, base=0,
                               pattern=[[1, P]], channel_multiplier=-1).then_inc(masks_made, 1)
            for m, fill in ((neg_cmp, NEG), (cmp_valid, 0.0)):
                pool.affine_select(out=m[:, :, :], in_=m[:, :, :], compare_op=ALU.is_ge, fill=fill,
                                   base=-(CMP_BLOCK - 1), pattern=[[P, NT], [-CMP_STRIDE, CMPW]],
                                   channel_multiplier=1).then_inc(masks_made, 1)
            pool.affine_select(out=gla_causal[:, :], in_=gla_causal[:, :], compare_op=ALU.is_ge, fill=0.0, base=0,
                               pattern=[[1, P]], channel_multiplier=-1).then_inc(masks_made, 1)
            pool.wait_ge(masks_made, 14)
            pool.memset(gla_causal[0:CHUNK, CHUNK:P], 0.0).then_inc(masks_made, 1)
            for k in range(2, 6):
                pool_norm(pool, k)

        @block.scalar
        def _(act):
            row = sg[:, :, :].rearrange("p a b -> p (a b)")

            def row_norm(h):
                for t in range(4):
                    i = 4 * h + t
                    act.wait_ge(x_loaded[i // 2], 16)
                    if i > 0:
                        act.wait_ge(rows_squared, i)
                    act.activation(row, fT[:, i, :], ACT.Square, accum_out=rms[:, h, 4 + t:5 + t]).then_inc(rows_squared, 1)
                act.wait_ge(rows_squared, 4 * (h + 1))
                act.wait_ge(const_ready, 2)
                act.activation(rms[:, h, 0:4], rms[:, h, 4:8], ACT.Sqrt, scale=1.0 / D, bias=eps[:, 0:1]).then_inc(rms_ready, 1)

            def empty_turned(h):
                for c in range(0, KC, 2):
                    r = KC * h + c
                    act.wait_ge(xt_turned, r + 1)
                    act.activation(half(xT, c, h), PS[:, 4 + r % 4, :], ACT.Copy).then_inc(xt_act, 1)

            row_norm(0)
            empty_turned(0)
            for u in range(2):
                act_round(act, u)
            for c in range(KC):
                act_hi(act, 0, c, u_first[:, c, :], (u32_ready, c + 1))
            row_norm(1)
            empty_turned(1)
            for u in range(2, AHEAD):
                act_round(act, u)
            act_silu(act, 0, 0, 0, True)
            act_hi_half(act, 1, fT, u32_done(0))
            act_ffn(act, 0, 0, True)
            with act.Fori(1, ITERS) as t:
                act_ffn(act, 0, t, False)
            act_cross(act, 2, 0, f_done(0))

            w_in_k = A["w_in"][0].rearrange("(k p) f -> p k f", p=P)
            for p in range(len(IN_PAIRS) + len(TOK_PAIRS)):
                for i in range(2):
                    u = U_IN + 2 * p + i + AHEAD
                    act_round(act, u, in_free(p))
                if p == 0:
                    act.wait_ge(ulo_ready, 32)
                if p == 2:
                    act.wait_ge(x_spilled, 16 * KC)
                    act.dma_start(small_raw[:, :, 0:GATES], w_in_k[:, :, COL["gate"]:COL["gate"] + GATES]).then_inc(small_loaded, 16)
                    act.dma_start(small_raw[:, :, GATES:SMALL], w_in_k[:, :, COL["gdown"]:COL["gdown"] + RANK]).then_inc(small_loaded, 16)
                if p == 6:
                    act.wait_ge(small_loaded, 32)
                    act.activation(small_hi[:, :, :], small_raw[:, :, :], ACT.Copy).then_inc(small_hi_ready, 1)
                if p < len(IN_PAIRS):
                    for v, name, m, h in in_tiles(p):
                        if tile_owner(v) != "act":
                            continue
                        act.wait_ge(v_ready, v + 1)
                        if name == "gog":
                            g = v % 4
                            if m >= 2:
                                act.wait_ge(gog_spilled[g], 16)
                            act.activation(gog_out[:, g, :], PS[:, v_bank(v), :], ACT.Silu).then_inc(v_act, 1)
                            act.wait_ge(v_act, owner_rank(v))
                            act.dma_start(gog_spill[m, :, h * HALF:(h + 1) * HALF], gog_out[:, g, :])\
                               .then_inc(gog_spilled[g], 16)
                        else:
                            dst, scale = fm_target(name, m, h)
                            act.activation(dst, PS[:, v_bank(v), :], ACT.Copy, scale=scale).then_inc(v_act, 1)
                else:
                    n = p - len(IN_PAIRS)
                    for t in range(0, NT, 2):
                        v = V_TOK + NT * n + t
                        act.wait_ge(v_ready, v + 1)
                        dst, w = (vtok[:, t, :], VT) if n == 0 else (gv[:, t, (n - 1) * 2 * P:n * 2 * P], 2 * P)
                        act.activation(dst, PS[:, v % 8, 0:w], ACT.Copy).then_inc(v_act, 1)
            for g in range(4):
                act.wait_ge(gog_spilled[g], 32)

        @block.vector
        def _(dve):
            dve.memset(ones[:, :], 1.0).then_inc(const_ready, 1)
            dve.memset(eps[:, :], EPS).then_inc(const_ready, 1)
            dve.memset(zero[:, :], 0.0)
            dve.wait_ge(vec_turned, 1)
            dve.tensor_copy(vec[:, :], PS[:, 0, 0:NVEC]).then_inc(vec_kept, 1)
            dve.wait_ge(vec_turned, 2)
            dve.tensor_copy(pe[:, :], PS[:, 1, 0:2 * CMP_BLOCK]).then_inc(vec_kept, 1)
            dve.wait_ge(vec_kept, 1)
            for name in HALVED:
                g = vec[:, VEC_AT[name]:VEC_AT[name] + KC]
                dve.tensor_scalar(g, g, 0.5, None, ALU.mult).then_inc(vec_kept, 1)

            def empty_turned(h):
                for c in range(1, KC, 2):
                    r = KC * h + c
                    dve.wait_ge(xt_turned, r + 1)
                    dve.tensor_copy(half(xT, c, h), PS[:, 4 + r % 4, :]).then_inc(xt_dve, 1)

            empty_turned(0)
            dve.wait_ge(masks_made, 8)
            dve_norm(dve, 0)
            for u in range(2):
                dve_rest(dve, u)
            dve.wait_ge(vec_kept, 2 + len(HALVED))
            dve.wait_ge(xt_act, 4)
            dve.wait_ge(xt_dve, 4)
            dve_apply(dve, 0, 0, "ffn1_pre_g", lambda c: u_first[:, c, :])
            empty_turned(1)
            dve_norm(dve, 1)
            for u in range(2, AHEAD):
                dve_rest(dve, u)
            dve.wait_ge(xt_act, 8)
            dve.wait_ge(xt_dve, 8)
            dve_h(dve, 0, 0, 0, True)
            dve_apply(dve, 0, 1, "ffn1_pre_g")
            dve_ffn(dve, 0, 0, True)
            with dve.Fori(1, LAST) as t:
                dve_ffn(dve, 0, t, False)
            dve_ffn_last(dve, 0, 2)
            dve_cross(dve, 2, 0, "ffn1_post_g", "mix_pre_g",
                      lambda c: dve_keep(dve, 0, LAST, 14 + c, False) if c < 2 else None)

            for p in range(len(IN_PAIRS) + len(TOK_PAIRS)):
                for i in range(2):
                    u = U_IN + 2 * p + i + AHEAD
                    dve_rest(dve, u)
                if p == 0:
                    dve.wait_ge(ulo_ready, 32)
                if p == 2:
                    dve.wait_ge(x_spilled, 16 * KC)
                if p == 6:
                    dve.wait_ge(small_hi_ready, 1)
                    dve.tensor_tensor(small_lo[:, :, :], small_raw[:, :, :], small_hi[:, :, :].bitcast(F32), ALU.subtract)\
                       .then_inc(small_lo_ready, 1)
                if p < len(IN_PAIRS):
                    for v, name, m, h in in_tiles(p):
                        if tile_owner(v) != "dve":
                            continue
                        dve.wait_ge(v_ready, v + 1)
                        dst, _scale = fm_target(name, m, h)
                        dve.tensor_copy(dst, PS[:, v_bank(v), :]).then_inc(v_dve, 1)
                else:
                    n = p - len(IN_PAIRS)
                    for t in range(1, NT, 2):
                        v = V_TOK + NT * n + t
                        dve.wait_ge(v_ready, v + 1)
                        dst, w = (vtok[:, t, :], VT) if n == 0 else (gv[:, t, (n - 1) * 2 * P:n * 2 * P], 2 * P)
                        dve.tensor_copy(dst, PS[:, v % 8, 0:w]).then_inc(v_dve, 1)

        @block.tensor
        def _(pe_):
            def turn_x(h, c):
                r = KC * h + c
                if c == 0:
                    pe_.wait_ge(x_loaded[2 * h], 16)
                    pe_.wait_ge(x_loaded[2 * h + 1], 16)
                if r >= 4:
                    pe_.wait_ge((xt_act, xt_dve)[r % 2], (r - 4) // 2 + 1)
                for t in range(4):
                    mm = pe_.transpose(PS[:, 4 + r % 4, t * P:(t + 1) * P], fT[:, 4 * h + t, c * P:(c + 1) * P], ident[:, :])
                mm.then_inc(xt_turned, 1)

            def second_half(k):
                if k == KC - 1:
                    pe_.wait_ge(xt_act, 8)
                    pe_row(pe_, 1)

            pe_.wait_ge(masks_made, 8)
            pe_.wait_ge(vec_loaded, 16 * (len(VEC_ROWS) + 2))
            pe_.transpose(PS[:, 0, 0:NVEC], vec_rows[0:NVEC, :], ident[0:NVEC, 0:NVEC]).then_inc(vec_turned, 1)
            pe_.transpose(PS[:, 1, 0:2 * CMP_BLOCK], pe_rows[:, :], ident[0:2 * CMP_BLOCK, 0:2 * CMP_BLOCK]).then_inc(vec_turned, 1)
            for c in range(KC):
                turn_x(0, c)
            pe_.wait_ge(const_ready, 1)
            pe_row(pe_, 0)
            pe_.wait_ge(vec_kept, 2)
            pe_gate_up(pe_, 0, 0, 0, 0, True)
            for c in range(KC):
                turn_x(1, c)
            pe_gate_up(pe_, 0, 0, 0, 1, True, second_half)
            for c in range(2):
                pe_gate_up(pe_, 0, 0, 1, c, True)
            pe_down(pe_, 0, 0, True)
            with pe_.Fori(1, LAST) as t:
                pe_ffn(pe_, 0, t, False)
            pe_ffn(pe_, 0, LAST, False, after_tile=lambda r: pe_early(pe_, 2, r))
            pe_between(pe_, 2)

            def bank_free(v):
                if v >= 8:
                    before = max(w for w in range(v) if v_bank(w) == v_bank(v))
                    pe_.wait_ge(v_act if tile_owner(before) == "act" else v_dve, owner_rank(before))

            for n, (p, h) in enumerate(IN_ORDER):
                u = U_IN + 2 * p
                if h == 0:
                    pe_.wait_ge(lo_ready, u + 2)
                for k in range(KC):
                    if p == 0:
                        pe_.wait_ge(ulo_ready, 16 + 8 * h + k + 1)
                    for i in range(2):
                        v = 2 * n + i
                        if k == 0:
                            bank_free(v)
                        w = [x[:, (u + i) % SLOTS, k * P:(k + 1) * P] for x in (w_hi, w_lo)]
                        for s, (a, b) in enumerate(passes(w, [half(x, k, h) for x in (u_hi, u_lo)])):
                            mm = pe_.matmul(PS[:, v_bank(v), :], a, b, start=(k == 0 and s == 0), stop=(k == KC - 1 and s == 2))
                        if k == KC - 1:
                            mm.then_inc(v_ready, 1)
                if n == 1:
                    pe_sum_up(pe_, 5)
                    pe_row(pe_, 5)
            for n in range(len(TOK_PAIRS)):
                u = U_IN + 2 * (len(IN_PAIRS) + n)
                pe_.wait_ge(lo_ready, u + 2)
                if n == 0:
                    pe_.wait_ge(small_lo_ready, 1)
                for t in range(NT):
                    v = V_TOK + NT * n + t
                    bank_free(v)
                    for k in range(KC):
                        x = [y[:, k, t * P:(t + 1) * P] for y in (u_hi, u_lo)]
                        w = [y[:, u % SLOTS:u % SLOTS + 2, k * P:(k + 1) * P] for y in (w_hi, w_lo)]
                        for s, (a, b) in enumerate(passes(x, w)):
                            mm = pe_.matmul(PS[:, v % 8, 0:2 * P].rearrange("p (a b) -> p a b", a=2), a, b,
                                            start=(k == 0 and s == 0), stop=(k == KC - 1 and s == 2))
                    if n == 0:
                        for k in range(KC):
                            x = [y[:, k, t * P:(t + 1) * P] for y in (u_hi, u_lo)]
                            w = [y[:, k, :] for y in (small_hi, small_lo)]
                            for s, (a, b) in enumerate(passes(x, w)):
                                mm = pe_.matmul(PS[:, v % 8, 2 * P:VT], a, b, start=(k == 0 and s == 0),
                                                stop=(k == KC - 1 and s == 2))
                    mm.then_inc(v_ready, 1)

    with nc.Block() as block:
        def outer(n, pair):
            col = ((n // 2) % 2 * PAIRS + pair) * P
            return PS[:, 4 * (n % 2) + n // 4, col:col + P]

        @block.sync
        def _(sp):
            sp.dma_start(gup[:, :], A["gla_gate_up"][0]).then_inc(gup_loaded, 16)
            for n in range(2):
                sp.dma_start(w2[:, n, :], A[("cmp_k_w2", "cmp_v_w2")[n]][0]).then_inc(w2_loaded, 16)
            for i in range(2, 2 * NW1):
                load_w1(sp, i)

        @block.scalar
        def _(act):
            flat = [x[:, :, :].rearrange("p a b -> p (a b)") for x in (gx, gb, ge)]
            act.activation(gate[:, :, :], vtok[:, :, 2 * P:2 * P + GATES], ACT.Sigmoid)
            act.wait_ge(gx_ready, 4)
            act.activation(flat[1], flat[0], ACT.Abs).then_inc(g_act, 1)
            act.wait_ge(g_act, 1)
            act.activation(flat[1], flat[1], ACT.Exp, scale=-1.0).then_inc(g_act, 1)
            act.wait_ge(g_act, 2)
            act.activation(flat[1], flat[1], ACT.Ln, bias=1.0).then_inc(g_act, 1)
            act.wait_ge(g_dve, 3)
            act.activation(flat[2], flat[1], ACT.Exp, scale=1.0 / GATE_NORM).then_inc(g_act, 1)
            act.wait_ge(g_dve, 4)
            act.activation(flat[0], flat[0], ACT.Exp, scale=1.0 / GATE_NORM).then_inc(g_act, 1)
            act.wait_ge(g_dve, 5)
            act.activation(flat[2], flat[1], ACT.Exp, scale=-1.0 / GATE_NORM).then_inc(g_act, 1)
            b_last = gb[:, :, :].rearrange("p a (n c) -> p a n c", c=CHUNK)[:, :, :, CHUNK - 1]
            act.activation(decay[:, :, :], b_last, ACT.Exp, scale=1.0 / GATE_NORM).then_inc(g_act, 1)
            for n in range(2):
                act.wait_ge(w1_used, NW1 * (n + 1))
                act.activation(hid[:, n, 0:N_CMP], PS[:, 6 + n, 0:N_CMP], ACT.Silu).then_inc(hid_kept, 1)
            for j in range(4):
                act.wait_ge(kend_turned, j + 1)
                act.activation(kend[:, 2 * j:2 * j + 2, :], PS[:, j, :].rearrange("p (a b) -> p a b", a=2), ACT.Copy)\
                   .then_inc(kend_kept, 1)
            for h in range(2):
                act.wait_ge(go_done, 4 * (h + 1))
                for hd in range(HEADS):
                    act.activation(half(oT, HEADS + hd, h), PS[:, hd, :], ACT.Copy).then_inc(go_kept, 1)

        @block.vector
        def _(dve):
            keep = scan_keep[:, :].rearrange("p (n c) -> p n c", c=CHUNK)
            chain = lambda n: dve.wait_ge(g_dve, n)
            for j in range(2):
                dve.wait_ge(gd_turned, j + 1)
                dve.tensor_copy(gdT[:, j * HALF:(j + 1) * HALF], PS[0:RANK, j, :]).then_inc(gd_kept, 1)
            for j in range(4):
                pair, h = divmod(j, 2)
                dve.wait_ge(gpre_ready, j + 1)
                bias = vec[:, VEC_AT["gla_gate_bias"] + pair:VEC_AT["gla_gate_bias"] + pair + 1]
                dve.tensor_scalar(half(gx, pair, h), PS[:, 2 + j, :], bias, None, ALU.add).then_inc(gx_ready, 1)
            for n in range(2):
                src = kcmp[:, n, :].rearrange("p (n c) -> p n c", c=CMP_STRIDE)
                for hb, dst in ((0, kv_a), (1, kv_b)):
                    at0 = n * CMP_BLOCK + hb * CMP_STRIDE
                    dve.tensor_tensor(dst[:, n, :].rearrange("p (n c) -> p n c", c=CMP_STRIDE), src,
                                      pe[:, at0:at0 + CMP_STRIDE].unsqueeze(1).to_broadcast([P, SEQ // CMP_STRIDE, CMP_STRIDE]),
                                      ALU.add).then_inc(kv_biased, 1)
            dve.memset(kcT[:, :], 0.0).then_inc(cmp_kept, 1)
            dve.memset(vc[:, :], 0.0).then_inc(cmp_kept, 1)
            dve.memset(scan_keep[:, :], 1.0).then_inc(cmp_kept, 1)
            dve.wait_ge(cmp_kept, 3)
            dve.memset(keep[:, :, 0:1], 0.0).then_inc(cmp_kept, 1)
            dve.wait_ge(g_act, 3)
            flat = [x[:, :, :].rearrange("p a b -> p (a b)") for x in (gx, gb, ge)]
            dve.scalar_tensor_tensor(flat[0], flat[0], 0.0, flat[1], ALU.min, ALU.subtract).then_inc(g_dve, 1)
            chain(1)
            dve.wait_ge(cmp_kept, 4)
            for pair in range(PAIRS):
                dve.tensor_tensor_scan(gb[:, pair, :], scan_keep[:, :], gx[:, pair, :], 0.0, ALU.mult, ALU.add)\
                   .then_inc(g_dve, 1)
            chain(3)
            by_chunk = [x[:, :, :].rearrange("p a (n c) -> p (a n) c", c=CHUNK) for x in (gx, gb)]
            dve.tensor_tensor(by_chunk[0], by_chunk[1][:, :, CHUNK - 1:CHUNK].to_broadcast([P, PAIRS * N_CHUNK, CHUNK]),
                              by_chunk[1], ALU.subtract).then_inc(g_dve, 1)
            dve.wait_ge(g_act, 4)
            dve.tensor_tensor(gq[:, :, :], gq[:, :, :], ge[:, :, :], ALU.mult).then_inc(g_dve, 1)
            dve.wait_ge(g_act, 5)
            dve.tensor_tensor(gx[:, :, :], gx[:, :, :], gk[:, :, :], ALU.mult).then_inc(g_dve, 1)
            chain(6)
            dve.wait_ge(g_act, 6)
            dve.tensor_tensor(gk[:, :, :], gk[:, :, :], ge[:, :, :], ALU.mult).then_inc(g_dve, 1)
            dve.wait_ge(cmp_ready, 1)
            dve.tensor_copy(kcT[:, 0:N_CMP], PS[:, 6, P:P + N_CMP]).then_inc(cmp_kept, 1)
            dve.wait_ge(cmp_ready, 2)
            dve.tensor_copy(vc[0:N_CMP, :], PS[0:N_CMP, 7, P:2 * P]).then_inc(cmp_kept, 1)
            dve.wait_ge(g_act, 7)
            for n in range(N_CHUNK - 1):
                dve.wait_ge(outer_ready, min(n // 4 * 4 + 2 + n % 2, N_CHUNK - 2) + 1)
                if n > 0:
                    dve.wait_ge(state_ready, 2 * n)
                for pair in range(PAIRS):
                    add = outer(n, pair)
                    if n == 0:
                        dve.tensor_copy(state[:, 1, pair, :], add).then_inc(state_ready, 1)
                    else:
                        dve.scalar_tensor_tensor(state[:, n + 1, pair, :], state[:, n, pair, :], decay[:, pair, n:n + 1],
                                                 add, ALU.mult, ALU.add).then_inc(state_ready, 1)
            for t in range(NT):
                dve.wait_ge(a_ready, t + 1)
                if t >= 2:
                    dve.wait_ge(go_done, t - 1)
                dve.tensor_tensor(at_sb[:, t % 2, :].rearrange("p (a b i) -> p a b i", a=2, b=2),
                                  PS[:, 4 + 2 * (t % 2):6 + 2 * (t % 2), 0:2 * P].rearrange("p a (b i) -> p a b i", b=2),
                                  gla_causal[:, :].unsqueeze(1).unsqueeze(1).to_broadcast([P, 2, 2, P]), ALU.mult).then_inc(a_masked, 1)

        @block.tensor
        def _(pe_):
            for t in range(NT):
                mm = pe_.transpose(PS[0:RANK, t // 4, (t % 4) * P:(t % 4 + 1) * P], vtok[:, t, 2 * P + GATES:VT], ident[:, :])
                if t % 4 == 3:
                    mm.then_inc(gd_turned, 1)
            pe_.wait_ge(gup_loaded, 16)
            for j in range(4):
                pair, h = divmod(j, 2)
                pe_.wait_ge(gd_kept, h + 1)
                pe_.matmul(PS[:, 2 + j, :], gup[:, pair * P:(pair + 1) * P], gdT[:, h * HALF:(h + 1) * HALF],
                           start=True, stop=True).then_inc(gpre_ready, 1)
            for i in range(2 * NW1):
                n = i // NW1
                if i % NW1 == 0:
                    pe_.wait_ge(kv_biased, 2 * n + 2)
                pe_.wait_ge(w1_loaded[i % 4], 16 * (i // 4 + 1))
                for l8 in range(8):
                    l = (i % NW1) * 8 + l8
                    src = (kv_a, kv_b)[l // CMP_STRIDE]
                    mm = pe_.matmul(PS[:, 6 + n, 0:N_CMP], w1[i % 4][:, l8, :],
                                    src[:, n, l:l + CMP_STRIDE * (N_CMP - 1) + 1:CMP_STRIDE],
                                    start=(l == 0), stop=(l == CMP_BLOCK - 1))
                mm.then_inc(w1_used, 1)
            pe_.wait_ge(w2_loaded, 32)
            pe_.wait_ge(hid_kept, 1)
            pe_.matmul(PS[:, 6, P:P + N_CMP], w2[:, 0, :], hid[:, 0, 0:N_CMP], start=True, stop=True).then_inc(cmp_ready, 1)
            pe_.wait_ge(hid_kept, 2)
            pe_.matmul(PS[0:N_CMP, 7, P:2 * P], hid[:, 1, 0:N_CMP], w2[:, 1, :], start=True, stop=True).then_inc(cmp_ready, 1)
            pe_.wait_ge(g_dve, 6)
            pe_.wait_ge(gx_ready, 4)
            for j in range(4):
                for i in range(4):
                    t, pair = 2 * j + i // 2, i % 2
                    mm = pe_.transpose(PS[:, j, i * P:(i + 1) * P], gx[:, pair, t * P:(t + 1) * P], ident[:, :])
                mm.then_inc(kend_turned, 1)
            pe_.wait_ge(cmp_kept, 6)
            for n in range(N_CHUNK - 1):
                t, lo = n // 2, (n % 2) * CHUNK
                if n % 4 == 0:
                    pe_.wait_ge(kend_kept, n // 4 + 1)
                if n == 0:
                    pe_.wait_ge(kend_kept, 4)
                for hd in range(HEADS):
                    pair, hh = divmod(hd, 2)
                    mm = pe_.matmul(outer(n, pair)[hh * GK:(hh + 1) * GK, :],
                                    kend[lo:lo + CHUNK, t, hd * GK:(hd + 1) * GK],
                                    gv[lo:lo + CHUNK, t, hd * GV:(hd + 1) * GV], start=True, stop=True)
                mm.then_inc(outer_ready, 1)
            pe_.wait_ge(g_dve, 7)
            pe_.wait_ge(state_ready, 2 * (N_CHUNK - 1))

            def scores(t):
                if t >= 2:
                    pe_.wait_ge(a_masked, t - 1)
                for hd in range(HEADS):
                    pair, hh = divmod(hd, 2)
                    rows = slice(hh * GK, (hh + 1) * GK)
                    mm = pe_.matmul(PS[:, 4 + 2 * (t % 2) + hh, pair * P:(pair + 1) * P], gk[rows, pair, t * P:(t + 1) * P],
                                    gq[rows, pair, t * P:(t + 1) * P], start=True, stop=True)
                mm.then_inc(a_ready, 1)

            scores(0)
            for t in range(NT):
                if t + 1 < NT:
                    scores(t + 1)
                if t == 4:
                    pe_.wait_ge(go_kept, HEADS)
                pe_.wait_ge(a_masked, t + 1)
                for hd in range(HEADS):
                    pair, hh = divmod(hd, 2)
                    rows = slice(hh * GK, (hh + 1) * GK)
                    col = (t % 4) * P
                    pe_.matmul(PS[:, hd, col:col + P], gv[:, t, hd * GV:(hd + 1) * GV], at_sb[:, t % 2, (2 * hh + pair) * P:(2 * hh + pair + 1) * P],
                               start=True, stop=True, skip_group_check=True)
                    for s in range(2):
                        n = 2 * t + s
                        if n > 0:
                            mm = pe_.matmul(PS[:, hd, col + s * CHUNK:col + (s + 1) * CHUNK], state[rows, n, pair, :],
                                            gq[rows, pair, n * CHUNK:(n + 1) * CHUNK], start=False, stop=True,
                                            skip_group_check=True)
                mm.then_inc(go_done, 1)

    OFF = [0, SEQ, SEQ + WINDOW + P]

    def factor(j):
        return HEADS + j

    def win_lo(i):
        return max(0, i - WT)

    def width(i, j):
        return (i + 1) * P if j < HEADS else (i + 1 - win_lo(i)) * P

    def key_tiles(i):
        return [(0, kt, kt * P) for kt in range(i + 1)] + \
               [(1, kt, (kt - win_lo(i)) * P) for kt in range(win_lo(i), i + 1)] + [(2, 0, 0)]

    first_tile = [sum(len(key_tiles(x)) for x in range(i)) for i in range(NT + 1)]

    def share(i, j):
        n = len(key_tiles(i))
        return range(n * j // 9, n * (j + 1) // 9)

    with nc.Block() as block:
        @block.sync
        def _(sp):
            for hd in range(HEADS):
                sp.dma_start(gog[:, hd, :], gog_spill[hd]).then_inc(gog_back, 16)
            sp.wait_ge(gog_back, 16 * HEADS)

        @block.scalar
        def _(act):
            for i in range(-1, NT):
                for j in range(9):
                    if i + 1 < NT:
                        it = 9 * (i + 1) + j
                        b, slot, par = j // HEADS, it % 2, (i + 1) % 2
                        act.wait_ge(max_done, it + 1)
                        if i + 1 >= 2 and j == 0:
                            act.wait_ge(pv_done, first_tile[i])
                        if b < 2:
                            w = width(i + 1, j)
                            act.activation(prob[:, par, j % HEADS, OFF[b]:OFF[b] + w],
                                           PS[:, 2 * slot:2 * slot + 2, :].rearrange("p a b -> p (a b)")[:, 0:w], ACT.Exp,
                                           bias=neg_max[:, par, factor(j):factor(j) + 1],
                                           accum_out=row_sum[:, par, factor(j):factor(j) + 1]).then_inc(exp_done, 1)
                        else:
                            for hd in range(HEADS):
                                ins = act.activation(prob[:, par, hd, OFF[2]:OFF[2] + CMPW],
                                                     PS[:, 2 * slot, hd * CMPW:(hd + 1) * CMPW], ACT.Exp,
                                                     bias=neg_max[:, par, hd:hd + 1],
                                                     accum_out=row_sum[:, par, hd:hd + 1])
                            ins.then_inc(exp_done, 1)
                    if i >= 0:
                        for m in share(i, j):
                            n = first_tile[i] + m
                            if n % 2 == 0:
                                rows = CMPW if key_tiles(i)[m][0] == 2 else P
                                act.wait_ge(pt_ready, n + 1)
                                if n >= 4:
                                    act.wait_ge(pv_done, n - 3)
                                act.activation(probT[0:rows, n % 4, :], PS[0:rows, 4 + n % 2, :], ACT.Copy).then_inc(pt_act, 1)
                if i >= 0:
                    act.wait_ge(pv_done, first_tile[i + 1])
                    act.activation(oT[:, 0:HEADS, i * P:(i + 1) * P],
                                   PS[:, 6 + i % 2, :].rearrange("p (h q) -> p h q", h=HEADS), ACT.Copy).then_inc(o_kept, 1)

        @block.vector
        def _(dve):
            for i in range(-1, NT):
                if i >= 0:
                    par = i % 2
                    dve.wait_ge(exp_done, 9 * (i + 1))
                    dve.reciprocal(inv_sum[:, par, :], row_sum[:, par, :]).then_inc(r_ready, 1)
                    dve.wait_ge(r_ready, i + 1)
                    dve.tensor_tensor(p_scale[:, par, :].rearrange("p (b h) -> p b h", b=3),
                                      inv_sum[:, par, :].rearrange("p (b h) -> p b h", b=3),
                                      gate[:, i, :].rearrange("p (h b) -> p b h", b=3),
                                      ALU.mult).then_inc(p_scaled, 1)
                    dve.wait_ge(p_scaled, 13 * i + 1)
                    for j in range(8):
                        b = j // HEADS
                        pr = prob[:, par, j % HEADS, OFF[b]:OFF[b] + width(i, j)]
                        dve.tensor_scalar(pr, pr, p_scale[:, par, factor(j):factor(j) + 1], None, ALU.mult).then_inc(p_scaled, 1)
                    for hd in range(HEADS):
                        pr = prob[:, par, hd, OFF[2]:OFF[2] + CMPW]
                        dve.scalar_tensor_tensor(pr, pr, p_scale[:, par, hd:hd + 1], cmp_valid[:, i, :],
                                                 ALU.mult, ALU.mult).then_inc(p_scaled, 1)
                for j in range(9):
                    if i + 1 < NT:
                        it = 9 * (i + 1) + j
                        slot, par = it % 2, (i + 1) % 2
                        dve.wait_ge(s_ready, it + 1)
                        if i + 1 >= 2 and j == 0:
                            dve.wait_ge(exp_done, 9 * i)
                        if j < 8:
                            w = width(i + 1, j)
                            dve.tensor_reduce(neg_max[:, par, factor(j):factor(j) + 1],
                                              PS[:, 2 * slot:2 * slot + 2, :].rearrange("p a b -> p (a b)")[:, 0:w],
                                              AX.X, ALU.max, negate=True).then_inc(max_done, 1)
                        else:
                            dve.tensor_reduce(neg_max[:, par, 0:HEADS],
                                              PS[:, 2 * slot, 0:HEADS * CMPW].rearrange("p (h n) -> p h n", h=HEADS),
                                              AX.X, ALU.max, negate=True).then_inc(max_done, 1)
                    if i >= 0:
                        for m in share(i, j):
                            n = first_tile[i] + m
                            if n % 2 == 1:
                                rows = CMPW if key_tiles(i)[m][0] == 2 else P
                                dve.wait_ge(pt_ready, n + 1)
                                if n >= 4:
                                    dve.wait_ge(pv_done, n - 3)
                                dve.tensor_copy(probT[0:rows, n % 4, :], PS[0:rows, 4 + n % 2, :]).then_inc(pt_dve, 1)

        @block.tensor
        def _(pe_):
            def scores(i, j):
                it = 9 * i + j
                slot = it % 2
                if it >= 2:
                    pe_.wait_ge(exp_done, it - 1)
                if j < 8:
                    hd, keys, lo = (j, ksT, 0) if j < HEADS else (j - HEADS, kwT, win_lo(i) * P)
                    w = width(i, j)
                    wide = PS[:, 2 * slot:2 * slot + 2, :].rearrange("p a b -> p (a b)")
                    for c0 in range(0, w, HALF):
                        c1 = min(w, c0 + HALF)
                        masks = [(m, at0) for m, at0, on in ((neg_past, 0, j >= HEADS and i >= WT), (neg_future, w - P, True))
                                 if on and c0 <= at0 < c1]
                        mm = pe_.matmul(wide[:, c0:c1], qT[:, hd, i * P:(i + 1) * P], keys[:, lo + c0:lo + c1],
                                        start=True, stop=True)
                        for m, at0 in masks:
                            mm = pe_.matmul(wide[:, at0:at0 + P], identb[:, :], m[:, :], start=False, stop=True,
                                            skip_group_check=True)
                else:
                    for hd in range(HEADS):
                        pe_.matmul(PS[:, 2 * slot, hd * CMPW:(hd + 1) * CMPW], qT[:, hd, i * P:(i + 1) * P], kcT[:, :],
                                   start=(hd == 0), stop=True, skip_group_check=True)
                    mm = pe_.matmul(PS[:, 2 * slot, 0:HEADS * CMPW].rearrange("p (h n) -> p h n", h=HEADS), identb[:, :],
                                    neg_cmp[:, i, :].unsqueeze(1).to_broadcast([P, HEADS, CMPW]), start=False, stop=True,
                                    skip_group_check=True)
                mm.then_inc(s_ready, 1)

            def turn(i, m):
                b, kt, at0 = key_tiles(i)[m]
                n = first_tile[i] + m
                rows = CMPW if b == 2 else P
                pe_.wait_ge(p_scaled, 13 * i + (5, 9, 13)[b])
                if n >= 2:
                    pe_.wait_ge((pt_act, pt_dve)[n % 2], (n - 2) // 2 + 1)
                for hd in range(HEADS):
                    mm = pe_.transpose(PS[0:rows, 4 + n % 2, hd * P:(hd + 1) * P],
                                       prob[:, i % 2, hd, OFF[b] + at0:OFF[b] + at0 + rows], ident[:, :])
                mm.then_inc(pt_ready, 1)

            def values(i, m):
                b, kt, at0 = key_tiles(i)[m]
                n, last = first_tile[i] + m, m == len(key_tiles(i)) - 1
                rows = CMPW if b == 2 else P
                v = (vtok[:, kt, 0:P], vtok[:, kt, P:2 * P], vc[:, :])[b]
                pe_.wait_ge((pt_act, pt_dve)[n % 2], n // 2 + 1)
                if m == 0 and i >= 2:
                    pe_.wait_ge(o_kept, i - 1)
                mm = pe_.matmul(PS[:, 6 + i % 2, :], v, probT[0:rows, n % 4, :], start=(m == 0), stop=last)
                mm.then_inc(pv_done, 1)

            waiting = []
            for i in range(-1, NT):
                for j in range(9):
                    if i + 1 < NT:
                        scores(i + 1, j)
                    if i >= 0:
                        for m in share(i, j):
                            turn(i, m)
                            waiting.append((i, m))
                            if len(waiting) > 1:
                                values(*waiting.pop(0))
                if i >= 0:
                    values(*waiting.pop(0))

    groups = [(h, kind) for h in range(2) for kind in range(2)]

    def scaled_first(x):
        return 6 * (x // 8 * 2) + (x % 8 + 1 if x % 8 < 4 else 4 + 2 * (x % 4) + 1)

    def scaled_at(x):
        return scaled_first(x) + (x // 4) % 2

    def hsum_bank(g):
        return (6, 7, 3, 3)[g]

    def hrow_bank(x):
        return x % 6 if x < 8 else x % 3

    def hrow_before(x):
        return max((y for y in range(x) if hrow_bank(y) == hrow_bank(x)), default=None)

    def out_kept(h, c):
        return f_kept, R_OUT + pair_tile(h, c) + 1

    def pair_tile(h, m):
        return 2 * PAIR_ORDER.index((m // 2, h)) + m % 2

    def t_done(h, c):
        return t_ready, pair_tile(h, c) + 1

    Y_ORDER = [(t, b) for t in range(4) for b in range(2)] + [(t, b) for b in range(2) for t in range(4, NT)]

    def y_emptied(n):
        if n < 12:
            return y_act, n + 1
        return (y_act, 12 + (n - 12) // 2 + 1) if n % 2 == 0 else (y_dve, (n - 12) // 2 + 1)

    with nc.Block() as block:
        @block.sync
        def _(sp):
            sp.wait_ge(mlo_ready, 16)
            for c in range(KC):
                sp.dma_start(xT[:, c, :], x_spill[c]).then_inc(x_back, 16)
            for u in range(U_OUT + AHEAD + RAWS, U_FFN[1] + 6):
                sp_load(sp, u)
            with sp.Fori(1, ITERS) as t:
                sp_ffn(sp, 1, t, 0)
            for u in range(U_PLE, U_END):
                sp_load(sp, u)
            for t in range(NT):
                sp.wait_ge(*y_emptied(Y_ORDER.index((t, 0))))
                sp.wait_ge(*y_emptied(Y_ORDER.index((t, 1))))
                sp.dma_start(out[0, t * P:(t + 1) * P, :], y_rows[:, t, :]).then_inc(y_stored, 16)
            sp.wait_ge(y_stored, 16 * NT)

        @block.gpsimd
        def _(pool):
            for k in range(6, 14):
                pool_norm(pool, k)

        @block.scalar
        def _(act):
            def head_squares(g):
                h, kind = groups[g]
                for hd in range(HEADS):
                    x = 4 * g + hd
                    if x >= 2:
                        act.wait_ge(hsq_used, x - 1)
                    act.activation(h_sq[:, x % 2, :], half(oT, 4 * kind + hd, h), ACT.Square).then_inc(hsq_ready, 1)
                act.wait_ge(hsq_used, 4 * (g + 1))
                if g >= 2:
                    act.wait_ge(hrstd_ready, g - 1)
                act.activation(rms[:, g % 2, :], PS[:, hsum_bank(g), 0:16], ACT.Sqrt, scale=1.0 / DH, bias=eps[:, 0:1])\
                   .then_inc(hrms_ready, 1)

            def head_round(g):
                h, kind = groups[g]
                for hd in range(HEADS):
                    x = 4 * g + hd
                    act.wait_ge(hn_scaled, scaled_at(x))
                    act.activation(half(u_hi, 4 * kind + hd, h), half(oT, 4 * kind + hd, h), ACT.Copy).then_inc(mhi_ready, 1)

            head_squares(0)
            head_squares(1)
            head_round(0)
            head_round(1)
            for g in (2, 3):
                head_squares(g)
                head_round(g)

            for s in range(4):
                for i in range(2):
                    u = U_OUT + 2 * s + i + AHEAD
                    act_round(act, u, ((v_ready, V_END), (f_ready, R_OUT + 6), (f_ready, R_OUT + 8), (f_ready, R_OUT + 12))[s])
            act_cross(act, 6, 1, out_kept, lambda: act_silu(act, 1, 0, 0, True))
            act_ffn(act, 1, 0, True)
            with act.Fori(1, ITERS) as t:
                act_ffn(act, 1, t, False)
            act.wait_ge(gu_ready, 2 * (Q0[1] + 4 * ITERS))
            for a in range(2):
                act.dma_start(p_place[:, 4:8, HALF + a * PLE:HALF + (a + 1) * PLE],
                              A["p"][0, 0].rearrange("(c a p) f -> a p c f", a=2, p=P)[a]).then_inc(p_loaded, 16)

            def keep_p(j):
                act.wait_ge(p_turned, j + 1)
                act.activation(p_place[:, j // 2:4:2, HALF + (j % 2) * 2 * P:HALF + (j % 2 + 1) * 2 * P]
                               .rearrange("p c (t q) -> p c t q", t=2),
                               PS[:, 3, :].rearrange("p (t c q) -> p c t q", t=2, c=2), ACT.Copy).then_inc(p_kept, 1)

            act_norm(act, 10, fT, f_done(1))
            keep_p(0)
            for c in range(KC):
                act_square(act, 11, c, fT, f_done(1))
                if c % 2 == 1 and c < 6:
                    keep_p(c // 2 + 1)
            act_sqrt(act, 11)
            act_hi_half(act, 0, xT, x_done(2))
            act.wait_ge(f_ready, R_G)
            act.wait_ge(p_kept, 4)
            for c in range(2):
                for hh in range(2):
                    act.activation(half(h_hi, c, hh), p_place[:, 2 * c + hh, HALF:SEQ], ACT.Copy).then_inc(p_hi, 1)

            def round_gate(m, free):
                for i in range(2):
                    act_round(act, U_PLE + 2 + m + i, free)

            def sigmoid(x):
                act.wait_ge(f_ready, R_G + x + 1)
                if x >= 2:
                    act.wait_ge(t_ready, x - 1)
                act.activation(sg[:, x % 2, :], PS[:, 4 + x % 4, :], ACT.Sigmoid).then_inc(sig_done, 1)

            round_gate(2, (f_ready, R_G))
            for c in range(KC):
                act_hi(act, 1, c, half(xT, c, 1), x_done(2)(1, c))
                if c == 0:
                    sigmoid(0)
                    sigmoid(1)
            for x in range(2, 14):
                sigmoid(x)
                if x == 5:
                    round_gate(4, (f_ready, R_G + 6))
                if x == 7:
                    round_gate(6, (f_ready, R_G + 8))
            act.wait_ge(lo_ready, U_END)
            act_norm(act, 12, fT, t_done)
            sigmoid(14)
            for c in range(KC):
                if c == 6:
                    sigmoid(15)
                act_square(act, 13, c, fT, t_done)
            act_sqrt(act, 13)
            for n, (t, b) in enumerate(Y_ORDER):
                if y_emptied(n)[0] is y_act:
                    act.wait_ge(y_turned, n + 1)
                    act.activation(y_rows[:, t, b * HALF:(b + 1) * HALF], PS[:, 4 + n % 4, :], ACT.Copy).then_inc(y_act, 1)

        @block.vector
        def _(dve):
            def keep_out(r):
                (s, h), i = PAIR_ORDER[r // 2], r % 2
                dve.wait_ge(f_ready, R_OUT + r + 1)
                dve.tensor_copy(half(fT, 2 * s + i, h), PS[:, 4 + r % 4, :]).then_inc(f_kept, 1)

            for g, (h, kind) in enumerate(groups):
                if g == 3:
                    keep_out(0)
                    keep_out(1)
                dve.wait_ge(hrms_ready, g + 1)
                dve.reciprocal(rstd[:, g % 2, :], rms[:, g % 2, :]).then_inc(hrstd_ready, 1)
                dve.wait_ge(hrstd_ready, g + 1)

                def diag(hd):
                    x = 4 * g + hd
                    if x >= 2:
                        dve.wait_ge(hrb_ready, x - 1)
                    dve.tensor_tensor(h_diag[:, x % 2, :].rearrange("p (t q) -> p t q", t=4),
                                      ident[:, :].unsqueeze(1).to_broadcast([P, 4, P]),
                                      rstd[:, g % 2, 4 * hd:4 * hd + 4].unsqueeze(2).to_broadcast([P, 4, P]),
                                      ALU.mult).then_inc(hdiag_ready, 1)

                def scale(hd):
                    x = 4 * g + hd
                    o = half(oT, 4 * kind + hd, h)
                    gn = VEC_AT[("nsa_out_g", "gla_out_g")[kind]] + hd
                    dve.wait_ge(hrb_ready, x + 1)
                    dve.scalar_tensor_tensor(o, o, vec[:, gn:gn + 1], PS[:, hrow_bank(x), :], ALU.mult, ALU.mult).then_inc(hn_scaled, 1)
                    if kind == 1:
                        dve.wait_ge(hn_scaled, scaled_first(x))
                        dve.tensor_tensor(o, o, half(gog, hd, h), ALU.mult).then_inc(hn_scaled, 1)

                def rest(hd):
                    x = 4 * g + hd
                    ch = 4 * kind + hd
                    dve.wait_ge(mhi_ready, x + 1)
                    dve.tensor_tensor(half(u_lo, ch, h), half(oT, ch, h), half(u_hi, ch, h).bitcast(F32), ALU.subtract)\
                       .then_inc(mlo_ready, 1)

                diag(0)
                diag(1)
                for hd in range(HEADS):
                    scale(hd)
                    if hd + 2 < HEADS:
                        diag(hd + 2)
                    if hd > 0:
                        rest(hd - 1)
                rest(HEADS - 1)

            for s, tiles in enumerate(((2, 3, 4, 5), (6, 7), (8, 9, 10, 11), (12, 13))):
                for i in range(2):
                    dve_rest(dve, U_OUT + 2 * s + i + AHEAD)
                for r in tiles:
                    keep_out(r)
            dve.wait_ge(x_back, 16 * KC)
            dve_norm(dve, 6)
            dve_cross(dve, 6, 1, "mix_post_g", "ffn2_pre_g", lambda c: keep_out((14, 15)[c // 3]) if c in (0, 3) else None,
                      lambda: dve_h(dve, 1, 0, 0, True))
            dve_ffn(dve, 1, 0, True)
            with dve.Fori(1, LAST) as t:
                dve_ffn(dve, 1, t, False)
            dve_ffn_last(dve, 1, 10)

            def gated(x):
                (s, h), i = PAIR_ORDER[x // 2], x % 2
                dve.wait_ge(sig_done, x + 1)
                dve.wait_ge(e_ready, x + 1)
                dve.tensor_tensor(half(fT, 2 * s + i, h), PS[:, x % 4, :], sg[:, x % 2, :], ALU.mult).then_inc(t_ready, 1)

            def first_half(c):
                if c < 2:
                    dve_keep(dve, 1, LAST, 14 + c, False)
                if c == 5:
                    dve_norm(dve, 11)
                for i in {6: (0,), 7: (1, 2), 8: (3, 4), 9: (5, 6)}.get(c, ()):
                    dve_lo(dve, 3, 0, i, half(xT, i, 0))

            def second_half(c):
                if c == 3:
                    gated(0)
                    gated(1)

            dve_residual(dve, 2, 10, "ffn2_post_g", first_half)
            dve_lo(dve, 3, 0, 7, half(xT, 7, 0))
            for c in range(2):
                for hh in range(2):
                    dve.wait_ge(p_hi, 2 * c + hh + 1)
                    dve.tensor_tensor(half(h_lo, c, hh), p_place[:, 2 * c + hh, HALF:SEQ], half(h_hi, c, hh).bitcast(F32),
                                      ALU.subtract).then_inc(p_lo, 1)
            for m in (2, 3):
                dve_rest(dve, U_PLE + 2 + m)
            dve.wait_ge(p_lo, 4)
            dve_residual(dve, 2, 11, "ffn2_post_g", second_half, lambda c: dve_lo(dve, 3, 1, c, half(xT, c, 1)))
            for x in range(2, 14):
                gated(x)
                if x in (5, 7):
                    for i in range(2):
                        dve_rest(dve, U_PLE + 2 + x - 1 + i)
            dve_norm(dve, 12)

            def last_tiles(c):
                if c == 0:
                    gated(14)
                if c == 4:
                    gated(15)
                if c == 6:
                    dve_norm(dve, 13)

            dve_residual(dve, 3, 12, "ple_post_g", last_tiles)
            dve_residual(dve, 3, 13, "ple_post_g")
            for n, (t, b) in enumerate(Y_ORDER):
                if y_emptied(n)[0] is y_dve:
                    dve.wait_ge(y_turned, n + 1)
                    dve.tensor_copy(y_rows[:, t, b * HALF:(b + 1) * HALF], PS[:, 4 + n % 4, :]).then_inc(y_dve, 1)

        @block.tensor
        def _(pe_):
            def product(u, bank, h, k):
                w = [x[:, slot_of(u), k * P:(k + 1) * P] for x in (w_hi, w_lo)]
                for s, (a, b) in enumerate(passes(w, [half(x, k, h) for x in (u_hi, u_lo)])):
                    mm = pe_.matmul(PS[:, bank, :], a, b, start=(k == 0 and s == 0), stop=(k == KC - 1 and s == 2))
                return mm

            def head_sum(g, hd):
                x = 4 * g + hd
                pe_.wait_ge(hsq_ready, x + 1)
                if hd == 0 and g == 3:
                    pe_.wait_ge(hrms_ready, 3)
                for t in range(4):
                    mm = pe_.matmul(PS[:, hsum_bank(g), 4 * hd + t:4 * hd + t + 1], h_sq[:, x % 2, t * P:(t + 1) * P],
                                    ones[:, 0:1], start=(hd == 0 and t == 0), stop=True, skip_group_check=True)
                mm.then_inc(hsq_used, 1)

            def head_row(g, hd):
                x = 4 * g + hd
                pe_.wait_ge(hdiag_ready, x + 1)
                if hrow_before(x) is not None:
                    pe_.wait_ge(hn_scaled, scaled_first(hrow_before(x)))
                pe_.matmul(PS[:, hrow_bank(x), :], ones[:, :], h_diag[:, x % 2, :], start=True, stop=True).then_inc(hrb_ready, 1)

            for g in range(2):
                for hd in range(HEADS):
                    head_sum(g, hd)
            for g in range(2):
                for hd in range(HEADS):
                    head_row(g, hd)

            for n, (s, h) in enumerate(PAIR_ORDER):
                u = U_OUT + 2 * s
                pe_.wait_ge(lo_ready, u + 2)
                last = n == len(PAIR_ORDER) - 1
                order = [(i, k) for i in range(2) for k in range(KC)] if last else [(i, k) for k in range(KC) for i in range(2)]
                for i, k in order:
                    r = 2 * n + i
                    if k == 0:
                        pe_.wait_ge(f_kept, R_OUT + r - 3)
                    if s == 0 and i == 0:
                        pe_.wait_ge(mlo_ready, 8 * h + k + 1)
                    mm = product(u + i, 4 + r % 4, h, k)
                    if k == KC - 1:
                        mm.then_inc(f_ready, 1)
                    if last and (i, k) == (0, 4):
                        pe_sum_up(pe_, 6)
                    if last and (i, k) == (1, 1):
                        pe_row(pe_, 6)
                    if n == 0 and i == 1 and 2 <= k < 6:
                        head_sum(2, k - 2)
                    if n == 1 and i == 1 and k < 4:
                        head_row(2, k)
                    if n == 1 and i == 1 and k >= 6:
                        head_sum(3, 2 * (k - 6))
                        head_sum(3, 2 * (k - 6) + 1)
                    if n == 2 and i == 1 and k < 4:
                        head_row(3, k)
            pe_between(pe_, 6)
            pe_gate_up(pe_, 1, 0, 0, 0, True)
            pe_gate_up(pe_, 1, 0, 0, 1, True)
            pe_sum_up(pe_, 9)
            pe_row(pe_, 9)
            for c in range(2):
                pe_gate_up(pe_, 1, 0, 1, c, True)
            pe_down(pe_, 1, 0, True)
            with pe_.Fori(1, LAST) as t:
                pe_ffn(pe_, 1, t, False)

            def turn_p(j):
                if j == 0:
                    pe_.wait_ge(p_loaded, 32)
                else:
                    pe_.wait_ge(p_kept, j)
                for t in (2 * j, 2 * j + 1):
                    for c in range(2):
                        at0 = HALF + (t % 2) * PLE + c * P
                        mm = pe_.transpose(PS[:, 3, ((t % 2) * 2 + c) * P:((t % 2) * 2 + c + 1) * P],
                                           p_place[:, 4 + t // 2, at0:at0 + P], ident[:, :])
                mm.then_inc(p_turned, 1)

            def after_tile(r):
                pe_early(pe_, 10, r)
                if r >= 9 and r % 2 == 1:
                    turn_p((r - 9) // 2)

            pe_ffn(pe_, 1, LAST, False, after_tile=after_tile)
            pe_sum_up(pe_, 11)
            pe_.wait_ge(p_kept, 4)
            pe_row(pe_, 11)

            def embed(x):
                (s, h), i = PAIR_ORDER[x // 2], x % 2
                m = 2 * s + i
                if x == 0:
                    pe_.wait_ge(p_lo, 4)
                if x == 3:
                    pe_.wait_ge(f_scaled, 16 * 2 + 16)
                for c in range(2):
                    w = [y[:, c, m * P:(m + 1) * P] for y in (w_hi, w_lo)]
                    for n, (a, b) in enumerate(passes(w, [half(y, c, h) for y in (h_hi, h_lo)])):
                        mm = pe_.matmul(PS[:, x % 4, :], a, b, start=(c == 0 and n == 0), stop=(c == 1 and n == 2))
                mm.then_inc(e_ready, 1)

            for n, (s, h) in enumerate(PAIR_ORDER):
                u = U_PLE + 2 + 2 * s
                pe_.wait_ge(lo_ready, u + 2)
                last = n == len(PAIR_ORDER) - 1
                order = [(i, k) for i in range(2) for k in range(KC)] if last else [(i, k) for k in range(KC) for i in range(2)]
                for i, k in order:
                    x = 2 * n + i
                    if k == 0:
                        if x >= 4:
                            pe_.wait_ge(t_ready, x - 3)
                        if last:
                            embed(x)
                    if s == 0 and i == 0:
                        pe_.wait_ge(ulo_ready, 16 * 3 + 8 * h + k + 1)
                    mm = product(u + i, 4 + x % 4, h, k)
                    if k == KC - 1:
                        mm.then_inc(f_ready, 1)
                    if last:
                        pe_.wait_ge(t_ready, 13 + i)
                        if (i, k) == (0, 5):
                            pe_sum_up(pe_, 12)
                        if (i, k) == (1, 2):
                            pe_row(pe_, 12)
                if not last:
                    embed(2 * n)
                    embed(2 * n + 1)
            pe_sum_up(pe_, 13)
            pe_row(pe_, 13)
            for n, (t, b) in enumerate(Y_ORDER):
                pe_.wait_ge(x_ready, 56 if n < 8 else 60 if n < 12 else 64)
                if n >= 4:
                    pe_.wait_ge(*y_emptied(n - 4))
                else:
                    pe_.wait_ge(t_ready, 16)
                for c in range(4):
                    mm = pe_.transpose(PS[:, 4 + n % 4, c * P:(c + 1) * P], xT[:, 4 * b + c, t * P:(t + 1) * P], ident[:, :])
                mm.then_inc(y_turned, 1)


_INS = ["x", "p", "ffn1_pre_g", "ffn1_post_g", "ffn1_w_gate", "ffn1_w_up", "ffn1_w_down", "mix_pre_g", "mix_post_g",
        "w_in", "cmp_k_pe", "cmp_k_w1", "cmp_k_w2", "cmp_v_pe", "cmp_v_w1", "cmp_v_w2", "nsa_out_g", "gla_gate_up",
        "gla_gate_bias", "gla_out_g", "w_out", "ffn2_pre_g", "ffn2_post_g", "ffn2_w_gate", "ffn2_w_up", "ffn2_w_down",
        "ple_proj", "ple_gate", "ple_post_g"]


def kernel(**inputs):
    import numpy as _np
    import concourse.bacc as _bacc
    from concourse import mybir as _mybir
    from concourse.bass_utils import run_bass_kernel_spmd as _run

    nc = _bacc.Bacc("TRN2", target_bir_lowering=False, num_devices=1, dynamic_dma_scratch_size=1024)
    arrays, aps = {}, {}
    for name in _INS:
        a = _np.ascontiguousarray(inputs[name])
        arrays[f"in_{name}_dram"] = a
        aps[name] = nc.dram_tensor(f"in_{name}_dram", a.shape, _mybir.dt.from_np(a.dtype), kind="ExternalInput").ap()
    out = nc.dram_tensor("out_0_dram", (1, SEQ, D), _mybir.dt.float32, kind="ExternalOutput").ap()
    build(nc, aps, out)
    r = _run(nc, [arrays], core_ids=[0])
    return r.results[0]["out_0_dram"]
```

```python
import concourse.bass as bass
from concourse import mybir
from concourse.alu_op_type import AluOpType as ALU

ACT = mybir.ActivationFunctionType
AX = mybir.AxisListType
F32 = mybir.dt.float32
F32R = mybir.dt.float32r
BF16 = mybir.dt.bfloat16

P = 128
SEQ = 1024
D = 1024
KC = D // P
HALF = 512
NT = SEQ // P
F = 2816
ITERS = F // (2 * P)
EPS = 1e-6
NEG = -1e30

HEADS = 4
DH = 128
CMP_BLOCK, CMP_STRIDE = 32, 16
N_CMP = (SEQ - CMP_BLOCK) // CMP_STRIDE + 1
CMPW = 64
WINDOW = 512
WT = WINDOW // P
SLC_BLOCK, SLC_TOPK = 64, 16
assert SLC_TOPK >= SEQ // SLC_BLOCK

GK, GV, RANK, CHUNK = 64, 128, 16, 64
PAIRS = 2
N_CHUNK = SEQ // CHUNK
GATE_NORM = 16.0
PLE = 256

IN_NAMES = ["q", "kc", "vc", "ks", "vs", "kw", "vw", "gate", "gq", "gk", "gv", "gdown", "gog"]
IN_SPLITS = [512, 128, 128, 128, 128, 128, 128, 12, 256, 256, 512, 16, 512]
COL = {n: sum(IN_SPLITS[:i]) for i, n in enumerate(IN_NAMES)}
GATES = 3 * HEADS
SMALL = GATES + RANK
VT = 2 * P

SLOTS, RAWS, AHEAD = 6, 3, 4
U_FFN = [0, 6 * ITERS + 22 + 8]
U_IN = 6 * ITERS
U_OUT = U_IN + 22
U_PLE = U_FFN[1] + 6 * ITERS
U_END = U_PLE + 2 + KC
assert all(u % SLOTS == 0 for u in U_FFN + [U_PLE])


def slot_of(u):
    return u % SLOTS if u < U_PLE + 2 else 2 + (u - U_PLE - 2) % (SLOTS - 2)


Q0 = [0, 4 * ITERS]
R0 = [0, 16 * ITERS + 16]
R_OUT = 16 * ITERS
R_G = R0[1] + 16 * ITERS

PAIR_ORDER = [(0, 0), (1, 0), (0, 1), (1, 1), (2, 0), (2, 1), (3, 0), (3, 1)]

IN_PAIRS = [(("q", 0), ("ks", 0)), (("q", 1), ("kw", 0)), (("q", 2), ("gk", 0)), (("q", 3), ("gk", 1)),
            (("gq", 0), ("kc", 0)), (("gq", 1), ("vc", 0)), (("gog", 0), ("gog", 1)), (("gog", 2), ("gog", 3))]
TOK_PAIRS = [(COL["vs"], COL["vw"]), (COL["gv"], COL["gv"] + P), (COL["gv"] + 2 * P, COL["gv"] + 3 * P)]
IN_ORDER = [(0, 0), (1, 0), (0, 1), (1, 1)] + [(p, h) for p in range(2, len(IN_PAIRS)) for h in range(2)]
V_SMALL = 4 * len(IN_PAIRS)
V_TOK = V_SMALL + 2
V_END = V_TOK + NT * len(TOK_PAIRS)


def tile_owner(v):
    if v < V_SMALL:
        (p, _), i = IN_ORDER[v // 2], v % 2
        return "act" if i == 0 or IN_PAIRS[p][0][0] == "gog" else "dve"
    return "act" if v % 2 == 0 else "dve"


def owner_rank(v):
    return sum(tile_owner(w) == tile_owner(v) for w in range(v + 1))


def v_bank(v):
    return (0, 2, 1, 3)[v] if v < 4 else v % 8


def passes(hi_lo_w, hi_lo_x):
    return ((hi_lo_w[0], hi_lo_x[0]), (hi_lo_w[0], hi_lo_x[1]), (hi_lo_w[1], hi_lo_x[0]))


VEC_ROWS = [("ffn1_pre_g", 8), ("ffn1_post_g", 8), ("mix_pre_g", 8), ("mix_post_g", 8), ("ffn2_pre_g", 8),
            ("ffn2_post_g", 8), ("ple_post_g", 8), ("nsa_out_g", 4), ("gla_out_g", 4), ("gla_gate_bias", 2)]
VEC_AT = {n: sum(c for _, c in VEC_ROWS[:i]) for i, (n, _) in enumerate(VEC_ROWS)}
NVEC = sum(c for _, c in VEC_ROWS)
HALVED = ("ffn1_post_g", "ffn2_post_g")


def build(nc, A, out):
    base = -(-nc.sbuf_base // 64) * 64

    def place(name, shape, dt, offset):
        return nc.alloc_sbuf_tensor_at(name, shape, dt, offset=offset)

    def size(shape, dt):
        n = 2 if dt == BF16 else 4
        for s in shape[1:]:
            n *= s
        return -(-n // 32) * 32

    class Region:

        def __init__(self, start, end):
            self.at, self.end = start, end

        def take(self, name, shape, dt=F32):
            t = place(name, shape, dt, self.at)
            self.at += size(shape, dt)
            assert self.at <= self.end, (name, self.at, self.end)
            return t

    const = Region(base, nc.sbuf_usable_end)
    ident = const.take("ident", [P, P])
    ones = const.take("ones", [P, P])
    identb = const.take("identb", [P, P], BF16)
    neg_future = const.take("neg_future", [P, P], BF16)
    neg_past = const.take("neg_past", [P, P], BF16)
    neg_cmp = const.take("neg_cmp", [P, NT, CMPW], BF16)
    cmp_valid = const.take("cmp_valid", [P, NT, CMPW])
    gla_causal = const.take("gla_causal", [P, P])
    vec_rows = const.take("vec_rows", [P, P])
    pe_rows = const.take("pe_rows", [2 * CMP_BLOCK, P])
    vec = const.take("vec", [P, NVEC])
    pe = const.take("pe", [P, 2 * CMP_BLOCK])
    rms = const.take("rms", [P, 2, 16])
    rstd = const.take("rstd", [P, 2, 16])
    eps = const.take("eps", [P, 1])
    w_raw = const.take("w_raw", [P, RAWS, KC * P])
    whi_at = const.at
    w_hi = const.take("w_hi", [P, SLOTS, KC * P], F32R)
    w_lo = const.take("w_lo", [P, SLOTS, KC * P], F32R)
    u_at = const.at
    u_hi = const.take("u_hi", [P, KC, SEQ], F32R)
    ulo_at = const.at
    u_lo = const.take("u_lo", [P, KC, SEQ], F32R)
    u_end = const.at
    stage_at, stage_end = const.at, nc.sbuf_usable_end

    ffn = Region(stage_at, stage_end)
    xT = ffn.take("xT", [P, KC, SEQ])
    fT = ffn.take("fT", [P, KC, SEQ])
    h_at = ffn.at
    h_hi = ffn.take("h_hi", [P, 2, SEQ], F32R)
    h_lo = ffn.take("h_lo", [P, 2, SEQ], F32R)
    sg = ffn.take("sg", [P, 2, HALF])
    h32 = ffn.take("h32", [P, 2, HALF])
    sq_sum = ffn.take("sq_sum", [P, HALF])
    u_first = place("u_first", [P, KC, HALF], F32, h_at)
    p_place = place("p_place", [P, KC, SEQ], F32, ulo_at)

    mix = Region(stage_at, stage_end)
    oT = mix.take("oT", [P, 2 * HEADS, SEQ])
    qT = mix.take("qT", [P, HEADS, SEQ])
    gq = mix.take("gq", [P, PAIRS, SEQ])
    gv_at = mix.at
    gv = mix.take("gv", [P, NT, HEADS * GV])
    ksT = mix.take("ksT", [P, SEQ])
    kwT = mix.take("kwT", [P, SEQ])
    vtok = mix.take("vtok", [P, NT, VT])
    kcT = mix.take("kcT", [P, CMPW])
    vc = mix.take("vc", [CMPW, P])
    gate = mix.take("gate", [P, NT, GATES])
    pre = Region(stage_at, stage_at + 4 * 2 * HEADS * SEQ)
    kcmp = pre.take("kcmp", [P, 2, SEQ])
    gk = pre.take("gk", [P, PAIRS, SEQ])
    gog_out = pre.take("gog_out", [P, 4, HALF])
    small_raw = pre.take("small_raw", [P, KC, SMALL])
    small_hi = pre.take("small_hi", [P, KC, SMALL], F32R)
    small_lo = pre.take("small_lo", [P, KC, SMALL], F32R)
    assert pre.at <= stage_at + 28 * 1024
    gla = Region(u_at, u_end)
    gx = gla.take("gx", [P, PAIRS, SEQ])
    gb = gla.take("gb", [P, PAIRS, SEQ])
    ge = gla.take("ge", [P, PAIRS, SEQ])
    kend = gla.take("kend", [P, NT, PAIRS * P])
    state = gla.take("state", [P, N_CHUNK, PAIRS, GV])
    at_sb = gla.take("at_sb", [P, 2, HEADS * P])
    scan_keep = gla.take("scan_keep", [P, SEQ])
    w1_late = gla.take("w1_late", [P, 2, 8, P])
    kv_a = place("kv_a", [P, 2, SEQ], F32, u_at + 8192 * 4)
    kv_b = place("kv_b", [P, 2, SEQ], F32, u_at + 8192 * 5)
    gla_small = Region(stage_at + 4 * HEADS * SEQ, stage_at + 8 * HEADS * SEQ)
    smallT = gla_small.take("smallT", [SMALL, SEQ])
    gup = gla_small.take("gup", [RANK, PAIRS * P])
    decay = gla_small.take("decay", [P, PAIRS, N_CHUNK])
    hid = gla_small.take("hid", [P, 2, CMPW])
    hid_rows = gla_small.take("hid_rows", [CMPW, 2, P])
    w2 = gla_small.take("w2", [P, 2, P])
    assert gla_small.at <= stage_at + 24 * 1024
    w1_early = place("w1_early", [P, 2, 8, P], F32, stage_at + 24 * 1024)
    w1 = [w1_early[:, 0], w1_early[:, 1], w1_late[:, 0], w1_late[:, 1]]
    PW = SEQ + WINDOW + P + CMPW
    att = Region(u_at, u_end)
    prob = att.take("prob", [P, 2, HEADS, PW])
    probT = att.take("probT", [P, 4, HALF])
    gog = place("gog", [P, HEADS, SEQ], F32, gv_at)
    mx_at = stage_at + 4 * (2 * HEADS * SEQ + HEADS * SEQ)
    small = Region(mx_at, mx_at + 8192)
    neg_max = small.take("neg_max", [P, 2, 3 * HEADS])
    row_sum = small.take("row_sum", [P, 2, 3 * HEADS])
    inv_sum = small.take("inv_sum", [P, 2, 3 * HEADS])
    p_scale = small.take("p_scale", [P, 2, 3 * HEADS])
    h_sq = place("h_sq", [P, 2, HALF], F32, mx_at + 4096)

    PS = nc.alloc_psum_tensor("PS", [P, 8, HALF], F32)

    y_rows = place("y_rows", [P, NT, D], F32, whi_at)

    x_spill = nc.dram_tensor("x_spill", [KC, P, SEQ], F32).ap()
    gog_spill = nc.dram_tensor("gog_spill", [HEADS, P, SEQ], F32).ap()

    def sem(name):
        return nc.alloc_semaphore(name)

    raw_loaded = [sem(f"raw_loaded{i}") for i in range(RAWS)]
    hi_ready, lo_ready = sem("hi_ready"), sem("lo_ready")
    x_loaded = [sem(f"x_loaded{i}") for i in range(4)]
    vec_loaded, masks_made, vec_turned, vec_kept = sem("vec_loaded"), sem("masks_made"), sem("vec_turned"), sem("vec_kept")
    xt_turned, xt_act, xt_dve = sem("xt_turned"), sem("xt_act"), sem("xt_dve")
    sq_ready, rms_ready, rstd_ready = sem("sq_ready"), sem("rms_ready"), sem("rstd_ready")
    sq_pooled, sq_summed, sums_ready = sem("sq_pooled"), sem("sq_summed"), sem("sums_ready")
    rows_squared, const_ready = sem("rows_squared"), sem("const_ready")
    rb_ready = sem("rb_ready")
    f_scaled, x_ready = sem("f_scaled"), sem("x_ready")
    u32_ready, uhi_ready, ulo_ready = sem("u32_ready"), sem("uhi_ready"), sem("ulo_ready")
    gu_ready, silu_done, h_done, hhi_ready, hlo_ready = sem("gu_ready"), sem("silu_done"), sem("h_done"), sem("hhi_ready"), sem("hlo_ready")
    f_ready, f_kept = sem("f_ready"), sem("f_kept")
    x_spilled, x_back = sem("x_spilled"), sem("x_back")
    v_ready, v_act, v_dve = sem("v_ready"), sem("v_act"), sem("v_dve")
    small_loaded, small_hi_ready, small_lo_ready = sem("small_loaded"), sem("small_hi_ready"), sem("small_lo_ready")
    gog_spilled = [sem(f"gog_spilled{i}") for i in range(4)]
    gog_back = sem("gog_back")
    gup_loaded, gates_turned, gpre_ready, gx_ready = sem("gup_loaded"), sem("gates_turned"), sem("gpre_ready"), sem("gx_ready")
    g_act, g_dve = sem("g_act"), sem("g_dve")
    w2_loaded = sem("w2_loaded")
    w1_loaded = [sem(f"w1_loaded{i}") for i in range(4)]
    q_zeroed = sem("q_zeroed")
    hid_silu, hid_turned = sem("hid_silu"), sem("hid_turned")
    w1_used, kv_biased, hid_kept, cmp_ready, cmp_kept = sem("w1_used"), sem("kv_biased"), sem("hid_kept"), sem("cmp_ready"), sem("cmp_kept")
    kend_turned, kend_kept = sem("kend_turned"), sem("kend_kept")
    outer_ready, state_ready = sem("outer_ready"), sem("state_ready")
    a_ready, a_masked, go_done, go_kept = sem("a_ready"), sem("a_masked"), sem("go_done"), sem("go_kept")
    s_ready, max_done, exp_done, p_scaled, r_ready = sem("s_ready"), sem("max_done"), sem("exp_done"), sem("p_scaled"), sem("r_ready")
    pt_ready, pt_act, pt_dve = sem("pt_ready"), sem("pt_act"), sem("pt_dve")
    o_kept, pv_done = sem("o_kept"), sem("pv_done")
    hsq_ready, hsq_used, hrms_ready, hrstd_ready, hrb_ready = (
        sem("hsq_ready"), sem("hsq_used"), sem("hrms_ready"), sem("hrstd_ready"), sem("hrb_ready"))
    hn_scaled, mhi_ready, mlo_ready = sem("hn_scaled"), sem("mhi_ready"), sem("mlo_ready")
    p_loaded, p_turned, p_kept, p_hi, p_lo = sem("p_loaded"), sem("p_turned"), sem("p_kept"), sem("p_hi"), sem("p_lo")
    e_ready = sem("e_ready")
    sig_done, t_ready = sem("sig_done"), sem("t_ready")
    y_turned, y_act, y_dve = sem("y_turned"), sem("y_act"), sem("y_dve")
    y_stored = sem("y_stored")

    def half(t, c, h):
        return t[:, c, h * HALF:(h + 1) * HALF]

    w_gate = [A["ffn1_w_gate"], A["ffn2_w_gate"]]
    w_up = [A["ffn1_w_up"], A["ffn2_w_up"]]
    w_down = [A["ffn1_w_down"], A["ffn2_w_down"]]

    def load_columns(sp, raw, w, col):
        return sp.dma_start(w_raw[:, raw, :].rearrange("p (k f) -> p k f", k=KC),
                            w[0].rearrange("(k p) f -> p k f", p=P)[:, :, bass.ds(col, P)])

    def load_rows(sp, raw, w, row):
        return sp.dma_start(w_raw[:, raw, :], w[0][bass.ds(row, P), :])

    def sp_load(sp, u):
        if u >= RAWS:
            sp.wait_ge(lo_ready, u - RAWS + 1)
        raw = u % RAWS
        for n in range(2):
            if U_FFN[n] <= u < U_FFN[n] + 6 * ITERS:
                t, j = divmod(u - U_FFN[n], 6)
                if j < 4:
                    ins = load_columns(sp, raw, (w_gate, w_up)[j % 2][n], (2 * t + j // 2) * P)
                else:
                    ins = load_rows(sp, raw, w_down[n], (2 * t + j - 4) * P)
        if U_IN <= u < U_OUT:
            p, i = divmod(u - U_IN, 2)
            if p < len(IN_PAIRS):
                name, m = IN_PAIRS[p][i]
                col = COL[name] + m * P
            else:
                col = TOK_PAIRS[p - len(IN_PAIRS)][i]
            ins = load_columns(sp, raw, A["w_in"], col)
        if U_OUT <= u < U_FFN[1]:
            ins = load_columns(sp, raw, A["w_out"], (u - U_OUT) * P)
        if U_PLE <= u < U_PLE + 2:
            ins = load_rows(sp, raw, A["ple_proj"], (u - U_PLE) * P)
        if u >= U_PLE + 2:
            ins = load_columns(sp, raw, A["ple_gate"], (u - U_PLE - 2) * P)
        ins.then_inc(raw_loaded[raw], 16)

    def sp_ffn(sp, n, t, first):
        for j in range(first, 6):
            sp.wait_ge(lo_ready, t * 6 + (U_FFN[n] + j - RAWS + 1))
            if j < 4:
                ins = load_columns(sp, j % RAWS, (w_gate, w_up)[j % 2][n], t * (2 * P) + (j // 2) * P)
            else:
                ins = load_rows(sp, j % RAWS, w_down[n], t * (2 * P) + (j - 4) * P)
            ins.then_inc(raw_loaded[j % RAWS], 16)

    def act_round(act, u, free=None):
        if free is not None:
            act.wait_ge(*free)
        act.wait_ge(raw_loaded[u % RAWS], (u // RAWS + 1) * 16)
        act.activation(w_hi[:, slot_of(u), :], w_raw[:, u % RAWS, :], ACT.Copy).then_inc(hi_ready, 1)

    def dve_rest(dve, u, j=None):
        slot, raw = (slot_of(u), u % RAWS) if j is None else (j % SLOTS, j % RAWS)
        dve.wait_ge(hi_ready, u + 1)
        dve.tensor_tensor(w_lo[:, slot, :], w_raw[:, raw, :], w_hi[:, slot, :].bitcast(F32),
                          ALU.subtract).then_inc(lo_ready, 1)

    SUM_BANK = [None, None, 0, 1, 0, 5, 0, 1, 0, 5, 0, 1, 0, 1]
    ROW_BANK = [3, 6, 2, 4, 3, 6, 2, 4, 3, 6, 2, 3, 0, 1]

    def squares(k, i):
        if k in URGENT:
            return u_first[:, i % KC, :]
        return sg[:, i % 2, :] if k < 12 else w_raw[:, 0, (i % 2) * HALF:(i % 2 + 1) * HALF]

    SQUARES = [(k, c) for k in range(2, 14) for c in range(KC)]
    URGENT = (4, 8)

    def adds(k):
        return sum(KC // 2 - 1 if x in URGENT else KC - 1 for x in range(2, k))

    def act_square(act, k, c, src, ready):
        i = SQUARES.index((k, c))
        act.wait_ge(*ready(k % 2, c))
        if k not in URGENT and i >= 2:
            last = c - 2 if c >= 2 else c + KC - 2
            norm = k if c >= 2 else k - 2 if k - 1 in URGENT else k - 1
            act.wait_ge(sq_pooled, adds(norm) + max(1, last))
        act.activation(squares(k, i), half(src, c, k % 2), ACT.Square).then_inc(sq_ready, 1)

    def act_sqrt(act, k):
        act.wait_ge(sums_ready, k - 1)
        act.wait_ge(rstd_ready, k - 1)
        act.activation(rms[:, k % 2, 0:4], PS[:, SUM_BANK[k], 0:4], ACT.Sqrt, scale=1.0 / D, bias=eps[:, 0:1])\
           .then_inc(rms_ready, 1)

    def act_norm(act, k, src, ready):
        for c in range(KC):
            act_square(act, k, c, src, ready)
        act_sqrt(act, k)

    def pool_norm(pool, k):
        if k in URGENT:
            for n, c in enumerate(range(2, KC, 2)):
                pool.wait_ge(sq_ready, SQUARES.index((k, c)) + 1)
                if n > 0:
                    pool.wait_ge(sq_pooled, adds(k) + n)
                pool.tensor_tensor(u_first[:, 0, :], u_first[:, 0, :], u_first[:, c, :], ALU.add).then_inc(sq_pooled, 1)
            return
        for c in range(1, KC):
            i = SQUARES.index((k, c))
            pool.wait_ge(sq_ready, i + 1)
            if c == 1:
                if k > 2:
                    pool.wait_ge(sums_ready, k - 2)
                pool.tensor_tensor(sq_sum[:, :], squares(k, i - 1), squares(k, i), ALU.add).then_inc(sq_pooled, 1)
            else:
                pool.wait_ge(sq_pooled, adds(k) + c - 1)
                pool.tensor_tensor(sq_sum[:, :], sq_sum[:, :], squares(k, i), ALU.add).then_inc(sq_pooled, 1)

    def dve_sum(dve, k):
        counted = KC // 2 * URGENT.index(k)
        for n, c in enumerate(range(3, KC, 2)):
            dve.wait_ge(sq_ready, SQUARES.index((k, c)) + 1)
            if n > 0:
                dve.wait_ge(sq_summed, counted + n)
            dve.tensor_tensor(u_first[:, 1, :], u_first[:, 1, :], u_first[:, c, :], ALU.add).then_inc(sq_summed, 1)
        dve.wait_ge(sq_summed, counted + KC // 2 - 1)
        dve.wait_ge(sq_pooled, adds(k + 1))
        dve.tensor_tensor(u_first[:, 1, :], u_first[:, 1, :], u_first[:, 0, :], ALU.add).then_inc(sq_summed, 1)

    def pe_sum_up(pe_, k):
        if k in URGENT:
            pe_.wait_ge(sq_summed, KC // 2 * (URGENT.index(k) + 1))
            total = u_first[:, 1, :]
        else:
            pe_.wait_ge(sq_pooled, adds(k + 1))
            total = sq_sum[:, :]
        for t in range(4):
            mm = pe_.matmul(PS[:, SUM_BANK[k], t:t + 1], total[:, t * P:(t + 1) * P], ones[:, 0:1],
                            start=(t == 0), stop=True, skip_group_check=True)
        mm.then_inc(sums_ready, 1)

    def spread(pe_, bank, column):
        for t in range(4):
            mm = pe_.matmul(PS[:, bank, t * P:(t + 1) * P], column(t).to_broadcast([P, P]), ident[:, :], start=True, stop=True)
        return mm

    def pe_row(pe_, k):
        pe_.wait_ge(rstd_ready, k + 1)
        spread(pe_, ROW_BANK[k], lambda t: rstd[:, k % 2, t:t + 1]).then_inc(rb_ready, 1)

    def pe_between(pe_, k):
        pe_sum_up(pe_, k + 1)
        pe_.wait_ge(f_kept, R_OUT if k == 2 else R_OUT + 16)
        pe_row(pe_, k + 1)
        pe_sum_up(pe_, k + 2)
        pe_row(pe_, k + 2)

    def dve_norm(dve, k):
        dve.wait_ge(rms_ready, k + 1)
        dve.reciprocal(rstd[:, k % 2, 0:4], rms[:, k % 2, 0:4]).then_inc(rstd_ready, 1)

    def dve_residual(dve, pi, k, gain, before=None, rest=None, steps=range(KC + 2)):
        h = k % 2
        for c in steps:
            if before is not None:
                before(c)
            if c == 0:
                dve.wait_ge(rb_ready, k + 1)
            if c < KC:
                g = vec[:, VEC_AT[gain] + c:VEC_AT[gain] + c + 1]
                dve.scalar_tensor_tensor(half(fT, c, h), half(fT, c, h), g, PS[:, ROW_BANK[k], :], ALU.mult, ALU.mult)\
                   .then_inc(f_scaled, 1)
            if 1 <= c <= KC:
                dve.wait_ge(f_scaled, 16 * pi + 8 * h + c)
                dve.tensor_tensor(half(xT, c - 1, h), half(xT, c - 1, h), half(fT, c - 1, h), ALU.add).then_inc(x_ready, 1)
            if rest is not None and c >= 2:
                rest(c - 2)

    def dve_apply(dve, a, k, gain, dst=None):
        h = k % 2
        if dst is None:
            dst = lambda c: half(fT, c, h)
        dve.wait_ge(rb_ready, k + 1)
        for c in range(KC + 1):
            if c < KC:
                g = vec[:, VEC_AT[gain] + c:VEC_AT[gain] + c + 1]
                if a > 0:
                    dve.wait_ge(x_ready, 16 * (a - 1) + 8 * h + c + 1)
                dve.scalar_tensor_tensor(dst(c), half(xT, c, h), g, PS[:, ROW_BANK[k], :], ALU.mult, ALU.mult)\
                   .then_inc(u32_ready, 1)
            if c > 0:
                dve_lo(dve, a, h, c - 1, dst(c - 1))

    def dve_lo(dve, a, h, c, src):
        dve.wait_ge(uhi_ready, 16 * a + 8 * h + c + 1)
        dve.tensor_tensor(half(u_lo, c, h), src, half(u_hi, c, h).bitcast(F32), ALU.subtract).then_inc(ulo_ready, 1)

    def act_hi(act, h, c, src, ready):
        act.wait_ge(*ready)
        act.activation(half(u_hi, c, h), src, ACT.Copy).then_inc(uhi_ready, 1)

    def act_hi_half(act, h, src, ready):
        for c in range(KC):
            act_hi(act, h, c, half(src, c, h), ready(h, c))

    def pe_gate_up(pe_, n, t, h, c, first, after_step=None):
        q = 2 * h + c
        if not (first and n == 0 and q < 2):
            pe_.wait_ge(h_done, t * 4 + (Q0[n] + q - 1))
        if h == 0:
            pe_.wait_ge(lo_ready, t * 6 + (U_FFN[n] + 2 * c + 2))
        order = [(k, i) for k in range(KC) for i in range(2)] if first else [(k, i) for i in range(2) for k in range(KC)]
        for k, i in order:
            if first and c == 0 and i == 0:
                pe_.wait_ge(ulo_ready, 16 * 2 * n + 8 * h + k + 1)
            w = [x[:, 2 * c + i, k * P:(k + 1) * P] for x in (w_hi, w_lo)]
            for s, (a, b) in enumerate(passes(w, [half(x, k, h) for x in (u_hi, u_lo)])):
                mm = pe_.matmul(PS[:, 2 * i + c, :], a, b, start=(k == 0 and s == 0), stop=(k == KC - 1 and s == 2))
            if k == KC - 1:
                mm.then_inc(gu_ready, 1)
            if after_step is not None and i == 1:
                after_step(k)

    def pe_down(pe_, n, t, first, after_tile=None):
        pe_.wait_ge(lo_ready, t * 6 + (U_FFN[n] + 6))
        for h in range(2):
            pe_.wait_ge(hlo_ready, t * 4 + (Q0[n] + 2 * h + 2))
            for m in range(KC):
                r = 8 * h + m
                if not (first and n == 0 and r < 4):
                    pe_.wait_ge(f_kept, t * 16 + (R0[n] + r - 3))
                for c in range(2):
                    w = [x[:, 4 + c, m * P:(m + 1) * P] for x in (w_hi, w_lo)]
                    for s, (a, b) in enumerate(passes(w, [half(x, c, h) for x in (h_hi, h_lo)])):
                        mm = pe_.matmul(PS[:, 4 + r % 4, :], a, b, start=(c == 0 and s == 0), stop=(c == 1 and s == 2))
                mm.then_inc(f_ready, 1)
                if after_tile is not None:
                    after_tile(r)

    def pe_ffn(pe_, n, t, first, after_second=None, after_tile=None):
        for h in range(2):
            for c in range(2):
                pe_gate_up(pe_, n, t, h, c, first, after_second if (h, c) == (0, 1) else None)
        pe_down(pe_, n, t, first, after_tile)

    def act_silu(act, n, t, q, first):
        act.wait_ge(gu_ready, t * 8 + (2 * (Q0[n] + q) + 1))
        if not (first and n == 0 and q < 2):
            act.wait_ge(h_done, t * 4 + (Q0[n] + q - 1))
        act.activation(sg[:, q % 2, :], PS[:, q % 2, :], ACT.Silu).then_inc(silu_done, 1)

    def act_ffn(act, n, t, first):
        for c in range(3):
            free = [(f_ready, t * 16 + R0[n]), (gu_ready, t * 8 + (2 * Q0[n] + 6)), (gu_ready, t * 8 + (2 * Q0[n] + 8))][c]
            if first and n == 0 and c == 0:
                free = None
            for i in range(2):
                j = 2 * c + i + AHEAD
                landed = t * 32 + ((U_FFN[n] + j) // RAWS + 1) * 16
                if free is not None:
                    act.wait_ge(*free)
                act.wait_ge(raw_loaded[j % RAWS], landed)
                act.activation(w_hi[:, j % SLOTS, :], w_raw[:, j % RAWS, :], ACT.Copy).then_inc(hi_ready, 1)
            for q in ((0, 1, 2), (3,), ())[c]:
                if not (first and q == 0):
                    act_silu(act, n, t, q, first)

    def dve_h(dve, n, t, q, first):
        h, c = divmod(q, 2)
        dve.wait_ge(silu_done, t * 4 + (Q0[n] + q + 1))
        dve.wait_ge(gu_ready, t * 8 + (2 * (Q0[n] + q) + 2))
        if not (first and n == 0 and q < 2):
            dve.wait_ge(hlo_ready, t * 4 + (Q0[n] + q - 1))
        dve.tensor_tensor(h32[:, c, :], sg[:, c, :], PS[:, 2 + c, :], ALU.mult).then_inc(h_done, 1)
        dve.wait_ge(h_done, t * 4 + (Q0[n] + q + 1))
        if not (first and n == 0):
            dve.wait_ge(f_ready, t * 16 + (R0[n] - 16 + 8 * (h + 1)))
        dve.tensor_copy(half(h_hi, c, h), h32[:, c, :]).then_inc(hhi_ready, 1)
        dve.wait_ge(hhi_ready, t * 4 + (Q0[n] + q + 1))
        dve.tensor_tensor(half(h_lo, c, h), h32[:, c, :], half(h_hi, c, h).bitcast(F32), ALU.subtract)\
           .then_inc(hlo_ready, 1)

    def dve_keep(dve, n, t, r, first):
        m, h = r % 8, r // 8
        dve.wait_ge(f_ready, t * 16 + (R0[n] + r + 1))
        if first:
            dve.tensor_copy(half(fT, m, h), PS[:, 4 + r % 4, :]).then_inc(f_kept, 1)
        else:
            dve.wait_ge(f_kept, t * 16 + (R0[n] + r - 15))
            dve.tensor_tensor(half(fT, m, h), half(fT, m, h), PS[:, 4 + r % 4, :], ALU.add).then_inc(f_kept, 1)

    def dve_ffn(dve, n, t, first, tiles=16):
        for c in range(3):
            for i in range(2):
                j = 2 * c + i + AHEAD
                dve_rest(dve, t * 6 + (U_FFN[n] + j), j)
            for q in ((0, 1, 2), (3,), ())[c]:
                if not (first and q == 0):
                    dve_h(dve, n, t, q, first)
        for r in range(tiles):
            dve_keep(dve, n, t, r, first)

    LAST = ITERS - 1

    def pe_early(pe_, k, r):
        if r == 11:
            pe_sum_up(pe_, k)
        if r == 13:
            pe_row(pe_, k)

    def act_cross(act, k, pi, f_at, between=None):
        act_norm(act, k, fT, f_at)
        for c in range(KC):
            act_square(act, k + 1, c, fT, f_at)
        act.wait_ge(f_ready, R_OUT if k == 2 else R_OUT + 16)
        for c in range(KC):
            if c == 5:
                act_sqrt(act, k + 1)
            act_square(act, k + 2, c, xT, x_done(pi))
        act_sqrt(act, k + 2)
        act_hi_half(act, 0, fT, u32_done(pi + 1))
        act_norm(act, k + 3, xT, x_done(pi))
        if between is not None:
            between()
        act_hi_half(act, 1, fT, u32_done(pi + 1))

    def dve_cross(dve, k, pi, post, nxt, before, between=None):
        def first_half(c):
            before(c)
            if c == 7:
                dve_norm(dve, k + 1)

        dve_residual(dve, pi, k, post, first_half)
        dve_sum(dve, k + 2)
        dve_residual(dve, pi, k + 1, post, steps=range(2))
        dve_norm(dve, k + 2)
        dve_apply(dve, pi + 1, k + 2, nxt)
        dve_residual(dve, pi, k + 1, post, steps=range(2, KC + 1))
        dve_norm(dve, k + 3)
        if between is not None:
            between()
        dve_apply(dve, pi + 1, k + 3, nxt)

    def dve_ffn_last(dve, n, k):
        dve_ffn(dve, n, LAST, False, tiles=12)
        dve_norm(dve, k)
        dve_keep(dve, n, LAST, 12, False)
        dve_keep(dve, n, LAST, 13, False)

    def f_done(n):
        return lambda h, c: (f_kept, R0[n] + 16 * (ITERS - 1) + 8 * h + c + 1)

    def x_done(pi):
        return lambda h, c: (x_ready, 16 * pi + 8 * h + c + 1)

    def u32_done(a):
        return lambda h, c: (u32_ready, 16 * a + 8 * h + c + 1)

    def fm_target(name, m, h):
        if name == "q":
            return half(qT, m, h), float(DH) ** -0.5
        if name == "gq":
            return half(gq, m, h), float(GK) ** -0.5
        if name == "ks":
            return ksT[:, h * HALF:(h + 1) * HALF], 1.0
        if name == "kw":
            return kwT[:, h * HALF:(h + 1) * HALF], 1.0
        if name == "gk":
            return half(gk, m, h), 1.0
        return half(kcmp, "kc vc".split().index(name), h), 1.0

    def in_free(p):
        if p == 0:
            return f_ready, R_OUT
        if p == 1:
            return v_ready, 2 * (IN_ORDER.index((0, 1)) + 1)
        return v_ready, 4 * p if p <= len(IN_PAIRS) else V_TOK + NT * (p - len(IN_PAIRS))

    def small_tile(h):
        return smallT[:, h * HALF:(h + 1) * HALF], PS[0:SMALL, (V_SMALL + h) % 8, :]

    def in_tiles(p):
        lo, hi = [(0, 6), (6, 8)][p] if p < 2 else (4 * p, 4 * p + 4)
        return [(v,) + IN_PAIRS[IN_ORDER[v // 2][0]][v % 2] + (IN_ORDER[v // 2][1],) for v in range(lo, hi)]

    W1 = [A["cmp_k_w1"][0], A["cmp_v_w1"][0]]
    NW1 = CMP_BLOCK // 8

    def load_w1(sp, i):
        n, l0 = i // NW1, (i % NW1) * 8
        if i >= 4:
            sp.wait_ge(w1_used, i - 3)
        sp.dma_start(w1[i % 4], W1[n][l0:l0 + 8].rearrange("l d e -> d l e")).then_inc(w1_loaded[i % 4], 16)

    with nc.Block() as block:
        @block.sync
        def _(sp):
            x_rows = A["x"][0].rearrange("(t p) d -> p t d", p=P)

            def load_x(i):
                sp.dma_start(fT[:, 2 * i:2 * i + 2, :], x_rows[:, 2 * i:2 * i + 2, :]).then_inc(x_loaded[i], 16)

            load_x(0)
            load_x(1)
            for name, rows in VEC_ROWS:
                src = A[name].rearrange("l (c p) -> (l c) p", p=P) if len(A[name].shape) == 2 \
                    else A[name].rearrange("l c p -> (l c) p")
                sp.dma_start(vec_rows[VEC_AT[name]:VEC_AT[name] + rows, :], src).then_inc(vec_loaded, 16)
            for i, name in enumerate(("cmp_k_pe", "cmp_v_pe")):
                sp.dma_start(pe_rows[i * CMP_BLOCK:(i + 1) * CMP_BLOCK, :], A[name][0]).then_inc(vec_loaded, 16)
            sp_load(sp, 0)
            sp_load(sp, 1)
            load_x(2)
            load_x(3)
            for u in range(2, 6):
                sp_load(sp, u)
            with sp.Fori(1, ITERS) as t:
                sp_ffn(sp, 0, t, 0)
            for u in range(U_IN, U_IN + AHEAD + RAWS):
                sp_load(sp, u)
            for c in range(KC):
                sp.wait_ge(x_ready, 8 + c + 1)
                sp.dma_start(x_spill[c], xT[:, c, :]).then_inc(x_spilled, 16)
            for u in range(U_IN + AHEAD + RAWS, U_OUT + AHEAD + RAWS):
                sp_load(sp, u)
                if u == U_OUT:
                    sp.wait_ge(v_ready, V_TOK + NT)
                    load_w1(sp, 1)
                    load_w1(sp, 0)

        @block.gpsimd
        def _(pool):
            pool.memset(ident[:, :], 0.0).then_inc(masks_made, 1)
            pool.memset(identb[:, :], 0.0).then_inc(masks_made, 1)
            pool.memset(neg_future[:, :], 0.0).then_inc(masks_made, 1)
            pool.memset(neg_past[:, :], 0.0).then_inc(masks_made, 1)
            pool.memset(neg_cmp[:, :, :], 0.0).then_inc(masks_made, 1)
            pool.memset(cmp_valid[:, :, :], 1.0).then_inc(masks_made, 1)
            pool.memset(gla_causal[:, :], 1.0).then_inc(masks_made, 1)
            pool.wait_ge(masks_made, 7)
            for m in (ident, identb):
                pool.affine_select(out=m[:, :], in_=m[:, :], compare_op=ALU.not_equal, fill=1.0, base=0,
                                   pattern=[[-1, P]], channel_multiplier=1).then_inc(masks_made, 1)
            pool.affine_select(out=neg_future[:, :], in_=neg_future[:, :], compare_op=ALU.is_ge, fill=NEG, base=0,
                               pattern=[[-1, P]], channel_multiplier=1).then_inc(masks_made, 1)
            pool.affine_select(out=neg_past[:, :], in_=neg_past[:, :], compare_op=ALU.is_gt, fill=NEG, base=0,
                               pattern=[[1, P]], channel_multiplier=-1).then_inc(masks_made, 1)
            for m, fill in ((neg_cmp, NEG), (cmp_valid, 0.0)):
                pool.affine_select(out=m[:, :, :], in_=m[:, :, :], compare_op=ALU.is_ge, fill=fill,
                                   base=-(CMP_BLOCK - 1), pattern=[[P, NT], [-CMP_STRIDE, CMPW]],
                                   channel_multiplier=1).then_inc(masks_made, 1)
            pool.affine_select(out=gla_causal[:, :], in_=gla_causal[:, :], compare_op=ALU.is_ge, fill=0.0, base=0,
                               pattern=[[1, P]], channel_multiplier=-1).then_inc(masks_made, 1)
            pool.wait_ge(masks_made, 14)
            pool.memset(gla_causal[0:CHUNK, CHUNK:P], 0.0).then_inc(masks_made, 1)
            for k in range(2, 6):
                pool_norm(pool, k)

        @block.scalar
        def _(act):
            row = sg[:, :, :].rearrange("p a b -> p (a b)")

            def row_norm(h):
                for t in range(4):
                    i = 4 * h + t
                    act.wait_ge(x_loaded[i // 2], 16)
                    if i > 0:
                        act.wait_ge(rows_squared, i)
                    act.activation(row, fT[:, i, :], ACT.Square, accum_out=rms[:, h, 4 + t:5 + t]).then_inc(rows_squared, 1)
                act.wait_ge(rows_squared, 4 * (h + 1))
                act.wait_ge(const_ready, 2)
                act.activation(rms[:, h, 0:4], rms[:, h, 4:8], ACT.Sqrt, scale=1.0 / D, bias=eps[:, 0:1]).then_inc(rms_ready, 1)

            def empty_turned(h):
                for c in range(0, KC, 2):
                    r = KC * h + c
                    act.wait_ge(xt_turned, r + 1)
                    act.activation(half(xT, c, h), PS[:, 4 + r % 4, :], ACT.Copy).then_inc(xt_act, 1)

            row_norm(0)
            empty_turned(0)
            for u in range(2):
                act_round(act, u)
            for c in range(KC):
                act_hi(act, 0, c, u_first[:, c, :], (u32_ready, c + 1))
            for u in range(2, AHEAD):
                act_round(act, u)
            empty_turned(1)
            row_norm(1)
            act_silu(act, 0, 0, 0, True)
            act_hi_half(act, 1, fT, u32_done(0))
            act_ffn(act, 0, 0, True)
            with act.Fori(1, ITERS) as t:
                act_ffn(act, 0, t, False)
            act_cross(act, 2, 0, f_done(0))

            w_in_k = A["w_in"][0].rearrange("(k p) f -> p k f", p=P)
            for p in range(len(IN_PAIRS) + len(TOK_PAIRS)):
                for i in range(2):
                    u = U_IN + 2 * p + i + AHEAD
                    act_round(act, u, in_free(p))
                if p == 0:
                    act.wait_ge(ulo_ready, 32)
                if p == 2:
                    act.wait_ge(x_spilled, 16 * KC)
                    act.dma_start(small_raw[:, :, 0:RANK], w_in_k[:, :, COL["gdown"]:COL["gdown"] + RANK]).then_inc(small_loaded, 16)
                    act.dma_start(small_raw[:, :, RANK:SMALL], w_in_k[:, :, COL["gate"]:COL["gate"] + GATES]).then_inc(small_loaded, 16)
                if p == 6:
                    act.wait_ge(small_loaded, 32)
                    act.activation(small_hi[:, :, :], small_raw[:, :, :], ACT.Copy).then_inc(small_hi_ready, 1)
                if p < len(IN_PAIRS):
                    for v, name, m, h in in_tiles(p):
                        if tile_owner(v) != "act":
                            continue
                        act.wait_ge(v_ready, v + 1)
                        if name == "gog":
                            g = v % 4
                            if m >= 2:
                                act.wait_ge(gog_spilled[g], 16)
                            act.activation(gog_out[:, g, :], PS[:, v_bank(v), :], ACT.Silu).then_inc(v_act, 1)
                            act.wait_ge(v_act, owner_rank(v))
                            act.dma_start(gog_spill[m, :, h * HALF:(h + 1) * HALF], gog_out[:, g, :])\
                               .then_inc(gog_spilled[g], 16)
                        else:
                            dst, scale = fm_target(name, m, h)
                            act.activation(dst, PS[:, v_bank(v), :], ACT.Copy, scale=scale).then_inc(v_act, 1)
                else:
                    n = p - len(IN_PAIRS)
                    if n == 0:
                        for g in range(4):
                            act.wait_ge(gog_spilled[g], 32)
                        act.wait_ge(v_ready, V_SMALL + 1)
                        act.activation(*small_tile(0), ACT.Copy).then_inc(v_act, 1)
                    for t in range(0, NT, 2):
                        v = V_TOK + NT * n + t
                        act.wait_ge(v_ready, v + 1)
                        dst, w = (vtok[:, t, :], VT) if n == 0 else (gv[:, t, (n - 1) * 2 * P:n * 2 * P], 2 * P)
                        act.activation(dst, PS[:, v % 8, 0:w], ACT.Copy).then_inc(v_act, 1)
        @block.vector
        def _(dve):
            dve.memset(ones[:, :], 1.0).then_inc(const_ready, 1)
            dve.memset(eps[:, :], EPS).then_inc(const_ready, 1)
            dve.wait_ge(vec_turned, 1)
            dve.tensor_copy(vec[:, :], PS[:, 0, 0:NVEC]).then_inc(vec_kept, 1)
            dve.wait_ge(vec_turned, 2)
            dve.tensor_copy(pe[:, :], PS[:, 1, 0:2 * CMP_BLOCK]).then_inc(vec_kept, 1)
            dve.wait_ge(vec_kept, 1)
            for name in HALVED:
                g = vec[:, VEC_AT[name]:VEC_AT[name] + KC]
                dve.tensor_scalar(g, g, 0.5, None, ALU.mult).then_inc(vec_kept, 1)

            def empty_turned(h):
                for c in range(1, KC, 2):
                    r = KC * h + c
                    dve.wait_ge(xt_turned, r + 1)
                    dve.tensor_copy(half(xT, c, h), PS[:, 4 + r % 4, :]).then_inc(xt_dve, 1)

            empty_turned(0)
            dve_norm(dve, 0)
            for u in range(2):
                dve_rest(dve, u)
            dve.wait_ge(vec_kept, 2 + len(HALVED))
            dve.wait_ge(xt_act, 4)
            dve.wait_ge(xt_dve, 4)
            dve_apply(dve, 0, 0, "ffn1_pre_g", lambda c: u_first[:, c, :])
            for u in range(2, AHEAD):
                dve_rest(dve, u)
            empty_turned(1)
            dve_norm(dve, 1)
            dve.wait_ge(xt_act, 8)
            dve.wait_ge(xt_dve, 8)
            dve_h(dve, 0, 0, 0, True)
            dve_apply(dve, 0, 1, "ffn1_pre_g")
            dve_ffn(dve, 0, 0, True)
            with dve.Fori(1, LAST) as t:
                dve_ffn(dve, 0, t, False)
            dve_ffn_last(dve, 0, 2)
            dve_cross(dve, 2, 0, "ffn1_post_g", "mix_pre_g",
                      lambda c: dve_keep(dve, 0, LAST, 14 + c, False) if c < 2 else None)

            for p in range(len(IN_PAIRS) + len(TOK_PAIRS)):
                for i in range(2):
                    u = U_IN + 2 * p + i + AHEAD
                    dve_rest(dve, u)
                if p == 0:
                    dve.wait_ge(ulo_ready, 32)
                if p == 2:
                    dve.wait_ge(x_spilled, 16 * KC)
                if p == 6:
                    dve.wait_ge(small_hi_ready, 1)
                    dve.tensor_tensor(small_lo[:, :, :], small_raw[:, :, :], small_hi[:, :, :].bitcast(F32), ALU.subtract)\
                       .then_inc(small_lo_ready, 1)
                if p < len(IN_PAIRS):
                    for v, name, m, h in in_tiles(p):
                        if tile_owner(v) != "dve":
                            continue
                        dve.wait_ge(v_ready, v + 1)
                        dst, _scale = fm_target(name, m, h)
                        dve.tensor_copy(dst, PS[:, v_bank(v), :]).then_inc(v_dve, 1)
                else:
                    n = p - len(IN_PAIRS)
                    if n == 0:
                        for g in range(4):
                            dve.wait_ge(gog_spilled[g], 32)
                        dve.wait_ge(v_ready, V_SMALL + 2)
                        dve.tensor_copy(*small_tile(1)).then_inc(v_dve, 1)
                    for t in range(1, NT, 2):
                        v = V_TOK + NT * n + t
                        dve.wait_ge(v_ready, v + 1)
                        dst, w = (vtok[:, t, :], VT) if n == 0 else (gv[:, t, (n - 1) * 2 * P:n * 2 * P], 2 * P)
                        dve.tensor_copy(dst, PS[:, v % 8, 0:w]).then_inc(v_dve, 1)

        @block.tensor
        def _(pe_):
            def turn_x(h, c):
                r = KC * h + c
                if c == 0:
                    pe_.wait_ge(x_loaded[2 * h], 16)
                    pe_.wait_ge(x_loaded[2 * h + 1], 16)
                if r >= 4:
                    pe_.wait_ge((xt_act, xt_dve)[r % 2], (r - 4) // 2 + 1)
                for t in range(4):
                    mm = pe_.transpose(PS[:, 4 + r % 4, t * P:(t + 1) * P], fT[:, 4 * h + t, c * P:(c + 1) * P], ident[:, :])
                mm.then_inc(xt_turned, 1)

            def second_half(k):
                if k == 4:
                    pe_.wait_ge(xt_act, 8)
                    pe_row(pe_, 1)

            pe_.wait_ge(masks_made, 8)
            pe_.wait_ge(vec_loaded, 16 * (len(VEC_ROWS) + 2))
            pe_.transpose(PS[:, 0, 0:NVEC], vec_rows[0:NVEC, :], ident[0:NVEC, 0:NVEC]).then_inc(vec_turned, 1)
            pe_.transpose(PS[:, 1, 0:2 * CMP_BLOCK], pe_rows[:, :], ident[0:2 * CMP_BLOCK, 0:2 * CMP_BLOCK]).then_inc(vec_turned, 1)
            for c in range(KC):
                turn_x(0, c)
            pe_.wait_ge(const_ready, 1)
            pe_row(pe_, 0)
            pe_.wait_ge(vec_kept, 2)
            pe_gate_up(pe_, 0, 0, 0, 0, True)
            for c in range(KC):
                turn_x(1, c)
            pe_gate_up(pe_, 0, 0, 0, 1, True, second_half)
            for c in range(2):
                pe_gate_up(pe_, 0, 0, 1, c, True)
            pe_down(pe_, 0, 0, True)
            with pe_.Fori(1, LAST) as t:
                pe_ffn(pe_, 0, t, False)
            pe_ffn(pe_, 0, LAST, False, after_tile=lambda r: pe_early(pe_, 2, r))
            pe_between(pe_, 2)

            def bank_free(v):
                if v >= 8:
                    before = max(w for w in range(v) if v_bank(w) == v_bank(v))
                    pe_.wait_ge(v_act if tile_owner(before) == "act" else v_dve, owner_rank(before))

            for n, (p, h) in enumerate(IN_ORDER):
                u = U_IN + 2 * p
                if h == 0:
                    pe_.wait_ge(lo_ready, u + 2)
                for k in range(KC):
                    if p == 0:
                        pe_.wait_ge(ulo_ready, 16 + 8 * h + k + 1)
                    for i in range(2):
                        v = 2 * n + i
                        if k == 0:
                            bank_free(v)
                        w = [x[:, (u + i) % SLOTS, k * P:(k + 1) * P] for x in (w_hi, w_lo)]
                        for s, (a, b) in enumerate(passes(w, [half(x, k, h) for x in (u_hi, u_lo)])):
                            mm = pe_.matmul(PS[:, v_bank(v), :], a, b, start=(k == 0 and s == 0), stop=(k == KC - 1 and s == 2))
                        if k == KC - 1:
                            mm.then_inc(v_ready, 1)
                    if n == 1 and k == 5:
                        pe_sum_up(pe_, 5)
                if n == 1:
                    pe_row(pe_, 5)
            pe_.wait_ge(small_lo_ready, 1)
            for h in range(2):
                bank_free(V_SMALL + h)
                for k in range(KC):
                    w = [y[:, k, :] for y in (small_hi, small_lo)]
                    for s, (a, b) in enumerate(passes(w, [half(x, k, h) for x in (u_hi, u_lo)])):
                        mm = pe_.matmul(small_tile(h)[1], a, b, start=(k == 0 and s == 0), stop=(k == KC - 1 and s == 2))
                mm.then_inc(v_ready, 1)
            for n in range(len(TOK_PAIRS)):
                u = U_IN + 2 * (len(IN_PAIRS) + n)
                pe_.wait_ge(lo_ready, u + 2)
                for t in range(NT):
                    v = V_TOK + NT * n + t
                    bank_free(v)
                    for k in range(KC):
                        x = [y[:, k, t * P:(t + 1) * P] for y in (u_hi, u_lo)]
                        w = [y[:, u % SLOTS:u % SLOTS + 2, k * P:(k + 1) * P] for y in (w_hi, w_lo)]
                        for s, (a, b) in enumerate(passes(x, w)):
                            mm = pe_.matmul(PS[:, v % 8, 0:2 * P].rearrange("p (a b) -> p a b", a=2), a, b,
                                            start=(k == 0 and s == 0), stop=(k == KC - 1 and s == 2))
                    mm.then_inc(v_ready, 1)

    with nc.Block() as block:
        def outer(n, pair):
            col = ((n // 2) % 2 * PAIRS + pair) * P
            return PS[:, 4 * (n % 2) + n // 4, col:col + P]

        @block.sync
        def _(sp):
            sp.dma_start(gup[:, :], A["gla_gate_up"][0]).then_inc(gup_loaded, 16)
            for n in range(2):
                sp.dma_start(w2[:, n, :], A[("cmp_k_w2", "cmp_v_w2")[n]][0]).then_inc(w2_loaded, 16)
            for i in range(2, 2 * NW1):
                load_w1(sp, i)

        @block.gpsimd
        def _(pool):
            pool.wait_ge(g_dve, 7)
            pool.memset(gq[GK:P, :, :], 0.0).then_inc(q_zeroed, 1)
            pool.memset(ge[0:GK, :, :], 0.0).then_inc(q_zeroed, 1)

        @block.scalar
        def _(act):
            flat = [x[:, :, :].rearrange("p a b -> p (a b)") for x in (gx, gb, ge)]
            act.wait_ge(gates_turned, 1)
            act.activation(gate[:, :, :], PS[:, 0, 0:NT * SMALL].rearrange("p (t s) -> p t s", s=SMALL)[:, :, RANK:SMALL],
                           ACT.Sigmoid)
            act.wait_ge(gx_ready, 4)
            act.activation(flat[1], flat[0], ACT.Abs).then_inc(g_act, 1)
            act.wait_ge(g_act, 1)
            act.activation(flat[1], flat[1], ACT.Exp, scale=-1.0).then_inc(g_act, 1)
            act.wait_ge(g_act, 2)
            act.activation(flat[1], flat[1], ACT.Ln, bias=1.0).then_inc(g_act, 1)
            act.wait_ge(g_dve, 4)
            act.activation(flat[0], flat[0], ACT.Exp, scale=1.0 / GATE_NORM).then_inc(g_act, 1)
            act.activation(flat[2], flat[1], ACT.Exp, scale=1.0 / GATE_NORM).then_inc(g_act, 1)
            b_last = gb[:, :, :].rearrange("p a (n c) -> p a n c", c=CHUNK)[:, :, :, CHUNK - 1]
            act.activation(decay[:, :, :], b_last, ACT.Exp, scale=1.0 / GATE_NORM).then_inc(g_act, 1)
            act.wait_ge(g_act, 6)
            act.activation(flat[1], flat[1], ACT.Exp, scale=-1.0 / GATE_NORM).then_inc(g_act, 1)
            for j in range(4):
                act.wait_ge(kend_turned, j + 1)
                act.activation(kend[:, 2 * j:2 * j + 2, :], PS[:, j, :].rearrange("p (a b) -> p a b", a=2), ACT.Copy)\
                   .then_inc(kend_kept, 1)
            for n in range(2):
                act.wait_ge(w1_used, NW1 * (n + 1))
                act.activation(hid_rows[0:N_CMP, n, :], PS[0:N_CMP, 6 + n, 0:P], ACT.Silu).then_inc(hid_silu, 1)
            for h in range(2):
                act.wait_ge(go_done, 4 * (h + 1))
                for hd in range(HEADS):
                    act.activation(half(oT, HEADS + hd, h), PS[:, hd, :], ACT.Copy).then_inc(go_kept, 1)

        @block.vector
        def _(dve):
            keep = scan_keep[:, :].rearrange("p (n c) -> p n c", c=CHUNK)
            chain = lambda n: dve.wait_ge(g_dve, n)
            for j in range(4):
                pair, h = divmod(j, 2)
                dve.wait_ge(gpre_ready, j + 1)
                bias = vec[:, VEC_AT["gla_gate_bias"] + pair:VEC_AT["gla_gate_bias"] + pair + 1]
                dve.tensor_scalar(half(gx, pair, h), PS[:, 2 + j, :], bias, None, ALU.add).then_inc(gx_ready, 1)
            for n in range(2):
                src = kcmp[:, n, :].rearrange("p (n c) -> p n c", c=CMP_STRIDE)
                for hb, dst in ((0, kv_a), (1, kv_b)):
                    at0 = n * CMP_BLOCK + hb * CMP_STRIDE
                    dve.tensor_tensor(dst[:, n, :].rearrange("p (n c) -> p n c", c=CMP_STRIDE), src,
                                      pe[:, at0:at0 + CMP_STRIDE].unsqueeze(1).to_broadcast([P, SEQ // CMP_STRIDE, CMP_STRIDE]),
                                      ALU.add).then_inc(kv_biased, 1)
            dve.memset(kcT[:, :], 0.0).then_inc(cmp_kept, 1)
            dve.memset(vc[:, :], 0.0).then_inc(cmp_kept, 1)
            dve.memset(scan_keep[:, :], 1.0).then_inc(cmp_kept, 1)
            dve.wait_ge(cmp_kept, 3)
            dve.memset(keep[:, :, 0:1], 0.0).then_inc(cmp_kept, 1)
            dve.wait_ge(g_act, 3)
            flat = [x[:, :, :].rearrange("p a b -> p (a b)") for x in (gx, gb, ge)]
            dve.scalar_tensor_tensor(flat[0], flat[0], 0.0, flat[1], ALU.min, ALU.subtract).then_inc(g_dve, 1)
            chain(1)
            dve.wait_ge(cmp_kept, 4)
            for pair in range(PAIRS):
                dve.tensor_tensor_scan(gb[:, pair, :], scan_keep[:, :], gx[:, pair, :], 0.0, ALU.mult, ALU.add)\
                   .then_inc(g_dve, 1)
            chain(3)
            by_chunk = [x[:, :, :].rearrange("p a (n c) -> p (a n) c", c=CHUNK) for x in (gx, gb)]
            dve.tensor_tensor(by_chunk[0], by_chunk[1][:, :, CHUNK - 1:CHUNK].to_broadcast([P, PAIRS * N_CHUNK, CHUNK]),
                              by_chunk[1], ALU.subtract).then_inc(g_dve, 1)
            dve.wait_ge(g_act, 4)
            dve.tensor_tensor(gx[:, :, :], gx[:, :, :], gk[:, :, :], ALU.mult).then_inc(g_dve, 1)
            dve.wait_ge(g_act, 5)
            dve.tensor_tensor(gq[0:GK, :, :], gq[0:GK, :, :], ge[0:GK, :, :], ALU.mult).then_inc(g_dve, 1)
            dve.tensor_tensor(ge[GK:P, :, :], gq[GK:P, :, :], ge[GK:P, :, :], ALU.mult).then_inc(g_dve, 1)
            chain(5)
            dve.wait_ge(g_act, 7)
            dve.tensor_tensor(gk[:, :, :], gk[:, :, :], gb[:, :, :], ALU.mult).then_inc(g_dve, 1)
            dve.wait_ge(g_act, 7)
            for n in range(N_CHUNK - 1):
                if n == 8:
                    for m in range(2):
                        dve.wait_ge(hid_turned, m + 1)
                        dve.tensor_copy(hid[:, m, 0:N_CMP], PS[:, 6 + m, 2 * P:2 * P + N_CMP]).then_inc(hid_kept, 1)
                    dve.wait_ge(cmp_ready, 1)
                    dve.tensor_copy(kcT[:, 0:N_CMP], PS[:, 6, P:P + N_CMP]).then_inc(cmp_kept, 1)
                    dve.wait_ge(cmp_ready, 2)
                    dve.tensor_copy(vc[0:N_CMP, :], PS[0:N_CMP, 7, P:2 * P]).then_inc(cmp_kept, 1)
                dve.wait_ge(outer_ready, min(n // 4 * 4 + 2 + n % 2, N_CHUNK - 2) + 1)
                for pair in range(PAIRS):
                    if n > 0:
                        dve.wait_ge(state_ready, 2 * (n - 1) + pair + 1)
                    add = outer(n, pair)
                    if n == 0:
                        dve.tensor_copy(state[:, 1, pair, :], add).then_inc(state_ready, 1)
                    else:
                        dve.scalar_tensor_tensor(state[:, n + 1, pair, :], state[:, n, pair, :], decay[:, pair, n:n + 1],
                                                 add, ALU.mult, ALU.add).then_inc(state_ready, 1)
            for t in range(NT):
                dve.wait_ge(a_ready, t + 1)
                if t >= 2:
                    dve.wait_ge(go_done, t - 1)
                dve.tensor_tensor(at_sb[:, t % 2, :].rearrange("p (a b i) -> p a b i", a=2, b=2),
                                  PS[:, 4 + 2 * (t % 2):6 + 2 * (t % 2), 0:2 * P].rearrange("p a (b i) -> p a b i", b=2),
                                  gla_causal[:, :].unsqueeze(1).unsqueeze(1).to_broadcast([P, 2, 2, P]), ALU.mult).then_inc(a_masked, 1)

        @block.tensor
        def _(pe_):
            for t in range(NT):
                mm = pe_.transpose(PS[:, 0, t * SMALL:(t + 1) * SMALL], smallT[:, t * P:(t + 1) * P], ident[0:SMALL, 0:SMALL])
            mm.then_inc(gates_turned, 1)
            pe_.wait_ge(gup_loaded, 16)
            for j in range(4):
                pair, h = divmod(j, 2)
                pe_.matmul(PS[:, 2 + j, :], gup[:, pair * P:(pair + 1) * P], smallT[0:RANK, h * HALF:(h + 1) * HALF],
                           start=True, stop=True).then_inc(gpre_ready, 1)
            for i in range(2 * NW1):
                n = i // NW1
                if i % NW1 == 0:
                    pe_.wait_ge(kv_biased, 2 * n + 2)
                pe_.wait_ge(w1_loaded[i % 4], 16 * (i // 4 + 1))
                for l8 in range(8):
                    l = (i % NW1) * 8 + l8
                    src = (kv_a, kv_b)[l // CMP_STRIDE]
                    mm = pe_.matmul(PS[0:N_CMP, 6 + n, 0:P], src[:, n, l:l + CMP_STRIDE * (N_CMP - 1) + 1:CMP_STRIDE],
                                    w1[i % 4][:, l8, :],
                                    start=(l == 0), stop=(l == CMP_BLOCK - 1))
                mm.then_inc(w1_used, 1)
            pe_.wait_ge(g_dve, 5)
            pe_.wait_ge(gx_ready, 4)
            for j in range(4):
                for i in range(4):
                    t, pair = 2 * j + i // 2, i % 2
                    mm = pe_.transpose(PS[:, j, i * P:(i + 1) * P], gx[:, pair, t * P:(t + 1) * P], ident[:, :])
                mm.then_inc(kend_turned, 1)
            def second_layer():
                for n in range(2):
                    pe_.wait_ge(hid_silu, n + 1)
                    pe_.transpose(PS[:, 6 + n, 2 * P:2 * P + N_CMP], hid_rows[0:N_CMP, n, :], ident[0:N_CMP, 0:N_CMP]).then_inc(hid_turned, 1)
                pe_.wait_ge(w2_loaded, 32)
                pe_.wait_ge(hid_kept, 1)
                pe_.matmul(PS[:, 6, P:P + N_CMP], w2[:, 0, :], hid[:, 0, 0:N_CMP], start=True, stop=True).then_inc(cmp_ready, 1)
                pe_.wait_ge(hid_kept, 2)
                pe_.matmul(PS[0:N_CMP, 7, P:2 * P], hid[:, 1, 0:N_CMP], w2[:, 1, :], start=True, stop=True).then_inc(cmp_ready, 1)

            for n in range(N_CHUNK - 1):
                t, lo = n // 2, (n % 2) * CHUNK
                if n % 4 == 0:
                    pe_.wait_ge(kend_kept, n // 4 + 1)
                if n == 0:
                    pe_.wait_ge(kend_kept, 4)
                if n == 8:
                    second_layer()
                    pe_.wait_ge(cmp_kept, 6)
                for hd in range(HEADS):
                    pair, hh = divmod(hd, 2)
                    mm = pe_.matmul(outer(n, pair)[hh * GK:(hh + 1) * GK, :],
                                    kend[lo:lo + CHUNK, t, hd * GK:(hd + 1) * GK],
                                    gv[lo:lo + CHUNK, t, hd * GV:(hd + 1) * GV], start=True, stop=True)
                mm.then_inc(outer_ready, 1)
            pe_.wait_ge(g_dve, 8)
            pe_.wait_ge(q_zeroed, 2)
            pe_.wait_ge(state_ready, 2 * (N_CHUNK - 1))
            q_of = (gq, ge)

            def scores(t):
                if t >= 2:
                    pe_.wait_ge(a_masked, t - 1)
                for hd in range(HEADS):
                    pair, hh = divmod(hd, 2)
                    mm = pe_.matmul(PS[:, 4 + 2 * (t % 2) + hh, pair * P:(pair + 1) * P], gk[:, pair, t * P:(t + 1) * P],
                                    q_of[hh][:, pair, t * P:(t + 1) * P], start=True, stop=True)
                mm.then_inc(a_ready, 1)

            scores(0)
            for t in range(NT):
                if t + 1 < NT:
                    scores(t + 1)
                if t == 4:
                    pe_.wait_ge(go_kept, HEADS)
                pe_.wait_ge(a_masked, t + 1)
                for hd in range(HEADS):
                    pair, hh = divmod(hd, 2)
                    col = (t % 4) * P
                    pe_.matmul(PS[:, hd, col:col + P], gv[:, t, hd * GV:(hd + 1) * GV], at_sb[:, t % 2, (2 * hh + pair) * P:(2 * hh + pair + 1) * P],
                               start=True, stop=True, skip_group_check=True)
                    for s in range(2):
                        n = 2 * t + s
                        if n > 0:
                            mm = pe_.matmul(PS[:, hd, col + s * CHUNK:col + (s + 1) * CHUNK], state[:, n, pair, :],
                                            q_of[hh][:, pair, n * CHUNK:(n + 1) * CHUNK], start=False, stop=True,
                                            skip_group_check=True)
                mm.then_inc(go_done, 1)

    groups = [(h, kind) for h in range(2) for kind in range(2)]

    def scaled_first(x):
        return 6 * (x // 8 * 2) + (x % 8 + 1 if x % 8 < 4 else 4 + 2 * (x % 4) + 1)

    def scaled_at(x):
        return scaled_first(x) + (x // 4) % 2

    def hsum_bank(g):
        return 3

    def hrow_bank(x):
        return x % 3

    def hrow_before(x):
        return max((y for y in range(x) if hrow_bank(y) == hrow_bank(x)), default=None)

    def head_square(act, g, hd):
        (h, kind), x = groups[g], 4 * g + hd
        if x >= 2:
            act.wait_ge(hsq_used, x - 1)
        act.activation(h_sq[:, x % 2, :], half(oT, 4 * kind + hd, h), ACT.Square).then_inc(hsq_ready, 1)

    def head_sqrt(act, g):
        act.wait_ge(hsq_used, 4 * (g + 1))
        if g >= 2:
            act.wait_ge(hrstd_ready, g - 1)
        act.activation(rms[:, g % 2, :], PS[:, hsum_bank(g), 0:16], ACT.Sqrt, scale=1.0 / DH, bias=eps[:, 0:1])\
           .then_inc(hrms_ready, 1)

    def head_round(act, g, hd):
        (h, kind), x = groups[g], 4 * g + hd
        act.wait_ge(hn_scaled, scaled_at(x))
        act.activation(half(u_hi, 4 * kind + hd, h), half(oT, 4 * kind + hd, h), ACT.Copy).then_inc(mhi_ready, 1)

    def head_sum(pe_, g, hd):
        x = 4 * g + hd
        pe_.wait_ge(hsq_ready, x + 1)
        if hd == 0 and g > 0:
            pe_.wait_ge(hrms_ready, g)
        for t in range(4):
            mm = pe_.matmul(PS[:, hsum_bank(g), 4 * hd + t:4 * hd + t + 1], h_sq[:, x % 2, t * P:(t + 1) * P],
                            ones[:, 0:1], start=(hd == 0 and t == 0), stop=True, skip_group_check=True)
        mm.then_inc(hsq_used, 1)

    def head_row(pe_, g, hd):
        x = 4 * g + hd
        pe_.wait_ge(hrstd_ready, g + 1)
        if hrow_before(x) is not None:
            pe_.wait_ge(hn_scaled, scaled_first(hrow_before(x)))
        spread(pe_, hrow_bank(x), lambda t: rstd[:, g % 2, 4 * hd + t:4 * hd + t + 1]).then_inc(hrb_ready, 1)

    def head_rstd(dve, g):
        dve.wait_ge(hrms_ready, g + 1)
        dve.reciprocal(rstd[:, g % 2, :], rms[:, g % 2, :]).then_inc(hrstd_ready, 1)

    def head_scale(dve, g, hd):
        h, kind = groups[g]
        x = 4 * g + hd
        o = half(oT, 4 * kind + hd, h)
        gn = VEC_AT[("nsa_out_g", "gla_out_g")[kind]] + hd
        dve.wait_ge(hrb_ready, x + 1)
        dve.scalar_tensor_tensor(o, o, vec[:, gn:gn + 1], PS[:, hrow_bank(x), :], ALU.mult, ALU.mult).then_inc(hn_scaled, 1)
        if kind == 1:
            dve.wait_ge(hn_scaled, scaled_first(x))
            dve.tensor_tensor(o, o, half(gog, hd, h), ALU.mult).then_inc(hn_scaled, 1)

    def head_rest(dve, g, hd):
        h, kind = groups[g]
        x = 4 * g + hd
        ch = 4 * kind + hd
        dve.wait_ge(mhi_ready, x + 1)
        dve.tensor_tensor(half(u_lo, ch, h), half(oT, ch, h), half(u_hi, ch, h).bitcast(F32), ALU.subtract)\
           .then_inc(mlo_ready, 1)

    OFF = [0, SEQ, SEQ + WINDOW + P]

    def factor(j):
        return HEADS + j

    def win_lo(i):
        return max(0, i - WT)

    def width(i, j):
        return (i + 1) * P if j < HEADS else (i + 1 - win_lo(i)) * P

    def key_tiles(i):
        return [(0, kt, kt * P) for kt in range(i + 1)] + \
               [(1, kt, (kt - win_lo(i)) * P) for kt in range(win_lo(i), i + 1)] + [(2, 0, 0)]

    def slot_banks(it):
        if it < 9 * (HALF // P):
            return [it % 4]
        return [2 * (it % 2), 2 * (it % 2) + 1]

    def slot_before(it):
        return max((x for x in range(it) if set(slot_banks(x)) & set(slot_banks(it))), default=None)

    def slot(it):
        banks = slot_banks(it)
        return PS[:, banks[0]:banks[-1] + 1, :].rearrange("p a b -> p (a b)")

    first_tile = [sum(len(key_tiles(x)) for x in range(i)) for i in range(NT + 1)]

    HEADS_AT = [(), (), (), (0,), (1, 2), (3, 4), (5, 6), (7,), (), ()]

    def share(i, j):
        n = len(key_tiles(i))
        return range(n * j // 9, n * (j + 1) // 9)

    with nc.Block() as block:
        @block.sync
        def _(sp):
            for hd in range(HEADS):
                sp.dma_start(gog[:, hd, :], gog_spill[hd]).then_inc(gog_back, 16)
            sp.wait_ge(gog_back, 16 * HEADS)

        @block.scalar
        def _(act):
            for i in range(-1, NT):
                for j in range(9):
                    if i + 1 < NT:
                        it = 9 * (i + 1) + j
                        b, par = j // HEADS, (i + 1) % 2
                        act.wait_ge(max_done, it + 1)
                        if i + 1 >= 2 and j == 0:
                            act.wait_ge(pv_done, first_tile[i])
                        if b < 2:
                            w = width(i + 1, j)
                            act.activation(prob[:, par, j % HEADS, OFF[b]:OFF[b] + w],
                                           slot(it)[:, 0:w], ACT.Exp,
                                           bias=neg_max[:, par, factor(j):factor(j) + 1],
                                           accum_out=row_sum[:, par, factor(j):factor(j) + 1]).then_inc(exp_done, 1)
                        else:
                            for hd in range(HEADS):
                                ins = act.activation(prob[:, par, hd, OFF[2]:OFF[2] + CMPW],
                                                     slot(it)[:, hd * CMPW:(hd + 1) * CMPW], ACT.Exp,
                                                     bias=neg_max[:, par, hd:hd + 1],
                                                     accum_out=row_sum[:, par, hd:hd + 1])
                            ins.then_inc(exp_done, 1)
                    if i == NT - 1:
                        if j in (2, 4):
                            head_sqrt(act, j // 2 - 1)
                        if j < 4:
                            for hd in (2 * (j % 2), 2 * (j % 2) + 1):
                                head_square(act, j // 2, hd)
                    if i >= 0:
                        for m in share(i, j):
                            n = first_tile[i] + m
                            if n % 2 == 0:
                                rows = CMPW if key_tiles(i)[m][0] == 2 else P
                                act.wait_ge(pt_ready, n + 1)
                                if n >= 4:
                                    act.wait_ge(pv_done, n - 3)
                                act.activation(probT[0:rows, n % 4, :], PS[0:rows, 4 + n % 2, :], ACT.Copy).then_inc(pt_act, 1)
                if i >= 0:
                    act.wait_ge(pv_done, first_tile[i + 1])
                    act.activation(oT[:, 0:HEADS, i * P:(i + 1) * P],
                                   PS[:, 6 + i % 2, :].rearrange("p (h q) -> p h q", h=HEADS), ACT.Copy).then_inc(o_kept, 1)

        @block.vector
        def _(dve):
            for i in range(-1, NT):
                if i >= 0:
                    par = i % 2
                    dve.wait_ge(exp_done, 9 * (i + 1))
                    dve.reciprocal(inv_sum[:, par, :], row_sum[:, par, :]).then_inc(r_ready, 1)
                    dve.wait_ge(r_ready, i + 1)
                    dve.tensor_tensor(p_scale[:, par, :].rearrange("p (b h) -> p b h", b=3),
                                      inv_sum[:, par, :].rearrange("p (b h) -> p b h", b=3),
                                      gate[:, i, :].rearrange("p (h b) -> p b h", b=3),
                                      ALU.mult).then_inc(p_scaled, 1)
                    dve.wait_ge(p_scaled, 13 * i + 1)
                    for j in range(8):
                        b = j // HEADS
                        pr = prob[:, par, j % HEADS, OFF[b]:OFF[b] + width(i, j)]
                        dve.tensor_scalar(pr, pr, p_scale[:, par, factor(j):factor(j) + 1], None, ALU.mult).then_inc(p_scaled, 1)
                    for hd in range(HEADS):
                        pr = prob[:, par, hd, OFF[2]:OFF[2] + CMPW]
                        dve.scalar_tensor_tensor(pr, pr, p_scale[:, par, hd:hd + 1], cmp_valid[:, i, :],
                                                 ALU.mult, ALU.mult).then_inc(p_scaled, 1)
                for j in range(9):
                    if i + 1 < NT:
                        it = 9 * (i + 1) + j
                        par = (i + 1) % 2
                        dve.wait_ge(s_ready, it + 1)
                        if i + 1 >= 2 and j == 0:
                            dve.wait_ge(exp_done, 9 * i)
                        if j < 8:
                            w = width(i + 1, j)
                            dve.tensor_reduce(neg_max[:, par, factor(j):factor(j) + 1],
                                              slot(it)[:, 0:w],
                                              AX.X, ALU.max, negate=True).then_inc(max_done, 1)
                        else:
                            dve.tensor_reduce(neg_max[:, par, 0:HEADS],
                                              slot(it)[:, 0:HEADS * CMPW].rearrange("p (h n) -> p h n", h=HEADS),
                                              AX.X, ALU.max, negate=True).then_inc(max_done, 1)
                    if i == NT - 1:
                        if j in (3, 5):
                            head_rstd(dve, (j - 3) // 2)
                        if j == 4:
                            dve.wait_ge(gog_back, 16 * HEADS)
                        for x in HEADS_AT[j - 1]:
                            head_scale(dve, x // HEADS, x % HEADS)
                    if i >= 0:
                        for m in share(i, j):
                            n = first_tile[i] + m
                            if n % 2 == 1:
                                rows = CMPW if key_tiles(i)[m][0] == 2 else P
                                dve.wait_ge(pt_ready, n + 1)
                                if n >= 4:
                                    dve.wait_ge(pv_done, n - 3)
                                dve.tensor_copy(probT[0:rows, n % 4, :], PS[0:rows, 4 + n % 2, :]).then_inc(pt_dve, 1)

        @block.tensor
        def _(pe_):
            def scores(i, j):
                it = 9 * i + j
                if slot_before(it) is not None:
                    pe_.wait_ge(exp_done, slot_before(it) + 1)
                if j < 8:
                    hd, keys, lo = (j, ksT, 0) if j < HEADS else (j - HEADS, kwT, win_lo(i) * P)
                    w = width(i, j)
                    wide = slot(it)
                    for c0 in range(0, w, HALF):
                        c1 = min(w, c0 + HALF)
                        masks = [(m, at0) for m, at0, on in ((neg_past, 0, j >= HEADS and i >= WT), (neg_future, w - P, True))
                                 if on and c0 <= at0 < c1]
                        mm = pe_.matmul(wide[:, c0:c1], qT[:, hd, i * P:(i + 1) * P], keys[:, lo + c0:lo + c1],
                                        start=True, stop=True)
                        for m, at0 in masks:
                            mm = pe_.matmul(wide[:, at0:at0 + P], identb[:, :], m[:, :], start=False, stop=True,
                                            skip_group_check=True)
                else:
                    for hd in range(HEADS):
                        pe_.matmul(slot(it)[:, hd * CMPW:(hd + 1) * CMPW], qT[:, hd, i * P:(i + 1) * P], kcT[:, :],
                                   start=(hd == 0), stop=True, skip_group_check=True)
                    mm = pe_.matmul(slot(it)[:, 0:HEADS * CMPW].rearrange("p (h n) -> p h n", h=HEADS), identb[:, :],
                                    neg_cmp[:, i, :].unsqueeze(1).to_broadcast([P, HEADS, CMPW]), start=False, stop=True,
                                    skip_group_check=True)
                mm.then_inc(s_ready, 1)

            def turn(i, m):
                b, kt, at0 = key_tiles(i)[m]
                n = first_tile[i] + m
                rows = CMPW if b == 2 else P
                pe_.wait_ge(p_scaled, 13 * i + (5, 9, 13)[b])
                if n >= 2:
                    pe_.wait_ge((pt_act, pt_dve)[n % 2], (n - 2) // 2 + 1)
                for hd in range(HEADS):
                    mm = pe_.transpose(PS[0:rows, 4 + n % 2, hd * P:(hd + 1) * P],
                                       prob[:, i % 2, hd, OFF[b] + at0:OFF[b] + at0 + rows], ident[:, :])
                mm.then_inc(pt_ready, 1)

            def values(i, m):
                b, kt, at0 = key_tiles(i)[m]
                n, last = first_tile[i] + m, m == len(key_tiles(i)) - 1
                rows = CMPW if b == 2 else P
                v = (vtok[:, kt, 0:P], vtok[:, kt, P:2 * P], vc[:, :])[b]
                pe_.wait_ge((pt_act, pt_dve)[n % 2], n // 2 + 1)
                if m == 0 and i >= 2:
                    pe_.wait_ge(o_kept, i - 1)
                mm = pe_.matmul(PS[:, 6 + i % 2, :], v, probT[0:rows, n % 4, :], start=(m == 0), stop=last)
                mm.then_inc(pv_done, 1)

            waiting = []
            for i in range(-1, NT):
                for j in range(9):
                    if i + 1 < NT:
                        scores(i + 1, j)
                    if i >= 0:
                        for m in share(i, j):
                            turn(i, m)
                            waiting.append((i, m))
                            if len(waiting) > 1:
                                values(*waiting.pop(0))
                    if i == NT - 1:
                        if j < 4:
                            for hd in (2 * (j % 2), 2 * (j % 2) + 1):
                                head_sum(pe_, j // 2, hd)
                        for x in HEADS_AT[j]:
                            head_row(pe_, x // HEADS, x % HEADS)
                if i >= 0:
                    values(*waiting.pop(0))

    def out_kept(h, c):
        return f_kept, R_OUT + pair_tile(h, c) + 1

    def pair_tile(h, m):
        return 2 * PAIR_ORDER.index((m // 2, h)) + m % 2

    def t_done(h, c):
        return t_ready, pair_tile(h, c) + 1

    Y_ORDER = [(t, b) for t in range(4) for b in range(2)] + [(t, b) for b in range(2) for t in range(4, NT)]

    def y_emptied(n):
        if n < 12:
            return y_act, n + 1
        return (y_act, 12 + (n - 12) // 2 + 1) if n % 2 == 0 else (y_dve, (n - 12) // 2 + 1)

    with nc.Block() as block:
        @block.sync
        def _(sp):
            sp.wait_ge(mlo_ready, 16)
            for c in range(KC):
                sp.dma_start(xT[:, c, :], x_spill[c]).then_inc(x_back, 16)
            for u in range(U_OUT + AHEAD + RAWS, U_FFN[1] + 6):
                sp_load(sp, u)
            with sp.Fori(1, ITERS) as t:
                sp_ffn(sp, 1, t, 0)
            for u in range(U_PLE, U_END):
                sp_load(sp, u)
            for n, (t, b) in enumerate(Y_ORDER):
                sp.wait_ge(*y_emptied(n))
                cols = slice(b * HALF, (b + 1) * HALF)
                sp.dma_start(out[0, t * P:(t + 1) * P, cols], y_rows[:, t, cols]).then_inc(y_stored, 16)
            sp.wait_ge(y_stored, 16 * len(Y_ORDER))

        @block.gpsimd
        def _(pool):
            for k in range(6, 14):
                pool_norm(pool, k)

        @block.scalar
        def _(act):
            for g in (0, 1):
                for hd in range(HEADS):
                    head_round(act, g, hd)
            for g in (2, 3):
                for hd in range(HEADS):
                    head_square(act, g, hd)
                head_sqrt(act, g)
                for hd in range(HEADS):
                    head_round(act, g, hd)

            for s in range(4):
                for i in range(2):
                    u = U_OUT + 2 * s + i + AHEAD
                    act_round(act, u, ((v_ready, V_END), (f_ready, R_OUT + 6), (f_ready, R_OUT + 8), (f_ready, R_OUT + 12))[s])
            act_cross(act, 6, 1, out_kept, lambda: act_silu(act, 1, 0, 0, True))
            act_ffn(act, 1, 0, True)
            with act.Fori(1, ITERS) as t:
                act_ffn(act, 1, t, False)
            act.wait_ge(gu_ready, 2 * (Q0[1] + 4 * ITERS))
            for a in range(2):
                act.dma_start(p_place[:, 4:8, HALF + a * PLE:HALF + (a + 1) * PLE],
                              A["p"][0, 0].rearrange("(c a p) f -> a p c f", a=2, p=P)[a]).then_inc(p_loaded, 16)

            def keep_p(j):
                act.wait_ge(p_turned, j + 1)
                act.activation(p_place[:, j // 2:4:2, HALF + (j % 2) * 2 * P:HALF + (j % 2 + 1) * 2 * P]
                               .rearrange("p c (t q) -> p c t q", t=2),
                               PS[:, 3, :].rearrange("p (t c q) -> p c t q", t=2, c=2), ACT.Copy).then_inc(p_kept, 1)

            act_norm(act, 10, fT, f_done(1))
            keep_p(0)
            for c in range(KC):
                act_square(act, 11, c, fT, f_done(1))
                if c % 2 == 1 and c < 6:
                    keep_p(c // 2 + 1)
            act_sqrt(act, 11)
            act_hi_half(act, 0, xT, x_done(2))
            act.wait_ge(f_ready, R_G)
            act.wait_ge(p_kept, 4)
            for c in range(2):
                for hh in range(2):
                    act.activation(half(h_hi, c, hh), p_place[:, 2 * c + hh, HALF:SEQ], ACT.Copy).then_inc(p_hi, 1)

            def round_gate(m, free):
                for i in range(2):
                    act_round(act, U_PLE + 2 + m + i, free)

            def sigmoid(x):
                act.wait_ge(f_ready, R_G + x + 1)
                if x >= 2:
                    act.wait_ge(t_ready, x - 1)
                act.activation(sg[:, x % 2, :], PS[:, 4 + x % 4, :], ACT.Sigmoid).then_inc(sig_done, 1)

            round_gate(2, (f_ready, R_G))
            for c in range(KC):
                act_hi(act, 1, c, half(xT, c, 1), x_done(2)(1, c))
                if c == 0:
                    sigmoid(0)
                    sigmoid(1)
            for x in range(2, 14):
                if x == 12:
                    act.wait_ge(lo_ready, U_END)
                    for c in range(6):
                        act_square(act, 12, c, fT, t_done)
                sigmoid(x)
                if x == 5:
                    round_gate(4, (f_ready, R_G + 6))
                if x == 7:
                    round_gate(6, (f_ready, R_G + 8))
            for c in range(6, KC):
                act_square(act, 12, c, fT, t_done)
            act_sqrt(act, 12)
            sigmoid(14)
            for c in range(KC):
                if c == 6:
                    sigmoid(15)
                act_square(act, 13, c, fT, t_done)
            act_sqrt(act, 13)
            for n, (t, b) in enumerate(Y_ORDER):
                if y_emptied(n)[0] is y_act:
                    act.wait_ge(y_turned, n + 1)
                    act.activation(y_rows[:, t, b * HALF:(b + 1) * HALF], PS[:, 4 + n % 4, :], ACT.Copy).then_inc(y_act, 1)

        @block.vector
        def _(dve):
            def keep_out(r):
                (s, h), i = PAIR_ORDER[r // 2], r % 2
                dve.wait_ge(f_ready, R_OUT + r + 1)
                dve.tensor_copy(half(fT, 2 * s + i, h), PS[:, 4 + r % 4, :]).then_inc(f_kept, 1)

            for g in range(2):
                for hd in range(HEADS):
                    head_rest(dve, g, hd)
            for g in (2, 3):
                if g == 3:
                    keep_out(0)
                    keep_out(1)
                head_rstd(dve, g)
                for hd in range(HEADS):
                    head_scale(dve, g, hd)
                    if hd > 0:
                        head_rest(dve, g, hd - 1)
                head_rest(dve, g, HEADS - 1)

            for s, tiles in enumerate(((2, 3, 4, 5), (6, 7), (8, 9, 10, 11), (12, 13))):
                for i in range(2):
                    dve_rest(dve, U_OUT + 2 * s + i + AHEAD)
                for r in tiles:
                    keep_out(r)
            dve.wait_ge(x_back, 16 * KC)
            dve_norm(dve, 6)
            dve_cross(dve, 6, 1, "mix_post_g", "ffn2_pre_g", lambda c: keep_out((14, 15)[c // 3]) if c in (0, 3) else None,
                      lambda: dve_h(dve, 1, 0, 0, True))
            dve_ffn(dve, 1, 0, True)
            with dve.Fori(1, LAST) as t:
                dve_ffn(dve, 1, t, False)
            dve_ffn_last(dve, 1, 10)

            def gated(x):
                (s, h), i = PAIR_ORDER[x // 2], x % 2
                dve.wait_ge(sig_done, x + 1)
                dve.wait_ge(e_ready, x + 1)
                dve.tensor_tensor(half(fT, 2 * s + i, h), PS[:, x % 4, :], sg[:, x % 2, :], ALU.mult).then_inc(t_ready, 1)

            def first_half(c):
                if c < 2:
                    dve_keep(dve, 1, LAST, 14 + c, False)
                if c == 5:
                    dve_norm(dve, 11)
                for i in {6: (0,), 7: (1, 2), 8: (3, 4), 9: (5, 6)}.get(c, ()):
                    dve_lo(dve, 3, 0, i, half(xT, i, 0))

            def second_half(c):
                if c == 3:
                    gated(0)
                    gated(1)

            dve_residual(dve, 2, 10, "ffn2_post_g", first_half)
            dve_lo(dve, 3, 0, 7, half(xT, 7, 0))
            for c in range(2):
                for hh in range(2):
                    dve.wait_ge(p_hi, 2 * c + hh + 1)
                    dve.tensor_tensor(half(h_lo, c, hh), p_place[:, 2 * c + hh, HALF:SEQ], half(h_hi, c, hh).bitcast(F32),
                                      ALU.subtract).then_inc(p_lo, 1)
            for m in (2, 3):
                dve_rest(dve, U_PLE + 2 + m)
            dve.wait_ge(p_lo, 4)
            dve_residual(dve, 2, 11, "ffn2_post_g", second_half, lambda c: dve_lo(dve, 3, 1, c, half(xT, c, 1)))
            for x in range(2, 14):
                gated(x)
                if x in (5, 7):
                    for i in range(2):
                        dve_rest(dve, U_PLE + 2 + x - 1 + i)
            dve_norm(dve, 12)

            def last_tiles(c):
                if c == 1:
                    gated(14)
                if c == 5:
                    gated(15)
                if c == 8:
                    dve_norm(dve, 13)

            dve_residual(dve, 3, 12, "ple_post_g", last_tiles)
            dve_residual(dve, 3, 13, "ple_post_g")
            for n, (t, b) in enumerate(Y_ORDER):
                if y_emptied(n)[0] is y_dve:
                    dve.wait_ge(y_turned, n + 1)
                    dve.tensor_copy(y_rows[:, t, b * HALF:(b + 1) * HALF], PS[:, 4 + n % 4, :]).then_inc(y_dve, 1)

        @block.tensor
        def _(pe_):
            def product(u, bank, h, k):
                w = [x[:, slot_of(u), k * P:(k + 1) * P] for x in (w_hi, w_lo)]
                for s, (a, b) in enumerate(passes(w, [half(x, k, h) for x in (u_hi, u_lo)])):
                    mm = pe_.matmul(PS[:, bank, :], a, b, start=(k == 0 and s == 0), stop=(k == KC - 1 and s == 2))
                return mm


            for n, (s, h) in enumerate(PAIR_ORDER):
                u = U_OUT + 2 * s
                pe_.wait_ge(lo_ready, u + 2)
                last = n == len(PAIR_ORDER) - 1
                order = [(i, k) for i in range(2) for k in range(KC)] if last else [(i, k) for k in range(KC) for i in range(2)]
                for i, k in order:
                    r = 2 * n + i
                    if k == 0:
                        pe_.wait_ge(f_kept, R_OUT + r - 3)
                    if s == 0 and i == 0:
                        pe_.wait_ge(mlo_ready, 8 * h + k + 1)
                    mm = product(u + i, 4 + r % 4, h, k)
                    if k == KC - 1:
                        mm.then_inc(f_ready, 1)
                    if last and (i, k) == (0, 4):
                        pe_sum_up(pe_, 6)
                    if last and (i, k) == (1, 1):
                        pe_row(pe_, 6)
                    if n == 0 and i == 1 and 2 <= k < 6:
                        head_sum(pe_, 2, k - 2)
                    if n == 1 and i == 1 and k < 4:
                        head_row(pe_, 2, k)
                    if n == 1 and i == 1 and k >= 6:
                        head_sum(pe_, 3, 2 * (k - 6))
                        head_sum(pe_, 3, 2 * (k - 6) + 1)
                    if n == 2 and i == 1 and k < 4:
                        head_row(pe_, 3, k)
            pe_between(pe_, 6)
            pe_gate_up(pe_, 1, 0, 0, 0, True)
            pe_gate_up(pe_, 1, 0, 0, 1, True, lambda k: pe_sum_up(pe_, 9) if k == 5 else None)
            pe_row(pe_, 9)
            for c in range(2):
                pe_gate_up(pe_, 1, 0, 1, c, True)
            pe_down(pe_, 1, 0, True)
            with pe_.Fori(1, LAST) as t:
                pe_ffn(pe_, 1, t, False)

            def turn_p(j):
                if j == 0:
                    pe_.wait_ge(p_loaded, 32)
                else:
                    pe_.wait_ge(p_kept, j)
                for t in (2 * j, 2 * j + 1):
                    for c in range(2):
                        at0 = HALF + (t % 2) * PLE + c * P
                        mm = pe_.transpose(PS[:, 3, ((t % 2) * 2 + c) * P:((t % 2) * 2 + c + 1) * P],
                                           p_place[:, 4 + t // 2, at0:at0 + P], ident[:, :])
                mm.then_inc(p_turned, 1)

            def after_tile(r):
                pe_early(pe_, 10, r)
                if r >= 9 and r % 2 == 1:
                    turn_p((r - 9) // 2)

            pe_ffn(pe_, 1, LAST, False, after_tile=after_tile)
            pe_sum_up(pe_, 11)
            pe_.wait_ge(p_kept, 4)
            pe_row(pe_, 11)

            def embed(x):
                (s, h), i = PAIR_ORDER[x // 2], x % 2
                m = 2 * s + i
                if x == 0:
                    pe_.wait_ge(p_lo, 4)
                if x == 3:
                    pe_.wait_ge(f_scaled, 16 * 2 + 16)
                for c in range(2):
                    w = [y[:, c, m * P:(m + 1) * P] for y in (w_hi, w_lo)]
                    for n, (a, b) in enumerate(passes(w, [half(y, c, h) for y in (h_hi, h_lo)])):
                        mm = pe_.matmul(PS[:, x % 4, :], a, b, start=(c == 0 and n == 0), stop=(c == 1 and n == 2))
                mm.then_inc(e_ready, 1)

            for n, (s, h) in enumerate(PAIR_ORDER):
                u = U_PLE + 2 + 2 * s
                pe_.wait_ge(lo_ready, u + 2)
                last = n == len(PAIR_ORDER) - 1
                order = [(i, k) for i in range(2) for k in range(KC)] if last else [(i, k) for k in range(KC) for i in range(2)]
                for i, k in order:
                    x = 2 * n + i
                    if k == 0:
                        if x >= 4:
                            pe_.wait_ge(t_ready, x - 3)
                        if last:
                            embed(x)
                    if s == 0 and i == 0:
                        pe_.wait_ge(ulo_ready, 16 * 3 + 8 * h + k + 1)
                    mm = product(u + i, 4 + x % 4, h, k)
                    if k == KC - 1:
                        mm.then_inc(f_ready, 1)
                    if last:
                        pe_.wait_ge(t_ready, 13 + i)
                        if (i, k) == (0, 4):
                            pe_sum_up(pe_, 12)
                        if (i, k) == (1, 0):
                            pe_row(pe_, 12)
                if not last:
                    embed(2 * n)
                    embed(2 * n + 1)
            pe_sum_up(pe_, 13)
            pe_row(pe_, 13)
            for n, (t, b) in enumerate(Y_ORDER):
                pe_.wait_ge(x_ready, 56 if n < 8 else 60 if n < 12 else 64)
                if n >= 4:
                    pe_.wait_ge(*y_emptied(n - 4))
                else:
                    pe_.wait_ge(t_ready, 16)
                for c in range(4):
                    mm = pe_.transpose(PS[:, 4 + n % 4, c * P:(c + 1) * P], xT[:, 4 * b + c, t * P:(t + 1) * P], ident[:, :])
                mm.then_inc(y_turned, 1)


_INS = ["x", "p", "ffn1_pre_g", "ffn1_post_g", "ffn1_w_gate", "ffn1_w_up", "ffn1_w_down", "mix_pre_g", "mix_post_g",
        "w_in", "cmp_k_pe", "cmp_k_w1", "cmp_k_w2", "cmp_v_pe", "cmp_v_w1", "cmp_v_w2", "nsa_out_g", "gla_gate_up",
        "gla_gate_bias", "gla_out_g", "w_out", "ffn2_pre_g", "ffn2_post_g", "ffn2_w_gate", "ffn2_w_up", "ffn2_w_down",
        "ple_proj", "ple_gate", "ple_post_g"]


def kernel(**inputs):
    import numpy as _np
    import concourse.bacc as _bacc
    from concourse import mybir as _mybir
    from concourse.bass_utils import run_bass_kernel_spmd as _run

    nc = _bacc.Bacc("TRN2", target_bir_lowering=False, num_devices=1, dynamic_dma_scratch_size=1024)
    arrays, aps = {}, {}
    for name in _INS:
        a = _np.ascontiguousarray(inputs[name])
        arrays[f"in_{name}_dram"] = a
        aps[name] = nc.dram_tensor(f"in_{name}_dram", a.shape, _mybir.dt.from_np(a.dtype), kind="ExternalInput").ap()
    out = nc.dram_tensor("out_0_dram", (1, SEQ, D), _mybir.dt.float32, kind="ExternalOutput").ap()
    build(nc, aps, out)
    r = _run(nc, [arrays], core_ids=[0])
    return r.results[0]["out_0_dram"]
```
